# Optimizing a Trainium2 kernel written in Bass

```python
import jax, jax.numpy as jnp
from jax import lax
import numpy as np

D_MODEL = 1024
BATCH = 1
SEQ = 512
DEPTH = 1

GRID_W = 64
CTX_LEN = 256
N_FOURIER_GROUPS = 4
FOURIER_GROUP_W = 128
FOURIER_W = N_FOURIER_GROUPS * FOURIER_GROUP_W
N_HEADS = 8
QK_NOPE = 64
QK_ROPE = 32
HEAD_QK = QK_NOPE + QK_ROPE
V_DIM = 64
Q_LORA = 256
KV_LORA = 128
MLA_W = N_HEADS * V_DIM
N_BRANCH = 2
D_FF = 4 * D_MODEL
D_IN = FOURIER_W + Q_LORA + KV_LORA + QK_ROPE + N_BRANCH * D_MODEL
ROPE_THETA = 10000.0
Q_BLOCK = 128
EPS = 1e-6


def rmsnorm(x, g):
    xf = x.astype(jnp.float32)
    y = xf * lax.rsqrt(jnp.mean(xf * xf, axis=-1, keepdims=True) + EPS)
    return (y * g.astype(jnp.float32)).astype(x.dtype)

def modulate(h, shift, scale):
    return h * (1 + scale) + shift

def axial_rope_tables(n):
    rows = n // GRID_W
    row = jnp.repeat(jnp.arange(rows, dtype=jnp.float32), GRID_W)
    col = jnp.tile(jnp.arange(GRID_W, dtype=jnp.float32), rows)
    n_freq = QK_ROPE // 4
    freqs = ROPE_THETA ** (-jnp.arange(n_freq, dtype=jnp.float32) / n_freq)
    ang_r = row[:, None] * freqs[None, :]
    ang_c = col[:, None] * freqs[None, :]
    ang = jnp.concatenate([ang_r, ang_r, ang_c, ang_c], axis=-1)
    return jnp.cos(ang), jnp.sin(ang)

def apply_rope(x, cos, sin):
    a1, a2, b1, b2 = jnp.split(x, 4, axis=-1)
    rot = jnp.concatenate([-a2, a1, -b2, b1], axis=-1)
    return x * cos[None, :, None, :].astype(x.dtype) + rot * sin[None, :, None, :].astype(x.dtype)

def split_proj(p):
    o1 = FOURIER_W
    o2 = o1 + Q_LORA
    o3 = o2 + KV_LORA
    o4 = o3 + QK_ROPE
    return p[..., :o1], p[..., o1:o2], p[..., o2:o3], p[..., o3:o4], p[..., o4:]

def fourier_mix(f):
    B, N, _ = f.shape
    fg = f.reshape(B, N, N_FOURIER_GROUPS, FOURIER_GROUP_W).astype(jnp.float32)
    y = jnp.fft.fft2(fg, axes=(1, 3), norm="ortho").real
    return y.reshape(B, N, FOURIER_W).astype(f.dtype)

def mla_kv(kv_lat, k_rope, kv_norm_g, w_kvb, k_gain, rope):
    B, N, _ = kv_lat.shape
    kv = (rmsnorm(kv_lat, kv_norm_g) @ w_kvb).reshape(B, N, N_HEADS, QK_NOPE + V_DIM)
    k_nope, v = kv[..., :QK_NOPE], kv[..., QK_NOPE:]
    k_r = jnp.broadcast_to(k_rope[:, :, None, :], (B, N, N_HEADS, QK_ROPE))
    k = rmsnorm(jnp.concatenate([k_nope, k_r], axis=-1), k_gain)
    if rope is not None:
        k = jnp.concatenate([k[..., :QK_NOPE], apply_rope(k[..., QK_NOPE:], *rope)], axis=-1)
    return k, v

def mla_q(q_lat, q_norm_g, w_qb, q_gain, rope):
    B, N, _ = q_lat.shape
    q = (rmsnorm(q_lat, q_norm_g) @ w_qb).reshape(B, N, N_HEADS, HEAD_QK)
    q = rmsnorm(q, q_gain)
    if rope is not None:
        q = jnp.concatenate([q[..., :QK_NOPE], apply_rope(q[..., QK_NOPE:], *rope)], axis=-1)
    return q

def latent_attention(q, k_all, v_all):
    B, S, H, Dh = q.shape
    nb = S // Q_BLOCK
    qb = q.reshape(B, nb, Q_BLOCK, H, Dh).transpose(1, 0, 2, 3, 4)
    scale = HEAD_QK ** -0.5

    def one_block(qblk):
        s = jnp.einsum('bqhd,bkhd->bhqk', qblk, k_all, preferred_element_type=jnp.float32) * scale
        p = jax.nn.softmax(s, axis=-1).astype(v_all.dtype)
        return jnp.einsum('bhqk,bkhd->bqhd', p, v_all)

    o = lax.map(one_block, qb)
    return o.transpose(1, 0, 2, 3, 4).reshape(B, S, H * V_DIM)

def context_attention(q, k, v):
    B, N = q.shape[0], q.shape[1]
    s = jnp.einsum('bqhd,bkhd->bhqk', q, k, preferred_element_type=jnp.float32) * (HEAD_QK ** -0.5)
    p = jax.nn.softmax(s, axis=-1).astype(v.dtype)
    return jnp.einsum('bhqk,bkhd->bqhd', p, v).reshape(B, N, N_HEADS * V_DIM)

def merge_branches(f_mix, att, gates, w_fourier, w_mla_o, b_gate, w_out):
    g = jax.nn.sigmoid(gates + b_gate)
    g_f, g_a = g[..., :D_MODEL], g[..., D_MODEL:]
    y = g_f * (f_mix @ w_fourier) + g_a * (att @ w_mla_o)
    return y @ w_out

def sq_relu_mlp(h, w_up, w_down):
    return jnp.square(jax.nn.relu(h @ w_up)) @ w_down

def first_inputs(seed: int = 0) -> dict:
    key = jax.random.key(seed)
    ks = jax.random.split(key, 24)
    D, L = D_MODEL, DEPTH

    def w(k, shape, fan_in, mult=1.0):
        return jax.random.normal(k, shape, jnp.float32) * (mult * fan_in ** -0.5)

    def gain(k, shape):
        return 1.0 + 0.05 * jax.random.normal(k, shape, jnp.float32)

    return {
        "x": jax.random.normal(ks[0], (BATCH, SEQ, D), jnp.float32),
        "c": jax.random.normal(ks[1], (BATCH, D), jnp.float32),
        "ctx": jax.random.normal(ks[2], (BATCH, CTX_LEN, D), jnp.float32),
        "c_ctx": jax.random.normal(ks[3], (D,), jnp.float32),
        "ada_w": w(ks[4], (L, D, 6 * D), D, 0.5),
        "ada_b": 0.02 * jax.random.normal(ks[5], (L, 6 * D), jnp.float32),
        "norm1_g": gain(ks[6], (L, D)),
        "norm2_g": gain(ks[7], (L, D)),
        "w_in": w(ks[8], (L, D, D_IN), D),
        "b_gate": 0.02 * jax.random.normal(ks[9], (L, N_BRANCH * D), jnp.float32),
        "w_fourier": w(ks[10], (L, FOURIER_W, D), FOURIER_W),
        "q_norm_g": gain(ks[11], (L, Q_LORA)),
        "w_qb": w(ks[12], (L, Q_LORA, N_HEADS * HEAD_QK), Q_LORA),
        "kv_norm_g": gain(ks[13], (L, KV_LORA)),
        "w_kvb": w(ks[14], (L, KV_LORA, N_HEADS * (QK_NOPE + V_DIM)), KV_LORA),
        "q_gain": gain(ks[15], (L, HEAD_QK)),
        "k_gain": gain(ks[16], (L, HEAD_QK)),
        "w_mla_o": w(ks[17], (L, MLA_W, D), MLA_W),
        "w_out": w(ks[18], (L, D, D), D),
        "w_up": w(ks[19], (L, D, D_FF), D),
        "w_down": w(ks[20], (L, D_FF, D), D_FF),
    }

def first_block(x, c, ctx, c_ctx, ada_w, ada_b, norm1_g, norm2_g, w_in, b_gate, w_fourier, q_norm_g, w_qb,
              kv_norm_g, w_kvb, q_gain, k_gain, w_mla_o, w_out, w_up, w_down):
    rope = axial_rope_tables(x.shape[1])
    for l in range(DEPTH):
        last = l == DEPTH - 1
        mod_x = jax.nn.silu(c) @ ada_w[l] + ada_b[l]
        sh1, sc1, g1, sh2, sc2, g2 = jnp.split(mod_x[:, None, :], 6, axis=-1)
        mod_c = jax.nn.silu(c_ctx) @ ada_w[l] + ada_b[l]
        csh1, csc1, cg1, csh2, csc2, cg2 = jnp.split(mod_c, 6, axis=-1)

        hc = modulate(rmsnorm(ctx, norm1_g[l]), csh1, csc1)
        pc = hc @ w_in[l]
        fc, qlc, kvlc, krc, gc = split_proj(pc)
        kc, vc = mla_kv(kvlc, krc, kv_norm_g[l], w_kvb[l], k_gain[l], None)

        hx = modulate(rmsnorm(x, norm1_g[l]), sh1, sc1)
        px = hx @ w_in[l]
        fx, qlx, kvlx, krx, gx = split_proj(px)
        kx, vx = mla_kv(kvlx, krx, kv_norm_g[l], w_kvb[l], k_gain[l], rope)
        qx = mla_q(qlx, q_norm_g[l], w_qb[l], q_gain[l], rope)
        att_x = latent_attention(qx, jnp.concatenate([kx, kc], axis=1), jnp.concatenate([vx, vc], axis=1))
        y_x = merge_branches(fourier_mix(fx), att_x, gx, w_fourier[l], w_mla_o[l], b_gate[l], w_out[l])

        if not last:
            qc = mla_q(qlc, q_norm_g[l], w_qb[l], q_gain[l], None)
            att_c = context_attention(qc, kc, vc)
            y_c = merge_branches(fourier_mix(fc), att_c, gc, w_fourier[l], w_mla_o[l], b_gate[l], w_out[l])
            ctx = ctx + cg1 * y_c
            hc2 = modulate(rmsnorm(ctx, norm2_g[l]), csh2, csc2)
            ctx = ctx + cg2 * sq_relu_mlp(hc2, w_up[l], w_down[l])

        x = x + g1 * y_x
        h2 = modulate(rmsnorm(x, norm2_g[l]), sh2, sc2)
        x = x + g2 * sq_relu_mlp(h2, w_up[l], w_down[l])
    return x


D_MIX = D_MODEL
D_CONV = D_MIX // 2
D_MLSTM = D_MIX - D_CONV
N_HEADS_2 = 4
HEAD_DIM = D_MLSTM // N_HEADS_2
CONV_WIDTH = 31
QK_CONV_WIDTH = 4
CHUNK = 128
N_GROUPS = 4
EXPERTS_PER_GROUP = 8
N_EXPERTS = N_GROUPS * EXPERTS_PER_GROUP
TOP_K = 2
D_EXPERT = D_MODEL // 2
MOE_BLOCK = 256
F_BIAS_LO = 3.0
F_BIAS_HI = 6.0
D_IN_2 = 2 * D_CONV + 4 * D_MLSTM + 2 * N_HEADS_2


def rmsnorm_2(x, g):
    xf = x.astype(jnp.float32)
    y = xf * lax.rsqrt(jnp.mean(xf * xf, axis=-1, keepdims=True) + EPS)
    return (y * g.astype(jnp.float32)).astype(x.dtype)

def layernorm(x, g, b):
    xf = x.astype(jnp.float32)
    mu = jnp.mean(xf, axis=-1, keepdims=True)
    var = jnp.mean(jnp.square(xf - mu), axis=-1, keepdims=True)
    y = (xf - mu) * lax.rsqrt(var + EPS)
    return (y * g.astype(jnp.float32) + b.astype(jnp.float32)).astype(x.dtype)

def causal_depthwise_conv(x, w, b):
    width, ch = w.shape
    y = lax.conv_general_dilated(
        x, w[:, None, :].astype(x.dtype), window_strides=(1,), padding=[(width - 1, 0)],
        dimension_numbers=("NWC", "WIO", "NWC"), feature_group_count=ch)
    return y + b.astype(x.dtype)

def mlstm_chunkwise(q, k, v, i_pre, f_pre):
    B, H, S, Dh = q.shape
    nc = S // CHUNK
    k = k * (Dh ** -0.5)
    log_f = jax.nn.log_sigmoid(f_pre)

    def to_chunks(a):
        a = a.reshape(a.shape[:2] + (nc, CHUNK) + a.shape[3:])
        return jnp.moveaxis(a, 2, 0)

    qc, kc, vc = to_chunks(q), to_chunks(k), to_chunks(v)
    ic, fc = to_chunks(i_pre), to_chunks(log_f)
    causal = jnp.tril(jnp.ones((CHUNK, CHUNK), dtype=bool))

    def step(carry, inp):
        C, n, m = carry
        qb, kb, vb, ib, fb = inp
        b = jnp.cumsum(fb, axis=-1)
        d = b[..., :, None] - b[..., None, :] + ib[..., None, :]
        d = jnp.where(causal, d, -jnp.inf)
        g = b + m[..., None]
        m_t = jnp.maximum(g, jnp.max(d, axis=-1))
        w_intra = jnp.exp(d - m_t[..., None])
        w_inter = jnp.exp(g - m_t)
        s = jnp.einsum("bhtd,bhsd->bhts", qb, kb) * w_intra
        num = (jnp.einsum("bhts,bhsd->bhtd", s, vb)
               + w_inter[..., None] * jnp.einsum("bhvk,bhtk->bhtv", C, qb))
        den = jnp.sum(s, axis=-1) + w_inter * jnp.einsum("bhk,bhtk->bht", n, qb)
        h = num / jnp.maximum(jnp.abs(den), jnp.exp(-m_t))[..., None]
        b_last = b[..., -1]
        log_w = b_last[..., None] - b + ib
        m_new = jnp.maximum(b_last + m, jnp.max(log_w, axis=-1))
        decay = jnp.exp(b_last + m - m_new)
        w_state = jnp.exp(log_w - m_new[..., None])
        kw = kb * w_state[..., None]
        C_new = decay[..., None, None] * C + jnp.einsum("bhsv,bhsk->bhvk", vb, kw)
        n_new = decay[..., None] * n + jnp.sum(kw, axis=2)
        return (C_new, n_new, m_new), h

    init = (jnp.zeros((B, H, Dh, Dh), jnp.float32),
            jnp.zeros((B, H, Dh), jnp.float32),
            jnp.zeros((B, H), jnp.float32))
    _, hc = lax.scan(step, init, (qc, kc, vc, ic, fc))
    return jnp.moveaxis(hc, 0, 2).reshape(B, H, S, Dh)

def hybrid_mixer(h, w_in, b_in, conv_w, conv_b, conv_ln_g, conv_ln_b,
                 qk_conv_w, qk_conv_b, mlstm_norm_g, w_out):
    B, S, _ = h.shape
    z = jnp.einsum("bsd,de->bse", h, w_in) + b_in
    splits = np.cumsum([D_CONV, D_CONV, D_MLSTM, D_MLSTM, D_MLSTM, D_MLSTM, N_HEADS_2])
    conv_a, conv_gate, q, k, v, o, i_pre, f_pre = jnp.split(z, [int(i) for i in splits], axis=-1)

    u = conv_a * jax.nn.sigmoid(conv_gate)
    u = causal_depthwise_conv(u, conv_w, conv_b)
    u = jax.nn.silu(layernorm(u, conv_ln_g, conv_ln_b))

    qk = jax.nn.silu(causal_depthwise_conv(jnp.concatenate([q, k], axis=-1), qk_conv_w, qk_conv_b))
    q, k = qk[..., :D_MLSTM], qk[..., D_MLSTM:]

    def heads(a):
        return jnp.transpose(a.reshape(B, S, N_HEADS_2, HEAD_DIM), (0, 2, 1, 3)).astype(jnp.float32)

    ht = mlstm_chunkwise(heads(q), heads(k), heads(v),
                         jnp.transpose(i_pre, (0, 2, 1)).astype(jnp.float32),
                         jnp.transpose(f_pre, (0, 2, 1)).astype(jnp.float32))
    ht = jnp.transpose(ht, (0, 2, 1, 3))
    hm = jax.nn.sigmoid(o.astype(jnp.float32)).reshape(B, S, N_HEADS_2, HEAD_DIM) * ht
    mu = jnp.mean(hm, axis=-1, keepdims=True)
    var = jnp.mean(jnp.square(hm - mu), axis=-1, keepdims=True)
    hm = (hm - mu) * lax.rsqrt(var + EPS) * mlstm_norm_g.astype(jnp.float32).reshape(N_HEADS_2, HEAD_DIM)
    hm = hm.reshape(B, S, D_MLSTM).astype(h.dtype)

    y = jnp.concatenate([u, hm], axis=-1)
    return jnp.einsum("bse,ed->bsd", y, w_out)

def hierarchical_moe(h, rg_w, rg_b, re_w, re_b, w_gate, w_up, w_down):
    B, S, D = h.shape
    T = B * S
    xt = h.reshape(T, D)
    group_logits = (xt @ rg_w + rg_b).astype(jnp.float32)
    group_prob = jax.nn.softmax(group_logits, axis=-1)
    grp = jnp.argmax(group_logits, axis=-1).astype(jnp.int32)
    p_grp = jnp.take_along_axis(group_prob, grp[:, None], axis=-1)
    expert_logits = (xt @ re_w + re_b).astype(jnp.float32).reshape(T, N_GROUPS, EXPERTS_PER_GROUP)
    in_group = expert_logits[jnp.arange(T), grp]
    top_val, top_idx = lax.top_k(in_group, TOP_K)
    gate = p_grp * jax.nn.softmax(top_val, axis=-1)
    expert_id = grp[:, None] * EXPERTS_PER_GROUP + top_idx.astype(jnp.int32)

    n_assign = T * TOP_K
    e_flat = expert_id.reshape(-1)
    tok_flat = jnp.repeat(jnp.arange(T, dtype=jnp.int32), TOP_K)
    g_flat = gate.reshape(-1)
    order = jnp.argsort(e_flat)
    e_sorted, tok_sorted, g_sorted = e_flat[order], tok_flat[order], g_flat[order]
    counts = jnp.zeros((N_EXPERTS,), jnp.int32).at[e_flat].add(1)
    starts = jnp.cumsum(counts) - counts
    padded = (counts + MOE_BLOCK - 1) // MOE_BLOCK * MOE_BLOCK
    padded_ends = jnp.cumsum(padded)
    padded_starts = padded_ends - padded
    dest = padded_starts[e_sorted] + (jnp.arange(n_assign, dtype=jnp.int32) - starts[e_sorted])
    n_blocks = -(-n_assign // MOE_BLOCK) + N_EXPERTS
    n_slots = n_blocks * MOE_BLOCK
    slot_tok = jnp.zeros((n_slots,), jnp.int32).at[dest].set(tok_sorted)
    slot_gate = jnp.zeros((n_slots,), jnp.float32).at[dest].set(g_sorted)
    block_start = jnp.arange(n_blocks, dtype=jnp.int32) * MOE_BLOCK
    block_expert = jnp.minimum(jnp.sum(block_start[:, None] >= padded_ends[None, :], axis=1),
                               N_EXPERTS - 1).astype(jnp.int32)

    xs = xt[slot_tok].reshape(n_blocks, MOE_BLOCK, D)

    def expert_block(args):
        xb, e = args
        a = xb @ w_gate[e]
        u = xb @ w_up[e]
        return (jax.nn.silu(a) * u) @ w_down[e]

    ys = lax.map(expert_block, (xs, block_expert)).reshape(n_slots, D)
    ys = ys * slot_gate[:, None].astype(ys.dtype)
    out = jnp.zeros((T, D), ys.dtype).at[slot_tok].add(ys)
    return out.reshape(B, S, D).astype(h.dtype)

def second_inputs(seed: int = 0) -> dict:
    key = jax.random.key(seed)
    ks = jax.random.split(key, 21)
    f32 = jnp.float32
    L = DEPTH

    def nrm(k, shape, scale):
        return jax.random.normal(k, shape, f32) * scale

    b_in = nrm(ks[3], (L, D_IN_2), 0.02)
    b_in = b_in.at[:, D_IN_2 - N_HEADS_2:].add(jnp.linspace(F_BIAS_LO, F_BIAS_HI, N_HEADS_2, dtype=f32))
    return {
        "x": nrm(ks[0], (BATCH, SEQ, D_MODEL), 1.0),
        "norm_mix_g": 1.0 + nrm(ks[1], (L, D_MODEL), 0.02),
        "w_in": nrm(ks[2], (L, D_MODEL, D_IN_2), D_MODEL ** -0.5),
        "b_in": b_in,
        "conv_w": nrm(ks[4], (L, CONV_WIDTH, D_CONV), CONV_WIDTH ** -0.5),
        "conv_b": nrm(ks[5], (L, D_CONV), 0.02),
        "conv_ln_g": 1.0 + nrm(ks[6], (L, D_CONV), 0.02),
        "conv_ln_b": nrm(ks[7], (L, D_CONV), 0.02),
        "qk_conv_w": nrm(ks[8], (L, QK_CONV_WIDTH, 2 * D_MLSTM), QK_CONV_WIDTH ** -0.5),
        "qk_conv_b": nrm(ks[9], (L, 2 * D_MLSTM), 0.02),
        "mlstm_norm_g": 1.0 + nrm(ks[10], (L, D_MLSTM), 0.02),
        "w_out": nrm(ks[11], (L, D_MIX, D_MODEL), D_MIX ** -0.5),
        "norm_ffn_g": 1.0 + nrm(ks[12], (L, D_MODEL), 0.02),
        "router_group_w": nrm(ks[13], (L, D_MODEL, N_GROUPS), D_MODEL ** -0.5),
        "router_group_b": nrm(ks[14], (L, N_GROUPS), 0.01),
        "router_expert_w": nrm(ks[15], (L, D_MODEL, N_EXPERTS), D_MODEL ** -0.5),
        "router_expert_b": nrm(ks[16], (L, N_EXPERTS), 0.01),
        "expert_w_gate": nrm(ks[17], (L, N_EXPERTS, D_MODEL, D_EXPERT), D_MODEL ** -0.5),
        "expert_w_up": nrm(ks[18], (L, N_EXPERTS, D_MODEL, D_EXPERT), D_MODEL ** -0.5),
        "expert_w_down": nrm(ks[19], (L, N_EXPERTS, D_EXPERT, D_MODEL), D_EXPERT ** -0.5),
        "final_norm_g": 1.0 + nrm(ks[20], (D_MODEL,), 0.02),
    }

def second_block(x, norm_mix_g, w_in, b_in, conv_w, conv_b, conv_ln_g, conv_ln_b,
              qk_conv_w, qk_conv_b, mlstm_norm_g, w_out, norm_ffn_g,
              router_group_w, router_group_b, router_expert_w, router_expert_b,
              expert_w_gate, expert_w_up, expert_w_down, final_norm_g):
    for l in range(DEPTH):
        h = rmsnorm_2(x, norm_mix_g[l])
        x = x + hybrid_mixer(h, w_in[l], b_in[l], conv_w[l], conv_b[l], conv_ln_g[l], conv_ln_b[l],
                             qk_conv_w[l], qk_conv_b[l], mlstm_norm_g[l], w_out[l])
        h = rmsnorm_2(x, norm_ffn_g[l])
        x = x + hierarchical_moe(h, router_group_w[l], router_group_b[l],
                                 router_expert_w[l], router_expert_b[l],
                                 expert_w_gate[l], expert_w_up[l], expert_w_down[l])
    return rmsnorm_2(x, final_norm_g)


def setup_inputs(seed=0):
    out = dict(first_inputs(seed))
    for name, value in second_inputs(seed + 1).items():
        if name != "x":
            out[name + "_2"] = value
    return out


def reference(
    x, c, ctx, c_ctx, ada_w, ada_b, norm1_g, norm2_g, w_in, b_gate, w_fourier, q_norm_g, w_qb,
    kv_norm_g, w_kvb, q_gain, k_gain, w_mla_o, w_out, w_up, w_down, norm_mix_g_2, w_in_2,
    b_in_2, conv_w_2, conv_b_2, conv_ln_g_2, conv_ln_b_2, qk_conv_w_2, qk_conv_b_2,
    mlstm_norm_g_2, w_out_2, norm_ffn_g_2, router_group_w_2, router_group_b_2,
    router_expert_w_2, router_expert_b_2, expert_w_gate_2, expert_w_up_2, expert_w_down_2,
    final_norm_g_2,
):
    x = first_block(
        x, c, ctx, c_ctx, ada_w, ada_b, norm1_g, norm2_g, w_in, b_gate, w_fourier, q_norm_g,
        w_qb, kv_norm_g, w_kvb, q_gain, k_gain, w_mla_o, w_out, w_up, w_down,
    )
    return second_block(
        x, norm_mix_g_2, w_in_2, b_in_2, conv_w_2, conv_b_2, conv_ln_g_2, conv_ln_b_2,
        qk_conv_w_2, qk_conv_b_2, mlstm_norm_g_2, w_out_2, norm_ffn_g_2, router_group_w_2,
        router_group_b_2, router_expert_w_2, router_expert_b_2, expert_w_gate_2, expert_w_up_2,
        expert_w_down_2, final_norm_g_2,
    )


_drawn_inputs = setup_inputs


def setup_inputs(seed=0):
    import zlib

    import numpy as np

    out = dict(_drawn_inputs(seed))
    spreads = {}
    factors = {'ctx': 3.928,
     'norm1_g': 4.459,
     'b_gate': 8.0,
     'q_norm_g': 8.0,
     'kv_norm_g': 8.0,
     'q_gain': 8.0,
     'k_gain': 8.0,
     'conv_b_2': 3.221,
     'conv_ln_g_2': 4.904,
     'conv_ln_b_2': 4.77,
     'qk_conv_b_2': 5.825,
     'mlstm_norm_g_2': 3.062,
     'norm_ffn_g_2': 2.908,
     'router_group_b_2': 8.0,
     'router_expert_b_2': 5.622,
     'final_norm_g_2': 2.806}
    for name, (base, spread) in spreads.items():
        noise = np.random.default_rng([zlib.crc32(name.encode()), seed]).standard_normal(out[name].shape)
        drawn = base * np.exp(spread * noise) if base else spread * noise
        out[name] = __import__('jax').numpy.asarray(drawn.astype(out[name].dtype))
    for name, factor in factors.items():
        out[name] = (out[name] * factor).astype(out[name].dtype)
    return out
```

```python
from contextlib import ExitStack

import concourse.bass as bass
from concourse import mybir
import numpy as np

F32 = mybir.dt.float32
FR = mybir.dt.float32r
I32 = mybir.dt.int32
U32 = mybir.dt.uint32
ALU = mybir.AluOpType
ACT = mybir.ActivationFunctionType
AX = mybir.AxisListType

P = 128
T = 512
TC = 256
D = 1024
DK = 8
EPS = 1e-6
NEXP = 32
NOV = 7
NBLK = NEXP + NOV
BIG = 1.0e30
SLOTW = 4096


def rope_tables():
    rows = T // 64
    row = np.repeat(np.arange(rows, dtype=np.float32), 64)
    col = np.tile(np.arange(64, dtype=np.float32), rows)
    freqs = (np.float32(10000.0) ** (-np.arange(8, dtype=np.float32) / np.float32(8))).astype(np.float32)
    ar = row[:, None] * freqs[None, :]
    ac = col[:, None] * freqs[None, :]
    ang = np.concatenate([ar, ar, ac, ac], axis=-1)
    return np.cos(ang).astype(np.float32), np.sin(ang).astype(np.float32)


def layout_constants():
    cols = {}
    n = 0
    for name, w in (("ident", 128), ("tri", 128), ("mask", 128), ("sel", 512), ("rot", 96), ("iota", 32),
                    ("e128", 32), ("dftc", 256), ("j7", 8), ("vals", 8)):
        cols[name] = (n, w)
        n += w
    return cols, n


def constants():
    cols, n = layout_constants()
    c = np.zeros((P, n), np.float32)

    def put(name, a):
        o, w = cols[name]
        c[:a.shape[0], o:o + a.shape[1]] = a

    i = np.arange(P)
    put("ident", np.eye(P))
    put("tri", (i[:, None] < i[None, :]).astype(np.float32))
    put("mask", np.where(i[:, None] <= i[None, :], 0.0, -BIG))
    sel = np.zeros((4, 4, 128))
    for h in range(4):
        sel[h, h, :] = 1
    put("sel", sel.reshape(4, 512))
    rot = np.zeros((96, 96))
    for j in range(8):
        rot[64 + 8 + j, 64 + j] = -1.0
        rot[64 + j, 64 + 8 + j] = 1.0
        rot[64 + 24 + j, 64 + 16 + j] = -1.0
        rot[64 + 16 + j, 64 + 24 + j] = 1.0
    put("rot", rot)
    put("iota", np.tile(np.arange(32), (P, 1)))
    put("e128", np.tile(np.arange(32) * 128, (P, 1)))
    ch = 2 * np.pi * ((i[:, None] * i[None, :]) % P) / P
    put("dftc", np.concatenate([np.cos(ch), np.sin(ch)], axis=1))
    put("j7", np.tile(np.arange(8), (P, 1)))
    put("vals", i[:, None] + 128 * np.arange(8)[None, :])
    s = np.arange(T)
    an = 2 * np.pi * ((s[:, None] * s[None, :]) % T) / T
    dfts = np.concatenate([np.cos(an), -np.sin(an)], axis=1) / 256.0
    cos, sin = rope_tables()
    rope = np.concatenate([cos.T, sin.T], axis=1)
    return c, dfts.astype(np.float32), np.ascontiguousarray(rope.astype(np.float32))


class Queue:

    def __init__(self, name, sem):
        self.name, self.sem, self.n, self.items = name, sem, 0, []

    def add(self, fn, after=(), inc=True):
        if inc:
            self.n += 1
        self.items.append((fn, after, self.sem if inc else None, 1))
        return (self.sem, self.n)

    def dma(self, fn, sem, count, after=()):
        self.items.append((fn, after, sem, 16))
        return (sem, 16 * count)

    def emit(self, eng):
        seen = {}

        def wait(after):
            for tok in after:
                while callable(tok):
                    tok = tok()
                if tok is None:
                    continue
                if isinstance(tok, list):
                    wait(tok)
                    continue
                s, v = tok
                if seen.get(id(s), 0) < v:
                    eng.wait_ge(s, v)
                    seen[id(s)] = v

        for fn, after, sem, by in self.items:
            wait(after)
            ins = fn(eng)
            if sem is not None:
                ins.then_inc(sem, by)


def program(nc, A, out):
    ctx = ExitStack()
    with ctx:
        build(nc, A, out, ctx)


def build(nc, A, out, ctx):
    def sb(name, shape, dt=F32):
        return ctx.enter_context(nc.sbuf_tensor(name, shape, dt))

    def sem(name):
        return ctx.enter_context(nc.semaphore(name))

    def pooled(fn, after=()):
        return pool.add(fn, list(after) + [(pool.sem, pool.n)])

    pe, act, dve, pool, sp = (Queue(n, sem("q_" + n)) for n in ("pe", "act", "dve", "pool", "sp"))
    dma_sems = [0]

    def load(q, dst, src, after=(), **kw):
        dma_sems[0] += 1
        s = sem(f"d{dma_sems[0]}")
        return q.dma(lambda e: e.dma_start(dst, src, **kw), s, 1, after)

    base0 = (nc.sbuf_base + 31) // 32 * 32
    NAR = 50400
    slab = ctx.enter_context(nc.sbuf_tensor("slab", [P, NAR], F32))
    made = [0]

    def at(off, shape, dt=F32):
        made[0] += 1
        t = nc.alloc_sbuf_tensor_at(f"t{made[0]}", [P] + list(shape), dt, offset=base0 + 4 * off, align_bytes=4)
        return t[tuple(slice(None) for _ in range(len(shape) + 1))]

    O_HH, O_CST, O_SCR, O_RST, O_RAW, O_HL, PH = 4096, 12288, 13632, 14656, 15168, 21312, 33600

    class Unit:
        pass

    class Place:

        def __init__(self, off, hl, free=None):
            self.free = free
            if hl:
                self.hi, self.lo = at(off, [2048], FR), at(off + 2048, [2048], FR)
            else:
                made[0] += 1
                self.raw, self.sem, self.count = at(off, [2048]), sem(f"rs{made[0]}"), 0

    raws = [Place(O_RAW + 2048 * i, False) for i in range(3)]
    hls = [Place(O_HL + 4096 * i, True) for i in range(3)]
    units = []
    state = {"queued": 0, "used": 0}

    def stream(view, split=True, guard=None):
        u = Unit()
        u.rp = raws.pop(0)
        raws.append(u.rp)
        u.k = view.shape[1]
        u.w = u.k * view.shape[2]
        u.raw = u.rp.raw[:, 0:u.w].rearrange("p (k n) -> p k n", k=u.k)
        u.rp.count += 1
        u.split, u.guard, u.read = split, guard, None
        before = u.rp.free
        u.rp.free = lambda: u.read
        u.tok = sp.dma(lambda e: e.dma_start(u.raw, view), u.rp.sem, u.rp.count, [before])
        units.append(u)

    def convert(u):
        if not u.split:
            return
        h = hls.pop(0)
        hls.append(h)
        u.hi = h.hi[:, 0:u.w].rearrange("p (k n) -> p k n", k=u.k)
        u.lo = h.lo[:, 0:u.w].rearrange("p (k n) -> p k n", k=u.k)
        before = h.free
        h.free = lambda: u.done_with
        t = act.add(lambda e: e.activation(u.hi, u.raw, ACT.Copy), [u.tok, before] + (u.guard() if u.guard else []))
        u.done = dve.add(lambda e: e.tensor_tensor(u.lo, u.raw, u.hi.bitcast(F32), ALU.subtract), [t])
        u.read = u.done

    AHEAD = [2]

    def use():
        n = state["used"]
        state["used"] += 1
        while state["queued"] < min(n + 1 + AHEAD[0], len(units)):
            if units[state["queued"]].guard is HOLD and state["queued"] > n:
                break
            convert(units[state["queued"]])
            state["queued"] += 1
        return units[n]

    def HOLD():
        return [(pe.sem, pe.n), (act.sem, act.n), (dve.sem, dve.n)]

    def give(u, tok):
        if u.split:
            u.done_with = tok
        else:
            u.read = tok

    def tri(w, x):
        return [(w[0], x[0]), (w[0], x[1]), (w[1], x[0])]

    banks = [ctx.enter_context(nc.psum_tensor(f"ps{i}", [P, 512], F32)) for i in range(8)]
    bank_free = [None] * 8
    bank_idle = list(range(8))

    class Bank:

        def __init__(self):
            self.i = bank_idle.pop(0)
            self.t = banks[self.i]
            self.wait = bank_free[self.i]

        def free(self, tok):
            assert self.i not in bank_idle
            bank_free[self.i] = tok
            bank_idle.append(self.i)

    def bank():
        return Bank()

    def mm(out_ap, pairs, after=()):
        n = len(pairs)
        for i, (l, r) in enumerate(pairs):
            tok = pe.add(lambda e, l=l, r=r, i=i: e.matmul(out_ap, l, r, start=(i == 0), stop=(i == n - 1)),
                         after if i == 0 else (), inc=(i == n - 1))
        return tok

    xT = at(0, [DK, T])
    hH = at(O_HH, [DK, T], FR)
    hL = at(O_HH + 4096, [DK, T], FR)

    ccols, cw = layout_constants()
    cst = at(O_CST, [cw])

    def C(name):
        o, w = ccols[name]
        return cst[:, o:o + w]

    ident = C("ident")
    ones = {}
    vA = sb("vA", [P, 128])
    vB = sb("vB", [P, 128])
    vC = sb("vC", [P, 128])
    gains = sb("gains", [P, 8])
    modc = sb("modc", [P, 48, 2])
    sil = sb("sil", [P, 16])
    A1 = sb("A1", [P, 8, 2])
    A2 = sb("A2", [P, 8])
    oneD = sb("oneD", [P, 4])
    oneQ = sb("oneQ", [P, 4])
    oneK = sb("oneK", [P, 128])
    oneH = sb("oneH", [P, 128])
    one1 = sb("one1", [P, 128])
    one5 = sb("one5", [P, 128])
    eps = sb("eps", [P, 1])
    scr = at(O_SCR, [2, 512])
    rst = at(O_RST, [512])

    hd_ = nc.dram_tensor("h_scratch", [T, D], F32, kind="Internal").ap()
    yd = nc.dram_tensor("y_scratch", [2 * T, D], F32, kind="Internal").ap()
    tbl = nc.dram_tensor("slot_table", [NBLK * P, 1], F32, kind="Internal").ap()

    t_cst = load(act, cst, A["cst"])
    tm = None
    for t, v in ((oneD, 1.0 / 1024), (oneQ, 1.0 / 256), (oneK, 1.0 / 128), (oneH, 1.0 / 96), (one1, 1.0),
                 (one5, 1.0 / 512), (eps, EPS)):
        tm = pool.add(lambda e, t=t, v=v: e.memset(t[:, :], v))
    t_one = tm
    z32 = sb("z32", [P, 32])
    t_z32 = pool.add(lambda e: e.memset(z32[:, :], 0.0))
    none = at(PH + 16400, [P])[0:NBLK]
    t_none = pool.add(lambda e: e.memset(none, 4096.0))
    t_tbl = load(act, tbl.rearrange("(b p) a -> b (p a)", p=P), none, [t_none])

    vr = at(PH + 12288, [3, 128])
    va = {}
    rowsA = [("ada_b", 48), ("norm1_g", 8), ("norm2_g", 8), ("b_gate", 16), ("q_norm_g", 2), ("kv_norm_g", 1),
             ("c", 8), ("c_ctx", 8), ("norm_mix_g_2", 8), ("norm_ffn_g_2", 8), ("conv_b_2", 4),
             ("conv_ln_g_2", 4), ("conv_ln_b_2", 4)]
    rowsB = [("b_in_2", 24), ("qk_conv_b_2", 8), ("mlstm_norm_g_2", 4), ("qk_conv_w_2", 32)]
    rowsC = [("conv_w_2", 124)]
    s_v = sem("s_v")
    nv = 0
    t_v0 = pool.add(lambda e: e.memset(vr[:, :, :], 0.0))
    for j, rows in enumerate((rowsA, rowsB, rowsC)):
        o = 0
        for name, n in rows:
            va[name] = (j, o)
            a = A[name]
            if name == "b_in_2":
                a = a[:, 0:3072]
            shp = a.shape
            if len(shp) == 1:
                flat = a.rearrange("(r c) -> r c", c=128)
            elif len(shp) == 2:
                flat = a.rearrange("a (r c) -> (a r) c", c=128) if shp[0] == 1 else None
            else:
                flat = a.rearrange("a w (r c) -> (a w r) c", c=128)
            nv += 1
            act.dma(lambda e, j=j, o=o, n=n, f=flat: e.dma_start(vr[o:o + n, j, :], f[0:n, :]), s_v, nv, [t_v0])
            o += n
    t_vl = (s_v, 16 * nv)
    t_g = []
    for j, name in enumerate(("q_gain", "k_gain")):
        t_g.append(load(act, gains[0:96, j:j + 1], A[name].rearrange("a n -> n a")))
    t_g.append(load(act, gains[0:4, 2:3], A["b_in_2"][:, 3072:3076].rearrange("a n -> n a")))
    t_g.append(load(act, gains[0:4, 3:4], A["b_in_2"][:, 3076:3080].rearrange("a n -> n a")))
    b = bank()
    for j in range(3):
        t = pe.add(lambda e, j=j, b=b: e.transpose(b.t[:, j * 128:(j + 1) * 128], vr[:, j, :], ident), [t_vl, t_cst, t_v0])
    for j, v in enumerate((vA, vB, vC)):
        t_vc = dve.add(lambda e, j=j, v=v, b=b: e.tensor_copy(v[:, :], b.t[:, j * 128:(j + 1) * 128]), [t])
    b.free(t_vc)

    def col(name, i=0):
        j, o = va[name]
        v = (vA, vB, vC)[j]
        return v[:, o + i:o + i + 1]

    def cols(name, n, step=1):
        j, o = va[name]
        return (vA, vB, vC)[j][:, o:o + n]

    xn = at(PH, [4, 1024])
    cn = at(PH + 4096, [2, 1024])
    ctxT = at(PH + 6144, [8, 256])
    t_xl = load(sp, xn, A["x"][0].rearrange("(t p) d -> p t d", p=P))
    t_cl = load(sp, cn, A["ctx"][0].rearrange("(t p) d -> p t d", p=P))
    t_x = None
    for d in range(DK):
        b = bank()
        for i in range(4):
            t = pe.add(lambda e, d=d, i=i, b=b: e.transpose(b.t[:, i * 128:(i + 1) * 128],
                                                          xn[:, i, d * 128:(d + 1) * 128], ident),
                       [t_xl, t_cst, b.wait])
        t_x = dve.add(lambda e, d=d, b=b: e.tensor_copy(xT[:, d, :], b.t[:, :]), [t])
        b.free(t_x)
    for d in range(DK):
        b = bank()
        for i in range(2):
            t = pe.add(lambda e, d=d, i=i, b=b: e.transpose(b.t[:, i * 128:(i + 1) * 128],
                                                          cn[:, i, d * 128:(d + 1) * 128], ident),
                       [t_cl, b.wait])
        t_c = act.add(lambda e, d=d, b=b: e.activation(ctxT[:, d, :], b.t[:, 0:256], ACT.Copy), [t])
        b.free(t_c)

    j, oc = va["c"]
    t_sg = act.add(lambda e: e.activation(sil[:, :], vA[:, oc:oc + 16], ACT.Sigmoid), [t_vc])
    t_sil = dve.add(lambda e: e.tensor_tensor(sil[:, :], sil[:, :], vA[:, oc:oc + 16], ALU.mult), [t_sg])
    silh = sb("silh", [P, 4, 8], FR)
    for q in range(2):
        t_sh = act.add(lambda e, q=q: e.activation(silh[:, 2 * q, :], sil[:, 8 * q:8 * q + 8], ACT.Copy), [t_sil])
        t_sl = dve.add(lambda e, q=q: e.tensor_tensor(silh[:, 2 * q + 1, :], sil[:, 8 * q:8 * q + 8],
                                                      silh[:, 2 * q, :].bitcast(F32), ALU.subtract), [t_sh])
    ada = A["ada_w"][0].rearrange("(k p) n -> p k n", p=P)
    rowbuf = sb("rowbuf", [4, 512])
    row_free = [None]
    modtok = {}
    mc = sb("mc", [P, 4, 2])

    def mod_chunk(j):
        b = bank()
        for half in range(2):
            u = use()
            for k in range(4):
                for w in (u.hi, u.lo):
                    kk = 4 * half + k
                    first, fin = kk == 0 and w is u.hi, kk == 7 and w is u.lo
                    t = pe.add(lambda e, w=w, k=k, kk=kk, first=first, fin=fin: e.matmul(
                        b.t[0:4, :], silh[:, :, kk], w[:, k, :], start=first, stop=fin),
                        [u.done, t_sl, b.wait] if k == 0 else (), inc=(k == 3 and w is u.lo))
            give(u, t)
        t = act.add(lambda e: e.activation(rowbuf[:, :], b.t[0:4, :], ACT.Copy), [t, row_free[0]])
        b.free(t)
        b2 = bank()
        for i in range(4):
            t2 = pe.add(lambda e, i=i: e.transpose(b2.t[:, 4 * i:4 * i + 4], rowbuf[:, i * 128:(i + 1) * 128],
                                                   ident[0:4, 0:4]), [t, b2.wait])
        row_free[0] = t2
        _, ob = va["ada_b"]
        v = b2.t[:, 0:16].rearrange("p (i q c) -> p i q c", i=4, q=2)
        t3 = dve.add(lambda e: e.tensor_copy(mc[:, :, :], v[:, :, :, 1]), [t2, modtok.get(j - 1)])
        t3 = dve.add(lambda e: e.tensor_tensor(mc[:, :, :], v[:, :, :, 0], mc[:, :, :], ALU.add), [t3])
        for q in range(2):
            t3 = dve.add(lambda e, q=q: e.tensor_tensor(
                modc[:, 4 * j:4 * j + 4, q], mc[:, :, q], vA[:, ob + 4 * j:ob + 4 * j + 4], ALU.add), [t3, t_vc])
        b2.free(t3)
        modtok[j] = t3

    win = A["w_in"][0].rearrange("(k p) n -> p k n", p=P)
    win2 = A["w_in_2"][0].rearrange("(k p) n -> p k n", p=P)
    dft_d = A["dfts"].rearrange("(t p) n -> p t n", p=P)

    def cols256(v, c0, c1):
        for c in range(c0, c1, 256):
            stream(v[:, :, c:min(c + 256, c1)])

    def stream_mod(js):
        for j in js:
            for half in range(2):
                stream(ada[:, 4 * half:4 * half + 4, j * 512:(j + 1) * 512])

    stream_mod(range(4))
    for j in range(4):
        mod_chunk(j)
    for q in range(2):
        t_a1 = dve.add(lambda e, q=q: e.scalar_tensor_tensor(
            out=A1[:, :, q], in0=modc[:, 8:16, q], scalar=1.0, in1=cols("norm1_g", 8), op0=ALU.add,
            op1=ALU.mult), [modtok[3]])

    scr_free = [None, None]
    rst_free = [None]

    rcol = sb("rcol", [P, 4])

    class Norm:

        def __init__(self, src, nd, n, one):
            self.src, self.nd, self.n, self.one = src, nd, n, one
            self.b = bank()
            self.sq = {}

        def square(self, d, after):
            self.sq[d] = act.add(lambda e: e.activation(scr[:, d % 2, 0:self.n], self.src(d), ACT.Square),
                                 list(after) + [scr_free[d % 2]])

        def sums(self, d):
            for i in range(self.n // 128):
                self.t = pe.add(lambda e, i=i: e.matmul(
                    self.b.t[:, i:i + 1], scr[:, d % 2, i * 128:(i + 1) * 128], self.one[:, 0:1],
                    start=(d == 0 and i == 0), stop=(d == self.nd - 1 and i == self.n // 128 - 1)),
                    [self.sq[d], t_one, self.b.wait])
            scr_free[d % 2] = self.t

        def finish(self):
            nt = self.n // 128
            t = act.add(lambda e: e.activation(rcol[:, 0:nt], self.b.t[:, 0:nt], ACT.Sqrt, bias=eps[:, :]), [self.t])
            self.b.free(t)
            return spread(rcol[:, 0:nt], nt, dve.add(lambda e: e.reciprocal(rcol[:, 0:nt], rcol[:, 0:nt]), [t]))

        def all(self, after):
            for d in range(self.nd):
                self.square(d, after)
                self.sums(d)
            return self.finish()

    def spread(colv, nt, tok):
        t = dve.add(lambda e: e.tensor_tensor(
            rst[:, 0:nt * 128].rearrange("p (i c) -> p i c", i=nt), ident.unsqueeze(1).broadcast_to([P, nt, 128]),
            colv.unsqueeze(2).broadcast_to([P, nt, 128]), ALU.mult), [tok, rst_free[0], t_cst])
        b = bank()
        t = mm(b.t[:, 0:nt * 128], [(one1[:, :], rst[:, 0:nt * 128])], [t, b.wait])
        rst_free[0] = t
        return b, t

    def norm_split(src, nd, n, one, gain, shift, hi, lo, after, norm=None):
        b, t = norm.finish() if norm else Norm(src, nd, n, one).all(after)
        t3 = [None] * nd

        def tail(d):
            r = d % 2
            if shift is None:
                t4 = dve.add(lambda e: e.tensor_tensor(lo(d), scr[:, r, 0:n], hi(d).bitcast(F32), ALU.subtract), [t3[d]])
            else:
                t4 = dve.add(lambda e: e.scalar_tensor_tensor(
                    out=lo(d), in0=scr[:, r, 0:n], scalar=shift(d), in1=hi(d).bitcast(F32), op0=ALU.add,
                    op1=ALU.subtract), [t3[d]])
            scr_free[r] = t4
            return t4

        for d in range(nd):
            r = d % 2
            if d > 1:
                tail(d - 2)
            t2 = dve.add(lambda e, d=d, r=r: e.scalar_tensor_tensor(out=scr[:, r, 0:n], in0=src(d), scalar=gain(d),
                                                                  in1=b.t[:, 0:n], op0=ALU.mult, op1=ALU.mult),
                         [t, scr_free[r]] + after)
            if shift is None:
                t3[d] = act.add(lambda e, d=d, r=r: e.activation(hi(d), scr[:, r, 0:n], ACT.Copy), [t2])
            else:
                t3[d] = act.add(lambda e, d=d, r=r: e.activation(hi(d), scr[:, r, 0:n], ACT.Identity, bias=shift(d)), [t2])
        b.free(t2)
        tail(nd - 2)
        return tail(nd - 1)

    def norm_plain(src, dst, nd, n, one, gain, after, norm=None):
        b, t = norm.finish() if norm else Norm(src, nd, n, one).all(after)
        for d in range(nd):
            t2 = dve.add(lambda e, d=d: e.scalar_tensor_tensor(out=dst(d), in0=src(d), scalar=gain(d),
                                                               in1=b.t[:, 0:n], op0=ALU.mult, op1=ALU.mult),
                         [t] + after)
        b.free(t2)
        return t2

    def wx(u, m0, mw, hi, lo, n0=0, n1=T, nk=8, k0=0):
        out_ = []
        for k in range(nk):
            out_ += tri((u.hi[:, k, m0:m0 + mw], u.lo[:, k, m0:m0 + mw]),
                        (hi[:, k0 + k, n0:n1], lo[:, k0 + k, n0:n1]))
        return out_

    hcH = at(PH + 8192, [8, 256], FR)
    hcL = at(PH + 8192 + 2048, [8, 256], FR)
    cols256(win, 512, 768)
    stream(win[:, :, 768:928])
    cols256(win, 0, 512)
    for i in range(2):
        stream(dft_d[:, 2 * i:2 * i + 2, :], split=False)
    wf_d = A["w_fourier"][0].rearrange("(k p) n -> p k n", p=P)
    wo_d = A["w_mla_o"][0].rearrange("(k p) n -> p k n", p=P)
    for i in range(2):
        stream(wf_d[:, :, i * 512:(i + 1) * 512])
    for i in range(8):
        c0 = 928 + 256 * i
        stream(win[:, :, c0:c0 + 256])
        stream_mod([4 + i])
    stream(wo_d[:, :, 0:512], guard=HOLD)
    stream(wo_d[:, :, 512:1024])
    cols256(A["w_out"][0].rearrange("(k p) n -> p k n", p=P), 0, 1024)
    wup = A["w_up"][0].rearrange("(k p) n -> p k n", p=P)
    wdn = A["w_down"][0].rearrange("(k p) n -> p k n", p=P)
    for ch in range(4):
        cols256(wup, ch * 1024, ch * 1024 + 1024)
        cols256(wdn[:, ch * 8:(ch + 1) * 8, :], 0, 1024)
    for c0 in (1024, 1536, 512, 0, 2048, 2560):
        cols256(win2, c0, c0 + 512)
    wo2 = A["w_out_2"][0].rearrange("(k p) n -> p k n", p=P)
    stream(wo2[:, :, 0:256], guard=HOLD)
    cols256(wo2, 256, 1024)

    t_hc = norm_split(lambda d: ctxT[:, d, :], 8, 256, oneD, lambda d: A1[:, d, 1:2], lambda d: modc[:, d, 1:2],
                      lambda d: hcH[:, d, :], lambda d: hcL[:, d, :], [t_c, t_a1])
    t_hx = norm_split(lambda d: xT[:, d, :], 8, T, oneD, lambda d: A1[:, d, 0:1], lambda d: modc[:, d, 0:1],
                      lambda d: hH[:, d, :], lambda d: hL[:, d, :], [t_x, t_a1])

    y = at(PH, [8, 512])
    qraw = at(PH, [2, 512])
    kvraw = at(PH + 1024, [768])
    qln = at(PH + 12672, [2, 512])
    kvn = at(PH + 13696, [768])
    kr = at(PH + 14464, [768])
    u = use()
    for m in range(2):
        b = bank()
        t = mm(b.t[:, :], wx(u, m * 128, 128, hH, hL), [u.done, t_hx, b.wait])
        t_qr = act.add(lambda e, m=m, b=b: e.activation(qraw[:, m, :], b.t[:, :], ACT.Copy), [t])
        b.free(t_qr)
    give(u, t)
    u = use()
    for n0, n1, o, hi, lo in ((0, 512, 0, hH, hL), (0, 256, 512, hcH, hcL)):
        nn = n1 - n0
        b = bank()
        t = mm(b.t[:, 0:nn], wx(u, 0, 128, hi, lo, n0, n1), [u.done, t_hc, b.wait])
        t_kvr = act.add(lambda e, b=b, nn=nn, o=o: e.activation(kvraw[:, o:o + nn], b.t[:, 0:nn], ACT.Copy), [t])
        b.free(t_kvr)
        b = bank()
        t = mm(b.t[0:32, 0:nn], wx(u, 128, 32, hi, lo, n0, n1), [b.wait])
        t_kr = act.add(lambda e, b=b, nn=nn, o=o: e.activation(kr[64:96, o:o + nn], b.t[0:32, 0:nn], ACT.Copy), [t, t_vc])
        b.free(t_kr)
    give(u, t)

    fT = at(PH + 2048, [4, 512])
    AB = at(PH + 4096, [4, 4, 256])
    fmH = at(PH + 8192, [4, 512], FR)
    fmL = at(PH + 8192 + 2048, [4, 512], FR)
    for m2 in range(2):
        u = use()
        for mi in range(2):
            m = 2 * m2 + mi
            b = bank()
            t = mm(b.t[:, :], wx(u, mi * 128, 128, hH, hL), [u.done, b.wait])
            t_f = act.add(lambda e, m=m, b=b: e.activation(fT[:, m, :], b.t[:, :], ACT.Copy), [t])
            b.free(t_f)
        give(u, t)
    t_qln = norm_plain(lambda d: qraw[:, d, :], lambda d: qln[:, d, :], 2, 512, oneQ, lambda d: col("q_norm_g", d),
                       [t_qr, t_vc])
    norm_plain(lambda d: kvraw[:, 0:512], lambda d: kvn[:, 0:512], 1, 512, oneK, lambda d: col("kv_norm_g"), [t_kvr])
    t_kvn = norm_plain(lambda d: kvraw[:, 512:768], lambda d: kvn[:, 512:768], 1, 256, oneK,
                       lambda d: col("kv_norm_g"), [t_kvr])
    for g in range(4):
        for t0 in range(0, 4, 2):
            b = bank()
            for i in range(2):
                t = mm(b.t[:, i * 256:(i + 1) * 256], [(fT[:, g, (t0 + i) * 128:(t0 + i + 1) * 128], C("dftc"))],
                       [t_f, b.wait])
            t_ab = dve.add(lambda e, b=b, g=g, t0=t0: e.tensor_copy(
                AB[:, t0:t0 + 2, g, :], b.t[:, :].rearrange("p (i c) -> p i c", i=2)), [t])
            b.free(t_ab)
    fb = [bank() for _ in range(4)]
    for half in range(2):
        u = use()
        for g in range(4):
            for i2 in range(2):
                i = 2 * half + i2
                for cs in range(2):
                    first, fin = i == 0 and cs == 0, i == 3 and cs == 1
                    t = pe.add(lambda e, g=g, i=i, i2=i2, cs=cs, u=u, first=first, fin=fin: e.matmul(
                        fb[g].t[:, :], AB[:, i, g, cs * 128:(cs + 1) * 128], u.raw[:, i2, cs * 512:(cs + 1) * 512],
                        start=first, stop=fin), [t_ab, u.tok, fb[g].wait], inc=(i2 == 1 and cs == 1))
            if half:
                t_f1 = act.add(lambda e, g=g: e.activation(fmH[:, g, :], fb[g].t[:, :], ACT.Copy), [t])
                t_fm = dve.add(lambda e, g=g: e.tensor_tensor(fmL[:, g, :], fb[g].t[:, :], fmH[:, g, :].bitcast(F32),
                                                              ALU.subtract), [t_f1])
                fb[g].free(t_fm)
        give(u, t)
    for half in range(2):
        u = use()
        for mi in range(4):
            m = 4 * half + mi
            b = bank()
            t = mm(b.t[:, :], wx(u, mi * 128, 128, fmH, fmL, nk=4), [u.done, t_fm, b.wait])
            t_y = act.add(lambda e, m=m, b=b: e.activation(y[:, m, :], b.t[:, :], ACT.Copy), [t, t_qln, t_kvn])
            b.free(t_y)
        give(u, t)
    ga = at(PH + 8192, [8, 512])
    for i in range(8):
        u = use()
        for mi in range(2):
            m = 2 * i + mi
            b = bank()
            t = mm(b.t[:, :], wx(u, mi * 128, 128, hH, hL), [u.done, b.wait])
            if m < 8:
                r = m % 2
                t = act.add(lambda e, b=b, m=m, r=r: e.activation(scr[:, r, :], b.t[:, :], ACT.Sigmoid,
                                                                bias=col("b_gate", m)), [t, scr_free[r]])
                b.free(t)
                t_y2 = dve.add(lambda e, m=m, r=r: e.tensor_tensor(y[:, m, :], y[:, m, :], scr[:, r, :], ALU.mult), [t, t_y])
                scr_free[r] = t_y2
            else:
                t_ga = act.add(lambda e, b=b, m=m: e.activation(ga[:, m - 8, :], b.t[:, :], ACT.Sigmoid,
                                                              bias=col("b_gate", m)), [t])
                b.free(t_ga)
        give(u, (pe.sem, pe.n))
        mod_chunk(4 + i)
    t_ge = (pe.sem, pe.n)
    t_a2 = dve.add(lambda e: e.scalar_tensor_tensor(out=A2[:, :], in0=modc[:, 32:40, 0], scalar=1.0,
                                                    in1=cols("norm2_g", 8), op0=ALU.add, op1=ALU.mult), [modtok[11]])

    attH = at(PH + 4096, [4, 512], FR)
    attL = at(PH + 4096 + 2048, [4, 512], FR)
    V = at(O_HH, [6, 512])
    wqb = at(O_HL + 3072, [2, 768])
    wkvb = at(PH + 15232, [1024])
    PT = [at(O_HH + 3072, [6, 512]), at(O_HL, [6, 512])]
    ph = [at(O_HH + 6144, [768]), at(O_HL + 8704, [768]), at(O_HL + 9472, [768]), at(O_HL + 10240, [768])]
    qhs = [at(O_HH + 7680, [512]), at(O_HL + 11008, [512])]
    ropet = at(O_HL + 4608, [1024])
    krs = at(O_HL + 5632, [768])
    rsk = at(O_HL + 6400, [768])
    khead = [at(O_HL + 7168, [768]), at(O_HL + 7936, [768])]
    sqk = kr[0:96]
    st = sb("st", [P, 4, 4])
    t_wk = load(act, wkvb, A["w_kvb"][0], [t_vc])
    t_wq = load(act, wqb, A["w_qb"][0].rearrange("(k p) n -> p k n", p=P), [t_ge])
    t_rp = load(act, ropet[64:96, :], A["rope"], [t_ge])
    cosv = ropet[64:96, 0:512]
    sinv = ropet[64:96, 512:1024]
    wkv_h = wkvb.rearrange("p (h c) -> p h c", h=8)
    krg = gains[64:96, 1:2]
    t_krz = pooled(lambda e: e.memset(krs[0:64, :], 0.0), [t_ge])
    t_krg = dve.add(lambda e: e.tensor_scalar(krs[64:96, :], kr[64:96, :], krg, None, ALU.mult), [t_kr, t_ge] + t_g)
    b = bank()
    t = pe.add(lambda e, b=b: e.matmul(b.t[0:96, :], C("rot")[0:96, :], krs[0:96, 0:512], start=True, stop=True),
               [t_krg, t_krz, b.wait])
    t1 = dve.add(lambda e, b=b: e.tensor_tensor(scr[64:96, 0, :], b.t[64:96, :], sinv, ALU.mult), [t, t_rp, scr_free[0]])
    b.free(t1)
    t2 = dve.add(lambda e: e.tensor_tensor(krs[64:96, 0:512], krs[64:96, 0:512], cosv, ALU.mult), [t1])
    t_krs = dve.add(lambda e: e.tensor_tensor(krs[64:96, 0:512], krs[64:96, 0:512], scr[64:96, 0, :], ALU.add), [t2])
    scr_free[0] = t_krs
    t_sqkr = act.add(lambda e: e.activation(sqk[64:96, :], kr[64:96, :], ACT.Square), [t_krg])
    for i in range(6):
        b = bank()
        t = mm(b.t[:, :], [(kvn[:, i * 128:(i + 1) * 128], wkv_h[:, :, 64:128])], [t_kvn, t_wk, b.wait])
        t_V = act.add(lambda e, i=i, b=b: e.activation(V[:, i, :], b.t[:, :], ACT.Copy), [t, t_ge])
        b.free(t_V)
    SC = float(96) ** -0.5
    head = [dict() for _ in range(8)]
    fre = {"kh": [None, None], "qh": [None, None], "pt": [None, None], "ph": [None] * 4, "sqk": None, "rsk": None}

    def rstd(b, t, n, dst, dst_free, pk=P):
        t = act.add(lambda e: e.activation(dst[0:pk, 0:n], b.t[0:pk, 0:n], ACT.Sqrt, bias=eps[0:pk, :]), [t, t_one, dst_free])
        b.free(t)
        return dve.add(lambda e: e.reciprocal(dst[0:pk, 0:n], dst[0:pk, 0:n]), [t])

    def prep_a(h):
        H = head[h]
        H["kb"] = [bank(), bank()]
        for b, n0, n1 in ((H["kb"][0], 0, 512), (H["kb"][1], 512, 768)):
            t = mm(b.t[0:64, 0:n1 - n0], [(wkv_h[:, h, 0:64], kvn[:, n0:n1])], [t_kvn, t_wk, b.wait])
            H["sqk"] = act.add(lambda e, b=b, n0=n0, n1=n1: e.activation(sqk[0:64, n0:n1], b.t[0:64, 0:n1 - n0], ACT.Square),
                               [t, fre["sqk"]])
        H["qb"] = b = bank()
        t = mm(b.t[0:96, :], [(wqb[:, k, h * 96:(h + 1) * 96], qln[:, k, :]) for k in range(2)], [t_wq, t_qln, b.wait])
        H["sqq"] = act.add(lambda e, b=b: e.activation(scr[0:96, 0, :], b.t[0:96, :], ACT.Square), [t, scr_free[0]])

    def prep_b(h):
        H = head[h]
        kh, qh = khead[h % 2], qhs[h % 2]
        for n0, n1 in ((0, 512), (512, 768)):
            b = bank()
            t3 = pe.add(lambda e, b=b, n0=n0, n1=n1: e.matmul(b.t[0:96, 0:n1 - n0], oneH[0:96, 0:96], sqk[:, n0:n1],
                                                             start=True, stop=True), [H["sqk"], t_sqkr, b.wait, t_one])
            t4 = act.add(lambda e, b=b, n0=n0, n1=n1: e.activation(rsk[0:96, n0:n1], b.t[0:96, 0:n1 - n0], ACT.Sqrt,
                                                                  bias=eps[0:96, :]), [t3, fre["rsk"]])
            b.free(t4)
        fre["sqk"] = t3
        b2 = bank()
        t2 = pe.add(lambda e, b2=b2: e.matmul(b2.t[0:96, :], oneH[0:96, 0:96], scr[0:96, 0, :], start=True, stop=True),
                    [H["sqq"], b2.wait])
        scr_free[0] = t2
        t3 = rstd(b2, t2, 512, rst, rst_free[0], 96)
        b = H["qb"]
        H["q1"] = dve.add(lambda e, b=b, qh=qh: e.scalar_tensor_tensor(
            out=qh[0:96, :], in0=b.t[0:96, :], scalar=gains[0:96, 0:1], in1=rst[0:96, :], op0=ALU.mult, op1=ALU.mult),
            [t3, fre["qh"][h % 2]] + t_g)
        b.free(H["q1"])
        rst_free[0] = H["q1"]
        t5 = dve.add(lambda e: e.reciprocal(rsk[0:96, :], rsk[0:96, :]), [t4])
        for b, n0, n1 in ((H["kb"][0], 0, 512), (H["kb"][1], 512, 768)):
            t6 = dve.add(lambda e, b=b, n0=n0, n1=n1, kh=kh: e.scalar_tensor_tensor(
                out=kh[0:64, n0:n1], in0=b.t[0:64, 0:n1 - n0], scalar=gains[0:64, 1:2], in1=rsk[0:64, n0:n1],
                op0=ALU.mult, op1=ALU.mult), [t5, fre["kh"][h % 2]] + t_g)
            b.free(t6)
        H["k2"] = pooled(lambda e, kh=kh: e.tensor_tensor(kh[64:96, :], krs[64:96, :], rsk[64:96, :], ALU.mult),
                           [t5, t_krs, fre["kh"][h % 2]])
        H["k1"] = t6
        fre["rsk"] = [t6, H["k2"]]

    def prep_c(h):
        H = head[h]
        qh = qhs[h % 2]
        b = bank()
        t5 = pe.add(lambda e, b=b, qh=qh: e.matmul(b.t[0:96, :], C("rot")[0:96, :], qh[0:96, :], start=True, stop=True),
                    [H["q1"], b.wait])
        t7 = pooled(lambda e, qh=qh: e.tensor_tensor(qh[64:96, :], qh[64:96, :], cosv, ALU.mult), [t5, t_rp])
        t6 = dve.add(lambda e, b=b: e.tensor_tensor(scr[64:96, 1, :], b.t[64:96, :], sinv, ALU.mult), [t5, scr_free[1]])
        b.free(t6)
        H["q"] = pooled(lambda e, qh=qh: e.tensor_tensor(qh[64:96, :], qh[64:96, :], scr[64:96, 1, :], ALU.add), [t7, t6])
        scr_free[1] = H["q"]

    S = {}

    def scores(n):
        h, i = divmod(n, 4)
        r = n % 4
        H = head[h]
        kh, qh = khead[h % 2], qhs[h % 2]
        sbk = [bank(), bank()]
        for b, n0, n1 in ((sbk[0], 0, 512), (sbk[1], 512, 768)):
            t = mm(b.t[:, 0:n1 - n0], [(qh[0:96, i * 128:(i + 1) * 128], kh[0:96, n0:n1])],
                   [H["q"], H["q1"], H["k1"], H["k2"], b.wait])
        if i == 3:
            fre["kh"][h % 2] = fre["qh"][h % 2] = t
        dve.add(lambda e, b=sbk[0]: e.tensor_reduce(st[:, r, 0:1], b.t[:, :], AX.X, ALU.max), [t, fre["ph"][r]])
        m2 = dve.add(lambda e, b=sbk[1]: e.tensor_reduce(st[:, r, 1:2], b.t[:, 0:256], AX.X, ALU.max), [])
        m3 = dve.add(lambda e: e.tensor_scalar(st[:, r, 2:3], st[:, r, 0:1], st[:, r, 1:2], -SC, ALU.max, ALU.mult), [m2])
        e1 = act.add(lambda e, b=sbk[0]: e.activation(ph[r][:, 0:512], b.t[:, :], ACT.Exp, bias=st[:, r, 2:3],
                                                    scale=SC, accum_out=st[:, r, 0:1]), [m3, fre["ph"][r]])
        e2 = act.add(lambda e, b=sbk[1]: e.activation(ph[r][:, 512:768], b.t[:, 0:256], ACT.Exp, bias=st[:, r, 2:3],
                                                    scale=SC, accum_out=st[:, r, 1:2]), [])
        sbk[0].free(e1)
        sbk[1].free(e2)
        d1 = dve.add(lambda e: e.tensor_tensor(st[:, r, 3:4], st[:, r, 0:1], st[:, r, 1:2], ALU.add), [e2])
        d2 = dve.add(lambda e: e.reciprocal(st[:, r, 3:4], st[:, r, 3:4]), [d1])
        S[n] = pooled(lambda e: e.tensor_scalar(ph[r], ph[r], st[:, r, 3:4], None, ALU.mult), [d2])

    def turn(n):
        h, i = divmod(n, 4)
        r = n % 4
        pt = PT[h % 2]
        for b0, nb in ((0, 4), (4, 2)):
            b = bank()
            for j in range(nb):
                t = pe.add(lambda e, b=b, j=j, b0=b0: e.transpose(
                    b.t[:, j * 128:(j + 1) * 128], ph[r][:, (b0 + j) * 128:(b0 + j + 1) * 128], ident), [S[n], b.wait])
            q, cp = (act, lambda e, o, a: e.activation(o, a, ACT.Copy)) if b0 == 0 else (dve, lambda e, o, a: e.tensor_copy(o, a))
            t_pt = q.add(lambda e, b=b, b0=b0, nb=nb, cp=cp: cp(
                e, pt[:, b0:b0 + nb, i * 128:(i + 1) * 128],
                b.t[:, 0:nb * 128].rearrange("p (j c) -> p j c", j=nb)), [t, fre["pt"][h % 2]])
            b.free(t_pt)
            head[h].setdefault("pt", []).append(t_pt)
        fre["ph"][r] = t

    def values(h):
        b = bank()
        pt = PT[h % 2]
        t = mm(b.t[0:64, :], [(V[:, j, h * 64:(h + 1) * 64], pt[:, j, :]) for j in range(6)], head[h]["pt"] + [t_V, b.wait])
        fre["pt"][h % 2] = t
        o = 64 * (h % 2)
        t1 = act.add(lambda e, b=b: e.activation(attH[o:o + 64, h // 2, :], b.t[0:64, :], ACT.Copy), [t])
        t2 = dve.add(lambda e, b=b: e.tensor_tensor(attL[o:o + 64, h // 2, :], b.t[0:64, :],
                                                    attH[o:o + 64, h // 2, :].bitcast(F32), ALU.subtract), [t1])
        b.free(t2)
        return t2

    prep_a(0)
    prep_b(0)
    prep_c(0)
    scores(0)
    scores(1)
    for n in range(32):
        h, i = divmod(n, 4)
        if h < 7:
            if i == 0:
                prep_a(h + 1)
            if i == 1:
                prep_b(h + 1)
            if i == 2:
                prep_c(h + 1)
        if n + 2 < 32:
            scores(n + 2)
        turn(n)
        if i == 0 and h:
            t_att = values(h - 1)
    t_att = values(7)

    for half in range(2):
        u = use()
        for mi in range(4):
            m = half * 4 + mi
            b = bank()
            r = m % 2
            t = mm(b.t[:, :], wx(u, mi * 128, 128, attH, attL, nk=4), [u.done, t_att, b.wait])
            t3 = dve.add(lambda e, b=b, m=m, r=r: e.tensor_tensor(scr[:, r, :], b.t[:, :], ga[:, m, :], ALU.mult),
                         [t, t_ga, scr_free[r]])
            b.free(t3)
            t4 = dve.add(lambda e, m=m, r=r: e.tensor_tensor(scr[:, r, :], y[:, m, :], scr[:, r, :], ALU.add), [t3])
            t5 = act.add(lambda e, m=m, r=r: e.activation(hH[:, m, :], scr[:, r, :], ACT.Copy), [t4])
            t_y = dve.add(lambda e, m=m, r=r: e.tensor_tensor(hL[:, m, :], scr[:, r, :], hH[:, m, :].bitcast(F32),
                                                             ALU.subtract), [t5])
            scr_free[r] = t_y
        give(u, t)

    def project(t_src, scale, hi, lo, t_scale=None, norm=None):
        for c in range(4):
            u = use()
            for mi in range(2):
                m = 2 * c + mi
                b = bank()
                t = mm(b.t[:, :], wx(u, mi * 128, 128, hi, lo), [u.done, t_src, b.wait])
                if scale is None:
                    t2 = dve.add(lambda e, b=b, m=m: e.tensor_tensor(xT[:, m, :], xT[:, m, :], b.t[:, :], ALU.add), [t, xprev[m]])
                else:
                    t2 = dve.add(lambda e, b=b, m=m: e.scalar_tensor_tensor(
                        out=xT[:, m, :], in0=b.t[:, :], scalar=scale(m), in1=xT[:, m, :], op0=ALU.mult, op1=ALU.add),
                        [t, t_scale, xprev[m]])
                xprev[m] = t2
                b.free(t2)
                if norm:
                    norm.square(m, [t2])
                    if m:
                        norm.sums(m - 1)
            give(u, t)
        if norm:
            norm.sums(7)
        return t2

    def xnorm():
        return Norm(lambda d: xT[:, d, :], 8, T, oneD)

    xprev = [None] * 8
    nx = xnorm()
    t_x = project(t_y, lambda m: modc[:, 16 + m, 0:1], hH, hL, modtok[11], nx)

    t_h = norm_split(lambda d: xT[:, d, :], 8, T, oneD, lambda d: A2[:, d:d + 1], lambda d: modc[:, 24 + d, 0:1],
                     lambda d: hH[:, d, :], lambda d: hL[:, d, :], [t_x, t_a2], nx)
    UH = [at(PH + 8192 * i, [8, 512], FR) for i in range(2)]
    UL = [at(PH + 8192 * i + 4096, [8, 512], FR) for i in range(2)]
    u_free = [None, None]
    t_u = [None] * 4

    def mlp_up(ch):
        q = ch % 2
        for c in range(4):
            u = use()
            for mi in range(2):
                m = 2 * c + mi
                r = m % 2
                b = bank()
                t = mm(b.t[:, :], wx(u, mi * 128, 128, hH, hL), [u.done, t_h, b.wait])
                t1 = act.add(lambda e, b=b, r=r: e.activation(scr[:, r, :], b.t[:, :], ACT.Relu), [t, scr_free[r]])
                t2 = dve.add(lambda e, b=b, r=r: e.tensor_tensor(scr[:, r, :], b.t[:, :], scr[:, r, :], ALU.mult), [t1])
                b.free(t2)
                t3 = act.add(lambda e, m=m, r=r: e.activation(UH[q][:, m, :], scr[:, r, :], ACT.Copy), [t2, u_free[q]])
                t_u[ch] = dve.add(lambda e, m=m, r=r: e.tensor_tensor(
                    UL[q][:, m, :], scr[:, r, :], UH[q][:, m, :].bitcast(F32), ALU.subtract), [t3])
                scr_free[r] = t_u[ch]
            give(u, t)

    for ch in range(4):
        mlp_up(ch)
        nx = xnorm() if ch == 3 else None
        t_x = project(t_u[ch], lambda m: modc[:, 40 + m, 0:1], UH[ch % 2], UL[ch % 2], modtok[11], nx)
        u_free[ch % 2] = (pe.sem, pe.n)

    t_pe = (pe.sem, pe.n)
    t_h = norm_split(lambda d: xT[:, d, :], 8, T, oneD, lambda d: col("norm_mix_g_2", d), None,
                     lambda d: hH[:, d, :], lambda d: hL[:, d, :], [t_x], nx)
    up = at(PH, [4, 542])
    acc = at(PH + 2168, [4, 512])
    qkp = at(PH + 4216, [8, 515])
    qkc = at(PH + 8336, [8, 512])
    vN = at(PH + 12432, [4, 512])
    og = at(PH + 14480, [4, 512])
    wif = at(PH + 16528, [8, 8])
    wifs = sb("wifs", [P, 8, 40], FR)
    wifH, wifL = wifs[:, :, 0:36], wifs[:, :, 4:40]
    kw = at(PH, [4, 512])
    t_z1 = pool.add(lambda e: e.memset(up[:, :, 0:30], 0.0), [t_pe])
    t_z2 = pool.add(lambda e: e.memset(qkp[:, :, 0:3], 0.0), [t_pe])
    t_wif = load(act, wif, win2[:, :, 3072:3080], [t_pe])
    t_wz = act.add(lambda e: e.activation(wifs[:, :, :], z32[:, 0:8].unsqueeze(2).broadcast_to([P, 8, 40]), ACT.Copy), [t_z32])
    for q in range(2):
        t_wz = act.add(lambda e, q=q: e.activation(wifH[:, :, 32 * q:32 * q + 4], wif[:, :, 4 * q:4 * q + 4], ACT.Copy),
                       [t_wif, t_wz])
    for q in range(2):
        t_wif = dve.add(lambda e, q=q: e.tensor_tensor(wifL[:, :, 32 * q:32 * q + 4], wif[:, :, 4 * q:4 * q + 4],
                                                       wifH[:, :, 32 * q:32 * q + 4].bitcast(F32), ALU.subtract), [t_wz])

    def bcol(i):
        return col("b_in_2", i)

    t_cv = [None] * 8
    for c in range(4):
        u = use()
        for mi in range(2):
            m = 2 * c + mi
            b = bank()
            t = mm(b.t[:, :], wx(u, mi * 128, 128, hH, hL), [u.done, t_h, b.wait])
            t_qk = act.add(lambda e, b=b, m=m: e.activation(qkp[:, m, 3:515], b.t[:, :], ACT.Identity, bias=bcol(8 + m)),
                           [t, t_z2])
            b.free(t_qk)
            for j in range(4):
                wc = col("qk_conv_w_2", j * 8 + m)
                if j == 0:
                    t2 = dve.add(lambda e, m=m, wc=wc: e.tensor_scalar(qkc[:, m, :], qkp[:, m, 0:512], wc,
                                                                      col("qk_conv_b_2", m), ALU.mult, ALU.add), [t_qk])
                else:
                    t2 = dve.add(lambda e, m=m, wc=wc, j=j: e.scalar_tensor_tensor(
                        out=qkc[:, m, :], in0=qkp[:, m, j:j + 512], scalar=wc, in1=qkc[:, m, :], op0=ALU.mult,
                        op1=ALU.add), [t2])
            t_cv[m] = t2
        give(u, t)
    sg = acc
    for c in range(2):
        u = use()
        for mi in range(2):
            m = 2 * c + mi
            b = bank()
            t = mm(b.t[:, :], wx(u, mi * 128, 128, hH, hL), [u.done, b.wait])
            t_s = act.add(lambda e, b=b, m=m: e.activation(sg[:, m, :], b.t[:, :], ACT.Sigmoid, bias=bcol(4 + m)), [t, t_pe])
            b.free(t_s)
        give(u, t)
    t_cu = [None] * 4
    for c in range(2):
        u = use()
        for mi in range(2):
            m = 2 * c + mi
            b = bank()
            t = mm(b.t[:, :], wx(u, mi * 128, 128, hH, hL), [u.done, b.wait])
            t_cu[m] = dve.add(lambda e, b=b, m=m: e.scalar_tensor_tensor(
                out=up[:, m, 30:542], in0=b.t[:, :], scalar=bcol(m), in1=sg[:, m, :], op0=ALU.add, op1=ALU.mult),
                [t, t_s, t_z1])
            b.free(t_cu[m])
        give(u, t)

    for m in range(8):
        r = m % 2
        t2 = act.add(lambda e, m=m, r=r: e.activation(scr[:, r, :], qkc[:, m, :], ACT.Sigmoid), [t_cv[m], scr_free[r]])
        kscale = 1.0 if m < 4 else float(128) ** -0.5
        t_qkc = dve.add(lambda e, m=m, r=r, ks=kscale: e.scalar_tensor_tensor(
            out=qkc[:, m, :], in0=qkc[:, m, :], scalar=ks, in1=scr[:, r, :], op0=ALU.mult, op1=ALU.mult), [t2])
        scr_free[r] = t_qkc

    taps = [(m, j) for m in range(4) for j in range(31)]
    conv = {"t": None}

    def convolve(n):
        for _ in range(n):
            if not taps:
                return
            m, j = taps.pop(0)
            wc = col("conv_w_2", j * 4 + m)
            if j == 0:
                conv["t"] = dve.add(lambda e, m=m, wc=wc: e.tensor_scalar(acc[:, m, :], up[:, m, 0:512], wc,
                                                             col("conv_b_2", m), ALU.mult, ALU.add), t_cu)
            else:
                conv["t"] = dve.add(lambda e, m=m, j=j, wc=wc: e.scalar_tensor_tensor(
                    out=acc[:, m, :], in0=up[:, m, j:j + 512], scalar=wc, in1=acc[:, m, :], op0=ALU.mult,
                    op1=ALU.add), [conv["t"]])

    brow = rowbuf[0:1, :]
    t_br = load(act, brow, A["b_in_2"][:, 2048:2560], [t_pe])
    for c in range(2):
        u = use()
        convolve(12)
        for i in range(4):
            vb = bank()
            prs = []
            for k in range(8):
                prs += tri((hH[:, k, i * 128:(i + 1) * 128], hL[:, k, i * 128:(i + 1) * 128]), (u.hi[:, k, :], u.lo[:, k, :]))
            t = mm(vb.t[:, 0:256], prs + [(one1[0:1, :], brow[0:1, c * 256:(c + 1) * 256])],
                   [u.done, t_br, vb.wait])
            t_vn = act.add(lambda e, i=i, c=c, vb=vb: e.activation(vN[:, i, c * 256:(c + 1) * 256],
                                                                 vb.t[:, 0:256], ACT.Copy), [t])
            vb.free(t_vn)
        give(u, t)
    for c in range(2):
        u = use()
        convolve(12)
        for mi in range(2):
            m = 2 * c + mi
            b = bank()
            t = mm(b.t[:, :], wx(u, mi * 128, 128, hH, hL), [u.done, b.wait])
            t_o = act.add(lambda e, b=b, m=m: e.activation(og[:, m, :], b.t[:, :], ACT.Sigmoid, bias=bcol(20 + m)), [t, t_tbl])
            b.free(t_o)
        give(u, t)
    g6 = at(PH + 4216, [6, 512])
    ga4 = [g6[0:4, i, :] for i in range(6)]
    aa, bc, Mm, negM, wi, ws = ga4
    ig, lf, em = aa, Mm, bc
    t0_ = rst[0:4, :]
    bi = bank()
    prs = []
    for k in range(8):
        prs += tri((wifH[:, k, :], wifL[:, k, :]), (hH[:, k, :], hL[:, k, :]))
    t_ig = mm(bi.t[0:36, :], prs, [t_wif, bi.wait])
    t_i = act.add(lambda e: e.activation(ig, bi.t[0:4, :], ACT.Identity, bias=gains[0:4, 2:3]), [t_ig, t_cv[7]] + t_g)
    t1 = act.add(lambda e: e.activation(lf, bi.t[32:36, :], ACT.Identity, bias=gains[0:4, 3:4]), [])
    bi.free(t1)
    t2 = act.add(lambda e: e.activation(t0_, lf, ACT.Abs), [t1, rst_free[0]])
    t2 = act.add(lambda e: e.activation(t0_, t0_, ACT.Exp, scale=-1.0), [t2])
    t2 = act.add(lambda e: e.activation(t0_, t0_, ACT.Ln, bias=one1[0:4, 0:1]), [t2, t_one])
    t_lf = dve.add(lambda e: e.scalar_tensor_tensor(out=lf, in0=lf, scalar=0.0, in1=t0_, op0=ALU.min, op1=ALU.subtract), [t2])
    rst_free[0] = t_lf
    z4 = sb("z4", [4, 128])
    t_z4 = pool.add(lambda e: e.memset(z4[:, :], 0.0))
    for c in range(4):
        sl = slice(c * 128, (c + 1) * 128)
        t = dve.add(lambda e, sl=sl: e.tensor_tensor_scan(bc[:, sl], lf[:, sl], z4[:, :], 0.0, ALU.add, ALU.add), [t_lf, t_z4])
    t = dve.add(lambda e: e.tensor_tensor(aa, ig, bc, ALU.subtract), [t, t_i])
    mp = sb("mp", [4, 8])
    t_mp = pool.add(lambda e: e.memset(mp[:, :], 0.0))
    for c in range(4):
        sl = slice(c * 128, (c + 1) * 128)
        l = c * 128 + 127
        t = dve.add(lambda e, sl=sl, c=c: e.tensor_tensor_scan(Mm[:, sl], aa[:, sl], aa[:, sl], mp[:, c:c + 1], ALU.max, ALU.max), [t, t_mp])
        t = dve.add(lambda e, l=l, c=c: e.tensor_tensor(mp[:, c + 1:c + 2], bc[:, l:l + 1], Mm[:, l:l + 1], ALU.add), [t])
    t_M = t
    dec = sb("dec", [4, 4])
    nml = sb("nml", [4, 4])
    t_negM = dve.add(lambda e: e.tensor_scalar(negM, Mm, -1.0, None, ALU.mult), [t_M])
    t_nml = dve.add(lambda e: e.tensor_scalar(nml[:, :], Mm[:, 127::128], -1.0, None, ALU.mult), [t_M])
    t_em = dve.add(lambda e: e.tensor_tensor(em, bc, Mm, ALU.add), [t_M])
    for c in range(4):
        sl = slice(c * 128, (c + 1) * 128)
        t = act.add(lambda e, sl=sl, c=c: e.activation(wi[:, sl], negM[:, sl], ACT.Exp, bias=mp[:, c:c + 1]), [t_negM])
        t = act.add(lambda e, sl=sl, c=c: e.activation(ws[:, sl], aa[:, sl], ACT.Exp, bias=nml[:, c:c + 1]), [t_nml])
        t = act.add(lambda e, c=c: e.activation(dec[:, c:c + 1], mp[:, c:c + 1], ACT.Exp, bias=nml[:, c:c + 1]), [])
    t_rows = act.add(lambda e: e.activation(em, em, ACT.Exp, scale=-1.0), [t_em])
    convolve(12)
    acol = sb("acol", [P, 4, 4])
    wcol = sb("wcol", [P, 4, 4])
    dbc = sb("dbc", [P, 4, 4])
    b = bank()
    for c in range(4):
        sl = slice(c * 128, (c + 1) * 128)
        pe.add(lambda e, sl=sl, c=c, b=b: e.transpose(b.t[:, 4 * c:4 * c + 4], aa[:, sl], ident[0:4, 0:4]), [t_M, b.wait])
        pe.add(lambda e, sl=sl, c=c, b=b: e.transpose(b.t[:, 16 + 4 * c:20 + 4 * c], ws[:, sl], ident[0:4, 0:4]), [t_rows])
    for h in range(4):
        t = mm(b.t[:, 32 + 4 * h:36 + 4 * h], [(C("sel")[0:4, h * 128:(h + 1) * 128], dec[:, :])], [])
    dve.add(lambda e, b=b: e.tensor_copy(acol[:, :, :], b.t[:, 0:16].rearrange("p (c h) -> p c h", c=4)), [t])
    dve.add(lambda e, b=b: e.tensor_copy(wcol[:, :, :], b.t[:, 16:32].rearrange("p (c h) -> p c h", c=4)), [])
    t_cols = dve.add(lambda e, b=b: e.tensor_copy(dbc[:, :, :], b.t[:, 32:48].rearrange("p (h c) -> p h c", h=4)), [])
    b.free(t_cols)
    t_zend = (pe.sem, pe.n)

    def bcast(row, h, after):
        b = bank()
        t = mm(b.t[:, :], [(C("sel")[0:4, h * 128:(h + 1) * 128], row)], after + [b.wait])
        return b, t

    Wm = [at(O_HL + 512 * h, [512]) for h in range(4)]
    qi = [at(O_HL + 2048 + 512 * h, [512]) for h in range(4)]
    den = [at(O_HL + 4096 + 512 * h, [512]) for h in range(4)]
    St = [at(O_HL + 6144 + 1024 * h, [4, 256]) for h in range(4)]
    kw = at(O_HL + 10240, [4, 512])
    t_S, t_qi, t_kw = [None] * 4, [None] * 4, [None] * 4
    for h in range(4):
        b, t = bcast(negM, h, [t_negM])
        for c in range(4):
            sl = slice(c * 128, (c + 1) * 128)
            t2 = dve.add(lambda e, b=b, sl=sl, c=c, h=h: e.scalar_tensor_tensor(
                out=Wm[h][:, sl], in0=b.t[:, sl], scalar=acol[:, c, h:h + 1], in1=C("mask"), op0=ALU.add, op1=ALU.add),
                [t, t_cols, t_zend])
        b.free(t2)
        t_W = act.add(lambda e, h=h: e.activation(Wm[h], Wm[h], ACT.Exp), [t2])
        b = bank()
        for c in range(4):
            t = pe.add(lambda e, b=b, c=c, h=h: e.transpose(b.t[:, c * 128:(c + 1) * 128],
                                                            qkc[:, 4 + h, c * 128:(c + 1) * 128], ident), [t_qkc, b.wait])
        for c in range(4):
            t_kw[h] = act.add(lambda e, b=b, c=c, h=h: e.activation(kw[:, c, h * 128:(h + 1) * 128],
                                                                  b.t[:, c * 128:(c + 1) * 128], ACT.Copy,
                                                                  scale=wcol[:, c, h:h + 1]), [t, t_cols, t_zend])
        b.free(t_kw[h])
        b, t = bcast(wi, h, [t_rows])
        t_qi[h] = dve.add(lambda e, b=b, h=h: e.tensor_tensor(qi[h], qkc[:, h, :], b.t[:, :], ALU.mult), [t, t_qkc])
        b.free(t_qi[h])
        b = bank()
        for c in range(4):
            sl = slice(c * 128, (c + 1) * 128)
            t = mm(b.t[:, sl], [(qkc[:, 4 + h, sl], qkc[:, h, sl])], [t_qkc, b.wait])
        t_S[h] = dve.add(lambda e, b=b, h=h: e.tensor_tensor(Wm[h], b.t[:, :], Wm[h], ALU.mult), [t, t_W])
        b.free(t_S[h])
        convolve(6)
    hd = [dict() for _ in range(4)]
    for h in range(4):
        t_St = [None] * 4
        for c in range(3):
            b = bank()
            mm(b.t[:, 0:128], [(kw[:, c, h * 128:(h + 1) * 128], vN[:, c, h * 128:(h + 1) * 128])], [t_kw[h], t_vn, b.wait])
            t = mm(b.t[:, 128:256], [(kw[:, c, h * 128:(h + 1) * 128], one1[:, :])], [t_one])
            if c == 0:
                t_St[1] = dve.add(lambda e, b=b, h=h: e.tensor_copy(St[h][:, 1, :], b.t[:, 0:256]), [t])
            else:
                t_St[c + 1] = dve.add(lambda e, b=b, c=c, h=h: e.scalar_tensor_tensor(
                    out=St[h][:, c + 1, :], in0=St[h][:, c, :], scalar=dbc[:, h, c:c + 1], in1=b.t[:, 0:256], op0=ALU.mult,
                    op1=ALU.add), [t, t_St[c]])
            b.free(t_St[c + 1])
        hd[h]["St"] = t_St
    yH, yL = hH, hL
    for h in range(4):
        t_St = hd[h]["St"]
        bn, bd = bank(), bank()
        for c in range(4):
            sl = slice(c * 128, (c + 1) * 128)
            n_ = [(vN[:, c, h * 128:(h + 1) * 128], Wm[h][:, sl])]
            d_ = [(one1[:, :], Wm[h][:, sl])]
            if c:
                n_.append((St[h][:, c, 0:128], qi[h][:, sl]))
                d_.append((St[h][:, c, 128:256], qi[h][:, sl]))
            tn = mm(bn.t[:, sl], n_, [t_S[h], t_qi[h], t_St[c], bn.wait])
            td = mm(bd.t[:, sl], d_, [bd.wait])
        b, t = bcast(em, h, [t_rows])
        t1 = act.add(lambda e, bd=bd, h=h: e.activation(den[h], bd.t[:, :], ACT.Abs), [td])
        bd.free(t1)
        t2 = dve.add(lambda e, b=b, h=h: e.tensor_tensor(den[h], b.t[:, :], den[h], ALU.max), [t1, t])
        b.free(t2)
        t3 = dve.add(lambda e, h=h: e.reciprocal(den[h], den[h]), [t2])
        t4 = dve.add(lambda e, h=h: e.tensor_tensor(den[h], den[h], og[:, h, :], ALU.mult), [t3, t_o])
        hd[h]["h"] = dve.add(lambda e, bn=bn, h=h: e.tensor_tensor(Wm[h], bn.t[:, :], den[h], ALU.mult), [t4, tn, td])
        bn.free(hd[h]["h"])
        convolve(3)

    def split_y(m, src, after):
        t1 = act.add(lambda e: e.activation(yH[:, m, :], src, ACT.Copy), after)
        return dve.add(lambda e: e.tensor_tensor(yL[:, m, :], src, yH[:, m, :].bitcast(F32), ALU.subtract), [t1])

    for h in range(4):
        b = bank()
        t = mm(b.t[:, :], [(oneK[:, :], Wm[h])], [hd[h]["h"], b.wait])
        t6 = dve.add(lambda e, b=b, h=h: e.tensor_tensor(Wm[h], Wm[h], b.t[:, :], ALU.subtract), [t])
        b.free(t6)
        hd[h]["c"] = t6
        convolve(3)
    for h in range(4):
        t9 = norm_plain(lambda d, h=h: Wm[h], lambda d, h=h: Wm[h], 1, 512, oneK, lambda d, h=h: col("mlstm_norm_g_2", h),
                        [hd[h]["c"]])
        t_yh = split_y(4 + h, Wm[h], [t9, t_zend])
    convolve(200)
    b = bank()
    t = mm(b.t[:, :], [(one5[:, :], acc[:, m, :]) for m in range(4)], [conv["t"], b.wait])
    for m in range(4):
        t2 = dve.add(lambda e, b=b, m=m: e.tensor_tensor(acc[:, m, :], acc[:, m, :], b.t[:, :], ALU.subtract), [t])
    b.free(t2)
    b, t = Norm(lambda d: acc[:, d, :], 4, 512, one5).all([t2])
    for m in range(4):
        r = m % 2
        t2 = dve.add(lambda e, m=m: e.scalar_tensor_tensor(out=acc[:, m, :], in0=acc[:, m, :], scalar=col("conv_ln_g_2", m),
                                                          in1=b.t[:, :], op0=ALU.mult, op1=ALU.mult), [t])
        if m == 3:
            b.free(t2)
        t3 = act.add(lambda e, m=m: e.activation(acc[:, m, :], acc[:, m, :], ACT.Identity, bias=col("conv_ln_b_2", m)), [t2])
        t3 = act.add(lambda e, m=m, r=r: e.activation(scr[:, r, :], acc[:, m, :], ACT.Sigmoid), [t3, scr_free[r]])
        t4 = dve.add(lambda e, m=m, r=r: e.tensor_tensor(acc[:, m, :], acc[:, m, :], scr[:, r, :], ALU.mult), [t3])
        scr_free[r] = t4
        t_yu = split_y(m, acc[:, m, :], [t4, t_zend])
    nx = xnorm()
    t_x = project(t_yu, None, yH, yL, None, nx)

    hF = at(O_HH, [8, 512])
    t_h = norm_plain(lambda d: xT[:, d, :], lambda d: hF[:, d, :], 8, T, oneD, lambda d: col("norm_ffn_g_2", d), [t_x], nx)
    xN = at(PH, [4, 1024])
    hN = at(PH + 4096, [4, 1024])
    RT = PH + 8192
    wr = at(RT, [8, 36])
    RT += 288
    t_pe = (pe.sem, pe.n)
    t_mid = [(pe.sem, pe.n), (act.sem, act.n), (dve.sem, dve.n)]
    t_wr = load(act, wr[:, :, 0:4], A["router_group_w_2"][0].rearrange("(k p) n -> p k n", p=P), t_mid)
    t_wr2 = load(act, wr[:, :, 4:36], A["router_expert_w_2"][0].rearrange("(k p) n -> p k n", p=P), t_mid)
    rb = sb("rb", [1, 36])
    t_rb = load(act, rb[:, 0:4], A["router_group_b_2"])
    t_rb2 = load(act, rb[:, 4:36], A["router_expert_b_2"])
    s_hd = sem("s_hd")

    def token_major(dst, src, tk, store):
        for i in range(4):
            for q in range(2):
                b = bank()
                for d in range(4):
                    t = pe.add(lambda e, b=b, d=d, q=q, i=i, src=src: e.transpose(
                        b.t[:, d * 128:(d + 1) * 128], src[:, 4 * q + d, i * 128:(i + 1) * 128], ident), [tk, b.wait])
                t_n = act.add(lambda e, b=b, q=q, i=i, dst=dst: e.activation(dst[:, i, q * 512:(q + 1) * 512], b.t[:, :],
                                                                           ACT.Copy), [t] + t_mid)
                b.free(t_n)
            if store:
                act.dma(lambda e, i=i: e.dma_start(hd_[i * 128:(i + 1) * 128, :], hN[:, i, :]), s_hd, i + 1, [t_n])
        return t_n

    wg_d, wu_d, wd_d = A["expert_w_gate_2"][0], A["expert_w_up_2"][0], A["expert_w_down_2"][0]

    def estream(what, e):
        if what == "d":
            v = wd_d[e].rearrange("(k p) n -> p k n", p=P)
            for h in range(2):
                stream(v[:, 2 * h:2 * h + 2, :])
        else:
            v = (wg_d if what == "g" else wu_d)[e].rearrange("(k p) n -> p k n", p=P)
            for h in range(2):
                stream(v[:, 4 * h:4 * h + 4, :])

    estream("g", 0)
    raws.append(Place(PH + 6144, False, lambda: t_mid2))
    hls.append(Place(PH + 12288, True, t_mid))
    estream("u", 0)
    for e in range(1, NEXP):
        estream("g", e)
        estream("d", e - 1)
        estream("u", e)
    estream("d", NEXP - 1)

    L = at(RT, [4, 36])
    RT += 144
    fgb = at(PH + 8192 + 3072, [1024])
    for q in range(2):
        t = load(act, rowbuf[0:1, :], A["final_norm_g_2"].rearrange("(a n) -> a n", a=1)[:, q * 512:(q + 1) * 512],
                 [(pe.sem, pe.n)])
        b = bank()
        t = mm(b.t[:, :], [(one1[0:1, :], rowbuf[0:1, :])], [t, b.wait])
        t_fgb = act.add(lambda e, b=b, q=q: e.activation(fgb[:, q * 512:(q + 1) * 512], b.t[:, :], ACT.Copy), [t])
        b.free(t_fgb)
    b = bank()
    for i in range(4):
        t = mm(b.t[:, i * 36:(i + 1) * 36], [(hF[:, k, i * 128:(i + 1) * 128], wr[:, k, :]) for k in range(8)]
               + [(one1[0:1, :], rb[0:1, :])], [t_h, t_wr, t_wr2, t_rb, t_rb2, b.wait])
    t = dve.add(lambda e, b=b: e.tensor_copy(L, b.t[:, 0:144].rearrange("p (i c) -> p i c", i=4)), [t] + t_mid)
    b.free(t)
    token_major(hN, hF, t_h, True)
    t_xN = token_major(xN, xT, t_x, False)

    def tmp(*shape):
        nonlocal RT
        n = 1
        for s_ in shape:
            n *= s_
        v = at(RT, list(shape))
        RT += n
        return v

    last = [t]

    def dv(fn, *more):
        last[0] = dve.add(fn, [last[0], *more])
        return last[0]

    def TT(o, a, c, op):
        return dv(lambda e: e.tensor_tensor(o, a, c, op))

    def TS(o, a, s1, s2, o1, o2=None):
        if o2 is None:
            return dv(lambda e: e.tensor_scalar(o, a, s1, None, o1))
        return dv(lambda e: e.tensor_scalar(o, a, s1, s2, o1, o2))

    def bc3(ap, n):
        return ap.unsqueeze(2).broadcast_to([P, 4, n])

    def rowb(ap, n):
        return ap.unsqueeze(1).broadcast_to([P, 4, n])

    iota = C("iota")
    gl = L[:, :, 0:4]
    el = L[:, :, 4:36]
    gm, gi, ee, pg = tmp(4), tmp(4), tmp(4, 4), tmp(4)
    oh4, q4 = tmp(4, 4), tmp(4, 4)

    def onehot(vals, mx, idx, oh, n):
        TT(oh, vals, bc3(mx, n), ALU.is_equal)
        TS(oh, oh, -64.0, 64.0, ALU.mult, ALU.add)
        TT(oh, oh, rowb(iota[:, 0:n], n), ALU.add)
        dv(lambda e: e.tensor_reduce(idx, oh, AX.X, ALU.min))
        TT(oh, rowb(iota[:, 0:n], n), bc3(idx, n), ALU.is_equal)

    dv(lambda e: e.tensor_reduce(gm, gl, AX.X, ALU.max), t_cst)
    onehot(gl, gm, gi, oh4, 4)
    TT(ee, gl, bc3(gm, 4), ALU.subtract)
    t = act.add(lambda e: e.activation(ee, ee, ACT.Exp), [last[0]])
    dv(lambda e: e.tensor_reduce(pg, ee, AX.X, ALU.add), t)
    dv(lambda e: e.reciprocal(pg, pg))
    eg = tmp(4, 32)
    pen4 = tmp(4, 4)
    TS(pen4, oh4, BIG, -BIG, ALU.mult, ALU.add)
    for i in range(4):
        eo_ = eg[:, i, :].rearrange("p (g c) -> p g c", g=4)
        ei_ = el[:, i, :].rearrange("p (g c) -> p g c", g=4)
        pb_ = pen4[:, i, :].unsqueeze(2).broadcast_to([P, 4, 8])
        TT(eo_, ei_, pb_, ALU.add)
    v1, v2, i1, i2 = tmp(4), tmp(4), tmp(4), tmp(4)
    O1, O2_, e2_ = tmp(4, 32), tmp(4, 32), tmp(4, 32)
    dv(lambda e: e.tensor_reduce(v1, eg, AX.X, ALU.max))
    onehot(eg, v1, i1, O1, 32)
    dv(lambda e: e.scalar_tensor_tensor(out=e2_, in0=O1, scalar=-2.0 * BIG, in1=eg, op0=ALU.mult, op1=ALU.add))
    dv(lambda e: e.tensor_reduce(v2, e2_, AX.X, ALU.max))
    onehot(e2_, v2, i2, O2_, 32)
    gk = tmp(2, 4)
    dd = tmp(4)
    TT(dd, v2, v1, ALU.subtract)
    t = act.add(lambda e: e.activation(dd, dd, ACT.Exp), [last[0]])
    TSt = dv(lambda e: e.tensor_scalar(gk[:, 0, :], dd, 1.0, None, ALU.add), t)
    dv(lambda e: e.reciprocal(gk[:, 0, :], gk[:, 0, :]))
    TT(gk[:, 0, :], gk[:, 0, :], pg, ALU.mult)
    TT(gk[:, 1, :], gk[:, 0, :], dd, ALU.mult)
    AS = tmp(4, 32)
    TT(AS, O1, O2_, ALU.add)
    b = bank()
    for i in range(4):
        prs = [(C("tri"), AS[:, i, :])] + [(one1[:, :], AS[:, j, :]) for j in range(i)]
        mm(b.t[:, i * 32:(i + 1) * 32], prs, [last[0], b.wait, t_one])
    t = mm(b.t[:, 128:160], [(one1[:, :], AS[:, j, :]) for j in range(4)], [])
    pos, cnt, nov, ob, oi = tmp(4, 32), tmp(32), tmp(32), tmp(32), tmp(32)
    dv(lambda e, b=b: e.tensor_copy(pos, b.t[:, 0:128].rearrange("p (i c) -> p i c", i=4)), t)
    dv(lambda e, b=b: e.tensor_copy(cnt, b.t[:, 128:160]))
    b.free(last[0])
    TS(nov, cnt, 128.5, None, ALU.is_gt)
    for lim in (256.5, 384.5):
        TS(oi, cnt, lim, None, ALU.is_gt)
        TT(nov, nov, oi, ALU.add)
    dv(lambda e: e.tensor_tensor_scan(oi, nov, z32[:, :], 0.0, ALU.add, ALU.add), t_z32)
    TT(ob, oi, nov, ALU.subtract)
    jump = tmp(32)
    TS(jump, ob, 128.0, 31.0 * 128.0, ALU.mult, ALU.add)
    TT(jump, jump, C("e128"), ALU.subtract)
    sl_ = tmp(4, 32)
    TS(sl_, pos, 127.5, None, ALU.is_gt)
    TT(sl_, sl_, rowb(jump, 32), ALU.mult)
    TT(sl_, sl_, pos, ALU.add)
    TT(sl_, sl_, rowb(C("e128"), 32), ALU.add)
    sidf = tmp(2, 4)
    for k, O_ in ((0, O1), (1, O2_)):
        TT(e2_, sl_, O_, ALU.mult)
        dv(lambda e, k=k: e.tensor_reduce(sidf[:, k, :], e2_, AX.X, ALU.add))
    sid = sb("sid", [P, 8], U32)
    t_sid = dv(lambda e: e.tensor_copy(sid[:, :].rearrange("p (k i) -> p k i", k=2), sidf))
    ovt, ovm, ovf = tmp(8, 32), tmp(8, 32), tmp(16)
    ovi = sb("ovi", [1, 16], I32)

    def b8(ap):
        return ap.unsqueeze(1).broadcast_to([P, 8, 32])

    j8 = C("j7").unsqueeze(2).broadcast_to([P, 8, 32])
    TT(ovt, b8(ob), j8, ALU.is_le)
    TT(ovm, b8(oi), j8, ALU.is_gt)
    TT(ovt, ovt, ovm, ALU.mult)
    TT(ovt, ovt, b8(iota), ALU.mult)
    dv(lambda e: e.tensor_reduce(ovf[:, 0:8], ovt, AX.X, ALU.add))
    dv(lambda e: e.tensor_copy(ovf[:, 8:16], oi[:, 31:32].broadcast_to([P, 8])))
    t_ovi = dv(lambda e: e.tensor_copy(ovi[:, :], ovf[0:1, :]))

    s_sc = sem("s_sc")
    for c in range(8):
        pool.dma(lambda e, c=c: e.indirect_dma_start(
            out=tbl[:, :], out_offset=bass.IndirectOffsetOnAxis(ap=sid[:, c:c + 1], axis=0),
            in_=C("vals")[:, c:c + 1], in_offset=None), s_sc, c + 1, [t_sid, t_tbl, t_cst])
    trow = at(RT, [128])[0:NBLK]
    tvf = at(RT + 128, [2, NBLK])
    RT += 128 + 2 * NBLK
    t = load(act, trow, tbl.rearrange("(b p) a -> b (p a)", p=P), [(s_sc, 16 * 8)] + t_mid)
    b = bank()
    t = pe.add(lambda e, b=b: e.transpose(b.t[:, 0:NBLK], trow, ident[0:NBLK, 0:NBLK]), [t, b.wait])
    idy = sb("idy", [P, NBLK], U32)
    idt = sb("idt", [P, NBLK], U32)
    t_iy = dve.add(lambda e, b=b: e.tensor_copy(idy[:, :], b.t[:, 0:NBLK]), [t])
    t2 = dve.add(lambda e, b=b: e.tensor_scalar(tvf[:, 0, :], b.t[:, 0:NBLK], 511.5, -512.0, ALU.is_gt, ALU.mult), [t])
    t3 = dve.add(lambda e, b=b: e.tensor_tensor(tvf[:, 1, :], b.t[:, 0:NBLK], tvf[:, 0, :], ALU.add), [t2])
    b.free(t3)
    t_id = dve.add(lambda e: e.tensor_copy(idt[:, :], tvf[:, 1, :]), [t3])

    assert RT <= PH + 8192 + 3072
    NXG = 4
    xg = [at(1024 * i, [1024]) for i in range(NXG)]
    xH = [at(O_HH + 1024 * i, [8, 128], FR) for i in range(2)]
    xL = [at(O_HH + 2048 + 1024 * i, [8, 128], FR) for i in range(2)]
    aH = [at(O_HH + 4096 + 512 * i, [4, 128], FR) for i in range(2)]
    aL = [at(O_HH + 5120 + 512 * i, [4, 128], FR) for i in range(2)]
    ac = [at(O_HH + 6144 + 512 * i, [512]) for i in range(2)]
    yb = [at(o, [1024]) for o in (O_HH + 7168, PH + 4096, PH + 5120)]
    s_xg = [sem(f"s_xg{i}") for i in range(NXG)]
    s_yb = [sem(f"s_yb{i}") for i in range(3)]
    t_mid2 = [(pe.sem, pe.n), (act.sem, act.n), (dve.sem, dve.n), (s_hd, 64)]
    for i in range(NXG):
        t_xgz = pool.add(lambda e, i=i: e.memset(xg[i], 0.0), t_mid2)

    X = [dict() for _ in range(NEXP)]
    fx = {"xg": [t_xgz] * NXG, "x": [None, None], "ac": [None, None], "a": [None, None], "yb": [None] * 3}

    def gather(e):
        r = e % NXG
        X[e]["xg"] = pool.dma(lambda en: en.indirect_dma_start(
            out=xg[r], out_offset=None, in_=hd_[:, :],
            in_offset=bass.IndirectOffsetOnAxis(ap=idt[:, e:e + 1], axis=0), bounds_check=T - 1, oob_is_err=False),
            s_xg[r], e // NXG + 1, [t_id, (s_hd, 64), t_xgz, fx["xg"][r]])

    def turn_x(e):
        r = e % 2
        for q in range(2):
            b = bank()
            for d in range(4):
                t = pe.add(lambda en, b=b, d=d, q=q: en.transpose(
                    b.t[:, d * 128:(d + 1) * 128], xg[e % NXG][:, (4 * q + d) * 128:(4 * q + d + 1) * 128], ident),
                    [X[e]["xg"], b.wait])
            v = b.t[:, :].rearrange("p (d c) -> p d c", d=4)
            t1 = act.add(lambda en, v=v, q=q: en.activation(xH[r][:, 4 * q:4 * q + 4, :], v, ACT.Copy),
                         [t, fx["x"][r]] + t_mid2)
            X[e]["x"] = dve.add(lambda en, v=v, q=q: en.tensor_tensor(
                xL[r][:, 4 * q:4 * q + 4, :], v, xH[r][:, 4 * q:4 * q + 4, :].bitcast(F32), ALU.subtract), [t1])
            b.free(X[e]["x"])
        fx["xg"][e % NXG] = t

    def half_mm(e, key, h):
        r = e % 2
        u = use()
        if h == 0:
            X[e][key] = bank()
        b = X[e][key]
        prs = []
        for k in range(4):
            kk = 4 * h + k
            prs += tri((xH[r][:, kk, :], xL[r][:, kk, :]), (u.hi[:, k, :], u.lo[:, k, :]))
        for i, (l, w) in enumerate(prs):
            t = pe.add(lambda en, l=l, w=w, i=i: en.matmul(b.t[:, :], l, w, start=(h == 0 and i == 0), stop=(h == 1 and i == 11)),
                       [X[e]["x"], u.done, b.wait] if i == 0 else (), inc=(i == 11))
        give(u, t)
        X[e]["t" + key] = t

    def silu(e):
        r = e % 2
        bg, bu = X[e]["g"], X[e]["u"]
        t2 = dve.add(lambda en: en.tensor_tensor(ac[r], ac[r], bg.t[:, :], ALU.mult), [X[e]["sig"]])
        bg.free(t2)
        t3 = dve.add(lambda en: en.tensor_tensor(ac[r], ac[r], bu.t[:, :], ALU.mult), [t2, X[e]["tu"]])
        bu.free(t3)
        X[e]["ac"] = t3

    def turn_a(e):
        r = e % 2
        b = bank()
        for d in range(4):
            t = pe.add(lambda en, d=d: en.transpose(b.t[:, d * 128:(d + 1) * 128], ac[r][:, d * 128:(d + 1) * 128], ident),
                       [X[e]["ac"], b.wait])
        fx["ac"][r] = t
        v = b.t[:, :].rearrange("p (d c) -> p d c", d=4)
        t1 = act.add(lambda en: en.activation(aH[r], v, ACT.Copy), [t, fx["a"][r]])
        X[e]["a"] = dve.add(lambda en: en.tensor_tensor(aL[r], v, aH[r].bitcast(F32), ALU.subtract), [t1])
        b.free(X[e]["a"])

    def down(e):
        r = e % 2
        ry = e % 3
        bs = [bank(), bank()]
        for h in range(2):
            u = use()
            for q in range(2):
                for k in range(2):
                    kk = 2 * h + k
                    prs = tri((aH[r][:, kk, :], aL[r][:, kk, :]),
                              (u.hi[:, k, q * 512:(q + 1) * 512], u.lo[:, k, q * 512:(q + 1) * 512]))
                    for i, (l, w) in enumerate(prs):
                        t = pe.add(lambda en, l=l, w=w, i=i, kk=kk, b=bs[q]: en.matmul(
                            b.t[:, :], l, w, start=(kk == 0 and i == 0), stop=(kk == 3 and i == 2)),
                            [X[e]["a"], u.done, bs[q].wait] if i == 0 else (), inc=(k == 1 and i == 2))
            give(u, t)
            if h == 0 and e + 2 < NEXP:
                turn_x(e + 2)
        fx["a"][r] = t
        t1 = act.add(lambda en: en.activation(yb[ry][:, 0:512], bs[0].t[:, :], ACT.Copy), [t, fx["yb"][ry]])
        bs[0].free(t1)
        t2 = act.add(lambda en: en.activation(yb[ry][:, 512:1024], bs[1].t[:, :], ACT.Copy), [t])
        bs[1].free(t2)
        fx["yb"][ry] = pool.dma(lambda en: en.indirect_dma_start(
            out=yd[:, :], out_offset=bass.IndirectOffsetOnAxis(ap=idy[:, e:e + 1], axis=0), in_=yb[ry],
            in_offset=None, bounds_check=2 * T - 1, oob_is_err=False), s_yb[ry], e // 3 + 1, [t2, t_iy])

    AHEAD[0] = 3
    for e in range(4):
        gather(e)
    turn_x(0)
    turn_x(1)
    half_mm(0, "g", 0)
    half_mm(0, "g", 1)
    for e in range(NEXP):
        if e + 4 < NEXP:
            gather(e + 4)
        r = e % 2
        X[e]["sig"] = act.add(lambda en, e=e, r=r: en.activation(ac[r], X[e]["g"].t[:, :], ACT.Sigmoid),
                              [X[e]["tg"], fx["ac"][r]])
        half_mm(e, "u", 0)
        half_mm(e, "u", 1)
        fx["x"][r] = (pe.sem, pe.n)
        silu(e)
        if e + 1 < NEXP:
            half_mm(e + 1, "g", 0)
            turn_a(e)
            half_mm(e + 1, "g", 1)
        else:
            turn_a(e)
        down(e)

    so_ = {n: sem("o_" + n) for n in ("ld", "xg", "pe", "act", "dve", "st")}
    yend = list(fx["yb"])
    OW = at(O_RAW, [3, 4096])
    OXG, OXT, OAC, OAT, OYB = xg[0], at(O_HH, [8, 128]), ac[0], at(O_HH + 4096, [4, 128]), yb[0]
    NPE, NACT, NDVE = 5, 4, 4

    def overflow(eng, body):
        n = eng.value_load(ovi[0:1, 8:9], min_val=0, max_val=NOV)
        for j in range(NOV):
            with eng.If(n > j):
                body(eng, j)
        return eng.nop()

    def o_sp(e, j):
        if j:
            e.wait_ge(so_["pe"], NPE * j)
        v = e.value_load(ovi[0:1, j:j + 1], min_val=0, max_val=NEXP - 1)
        for k, wv in enumerate((wg_d, wu_d, wd_d)):
            dst = OW[:, k, :].rearrange("p (k n) -> p k n", k=8 if k < 2 else 4)
            e.dma_start(dst, wv[bass.ds(v, 1)].rearrange("a (k p) n -> p (a k) n", p=P)).then_inc(so_["ld"], 16)

    def o_pool(e, j):
        if j:
            e.wait_ge(so_["pe"], NPE * (j - 1) + 1)
        c = NEXP + j
        e.indirect_dma_start(out=OXG, out_offset=None, in_=hd_[:, :],
                             in_offset=bass.IndirectOffsetOnAxis(ap=idt[:, c:c + 1], axis=0), bounds_check=T - 1,
                             oob_is_err=False).then_inc(so_["xg"], 16)
        e.wait_ge(so_["act"], NACT * (j + 1))
        e.indirect_dma_start(out=yd[:, :], out_offset=bass.IndirectOffsetOnAxis(ap=idy[:, c:c + 1], axis=0), in_=OYB,
                             in_offset=None, bounds_check=2 * T - 1, oob_is_err=False).then_inc(so_["st"], 16)
        e.wait_ge(so_["st"], 16 * (j + 1))

    def o_pe(e, j):
        o = so_["pe"]
        e.wait_ge(so_["xg"], 16 * (j + 1))
        wv = [OW[:, k, :].rearrange("p (k n) -> p k n", k=8 if k < 2 else 4) for k in range(3)]
        for d in range(8):
            l = e.transpose(banks[d // 4][:, (d % 4) * 128:(d % 4 + 1) * 128], OXG[:, d * 128:(d + 1) * 128], ident)
        l.then_inc(o, 1)
        e.wait_ge(so_["dve"], NDVE * j + 2)
        e.wait_ge(so_["ld"], 48 * (j + 1))
        for k in range(8):
            l = e.matmul(banks[2][:, :], OXT[:, k, :], wv[0][:, k, :], start=(k == 0), stop=(k == 7))
        l.then_inc(o, 1)
        for k in range(8):
            l = e.matmul(banks[3][:, :], OXT[:, k, :], wv[1][:, k, :], start=(k == 0), stop=(k == 7))
        l.then_inc(o, 1)
        e.wait_ge(so_["dve"], NDVE * j + 4)
        for d in range(4):
            l = e.transpose(banks[4][:, d * 128:(d + 1) * 128], OAC[:, d * 128:(d + 1) * 128], ident)
        l.then_inc(o, 1)
        e.wait_ge(so_["act"], NACT * j + 2)
        for q in range(2):
            for k in range(4):
                l = e.matmul(banks[5 + q][:, :], OAT[:, k, :], wv[2][:, k, q * 512:(q + 1) * 512],
                             start=(k == 0), stop=(k == 3))
        l.then_inc(o, 1)
        e.wait_ge(so_["act"], NACT * (j + 1))

    def o_act(e, j):
        o = so_["act"]
        e.wait_ge(so_["pe"], NPE * j + 2)
        e.activation(OAC, banks[2][:, :], ACT.Sigmoid).then_inc(o, 1)
        e.wait_ge(so_["pe"], NPE * j + 4)
        e.activation(OAT, banks[4][:, :].rearrange("p (d c) -> p d c", d=4), ACT.Copy).then_inc(o, 1)
        e.wait_ge(so_["pe"], NPE * j + 5)
        if j:
            e.wait_ge(so_["st"], 16 * j)
        for q in range(2):
            e.activation(OYB[:, q * 512:(q + 1) * 512], banks[5 + q][:, :], ACT.Copy).then_inc(o, 1)

    def o_dve(e, j):
        o = so_["dve"]
        e.wait_ge(so_["pe"], NPE * j + 1)
        for q in range(2):
            e.tensor_copy(OXT[:, 4 * q:4 * q + 4, :], banks[q][:, :].rearrange("p (d c) -> p d c", d=4)).then_inc(o, 1)
        e.wait_ge(so_["act"], NACT * j + 1)
        e.wait_ge(so_["pe"], NPE * j + 3)
        e.tensor_tensor(OAC, OAC, banks[2][:, :], ALU.mult).then_inc(o, 1)
        e.wait_ge(o, NDVE * j + 3)
        e.tensor_tensor(OAC, OAC, banks[3][:, :], ALU.mult).then_inc(o, 1)

    enter = [(pe.sem, pe.n), (act.sem, act.n), (dve.sem, dve.n), t_ovi] + yend
    for q, body in ((sp, o_sp), (pe, o_pe), (act, o_act), (dve, o_dve), (pool, o_pool)):
        q.add(lambda e, body=body: overflow(e, body), enter)
    t_past = [(q.sem, q.n) for q in (sp, pe, act, dve, pool)]

    Y = [at(O_HL + 4096 * k, [4, 1024]) for k in range(2)]
    s_ga = sem("s_ga")
    for i in range(4):
        for k in range(2):
            sp.dma(lambda e, k=k, i=i: e.dma_start(Y[k][:, i, :], yd[k * T + i * 128:k * T + (i + 1) * 128, :]),
                   s_ga, 2 * i + k + 1, t_past + yend)
    t_ga = (s_ga, 16 * 8)
    fs = sb("fs", [P, 8])
    s_o = sem("s_o")
    for i in range(4):
        t = dve.add(lambda e, i=i: e.scalar_tensor_tensor(out=xN[:, i, :], in0=Y[0][:, i, :], scalar=gk[:, 0, i:i + 1],
                                                          in1=xN[:, i, :], op0=ALU.mult, op1=ALU.add), [t_ga])
        t = dve.add(lambda e, i=i: e.scalar_tensor_tensor(out=xN[:, i, :], in0=Y[1][:, i, :], scalar=gk[:, 1, i:i + 1],
                                                          in1=xN[:, i, :], op0=ALU.mult, op1=ALU.add), [t])
        t = act.add(lambda e, i=i: e.activation(Y[0][:, i, :], xN[:, i, :], ACT.Square, accum_out=fs[:, i:i + 1]), [t])
        t = act.add(lambda e, i=i: e.activation(fs[:, 4 + i:5 + i], fs[:, i:i + 1], ACT.Sqrt, bias=eps[:, :],
                                                scale=1.0 / 1024), [t])
        t = dve.add(lambda e, i=i: e.reciprocal(fs[:, 4 + i:5 + i], fs[:, 4 + i:5 + i]), [t])
        t = dve.add(lambda e, i=i: e.scalar_tensor_tensor(out=xN[:, i, :], in0=xN[:, i, :], scalar=fs[:, 4 + i:5 + i],
                                                          in1=fgb, op0=ALU.mult, op1=ALU.mult), [t, t_fgb])
        sp.dma(lambda e, i=i: e.dma_start(out[0, i * 128:(i + 1) * 128, :], xN[:, i, :]), s_o, i + 1, [t])
    sp.add(lambda e: e.nop(), [(s_o, 64)])

    block = ctx.enter_context(nc.Block())

    @block.sync
    def _(e):
        sp.emit(e)

    @block.tensor
    def _(e):
        pe.emit(e)

    @block.scalar
    def _(e):
        act.emit(e)

    @block.vector
    def _(e):
        dve.emit(e)

    @block.gpsimd
    def _(e):
        pool.emit(e)


_INS = ["x", "c", "ctx", "c_ctx", "ada_w", "ada_b", "norm1_g", "norm2_g", "w_in", "b_gate", "w_fourier", "q_norm_g",
        "w_qb", "kv_norm_g", "w_kvb", "q_gain", "k_gain", "w_mla_o", "w_out", "w_up", "w_down", "norm_mix_g_2",
        "w_in_2", "b_in_2", "conv_w_2", "conv_b_2", "conv_ln_g_2", "conv_ln_b_2", "qk_conv_w_2", "qk_conv_b_2",
        "mlstm_norm_g_2", "w_out_2", "norm_ffn_g_2", "router_group_w_2", "router_group_b_2", "router_expert_w_2",
        "router_expert_b_2", "expert_w_gate_2", "expert_w_up_2", "expert_w_down_2", "final_norm_g_2"]


def kernel(**inputs):
    import concourse.bacc as _bacc
    from concourse.bass_utils import run_bass_kernel_spmd as _run

    nc = _bacc.Bacc("TRN2", target_bir_lowering=False, num_devices=1)
    arrays, args = {}, {}

    def give(name, a):
        arrays[f"in_{name}"] = a
        args[name] = nc.dram_tensor(f"in_{name}", a.shape, mybir.dt.from_np(a.dtype), kind="ExternalInput").ap()

    for name in _INS:
        give(name, np.ascontiguousarray(inputs[name]))
    cst, dfts, rope = constants()
    give("cst", cst)
    give("dfts", dfts)
    give("rope", rope)
    out = nc.dram_tensor("out_0", (1, T, D), F32, kind="ExternalOutput").ap()
    program(nc, args, out)
    r = _run(nc, [arrays], core_ids=[0])
    return r.results[0]["out_0"]
```

```python
from contextlib import ExitStack

import concourse.bass as bass
from concourse import mybir
import numpy as np

F32 = mybir.dt.float32
FR = mybir.dt.float32r
BF = mybir.dt.bfloat16
I32 = mybir.dt.int32
U32 = mybir.dt.uint32
ALU = mybir.AluOpType
ACT = mybir.ActivationFunctionType
AX = mybir.AxisListType

P = 128
T = 512
TC = 256
D = 1024
DK = 8
EPS = 1e-6
NEXP = 32
NOV = 7
NBLK = NEXP + NOV
BIG = 1.0e30
SLOTW = 4096


def rope_tables():
    rows = T // 64
    row = np.repeat(np.arange(rows, dtype=np.float32), 64)
    col = np.tile(np.arange(64, dtype=np.float32), rows)
    freqs = (np.float32(10000.0) ** (-np.arange(8, dtype=np.float32) / np.float32(8))).astype(np.float32)
    ar = row[:, None] * freqs[None, :]
    ac = col[:, None] * freqs[None, :]
    ang = np.concatenate([ar, ar, ac, ac], axis=-1)
    return np.cos(ang).astype(np.float32), np.sin(ang).astype(np.float32)


def layout_constants():
    cols = {}
    n = 0
    for name, w in (("ident", 128), ("tri", 128), ("mask", 128), ("sel", 512), ("iota", 32),
                    ("e128", 32), ("dftc", 256), ("j7", 8), ("vals", 8)):
        cols[name] = (n, w)
        n += w
    return cols, n


def constants():
    cols, n = layout_constants()
    c = np.zeros((P, n), np.float32)

    def put(name, a):
        o, w = cols[name]
        c[:a.shape[0], o:o + a.shape[1]] = a

    i = np.arange(P)
    put("ident", np.eye(P))
    put("tri", (i[:, None] < i[None, :]).astype(np.float32))
    put("mask", np.where(i[:, None] <= i[None, :], 0.0, -BIG))
    sel = np.zeros((4, 4, 128))
    for h in range(4):
        sel[h, h, :] = 1
    put("sel", sel.reshape(4, 512))
    put("iota", np.tile(np.arange(32), (P, 1)))
    put("e128", np.tile(np.arange(32) * 128, (P, 1)))
    ch = 2 * np.pi * ((i[:, None] * i[None, :]) % P) / P
    put("dftc", np.concatenate([np.cos(ch), np.sin(ch)], axis=1))
    put("j7", np.tile(np.arange(8), (P, 1)))
    put("vals", i[:, None] + 128 * np.arange(8)[None, :])
    s = np.arange(T)
    an = 2 * np.pi * ((s[:, None] * s[None, :]) % T) / T
    dfts = np.concatenate([np.cos(an), -np.sin(an)], axis=1) / 256.0
    cos, sin = rope_tables()
    sign = np.repeat(np.array([-1, 1, -1, 1], np.float32), 8)
    rope = np.concatenate([cos, sin * sign], axis=1)
    return c, dfts.astype(np.float32), np.ascontiguousarray(rope.astype(np.float32))


class Queue:

    def __init__(self, name, sem):
        self.name, self.sem, self.n, self.items = name, sem, 0, []

    def add(self, fn, after=(), inc=True):
        if inc:
            self.n += 1
        self.items.append((fn, after, self.sem if inc else None, 1))
        return (self.sem, self.n)

    def dma(self, fn, sem, count, after=()):
        self.items.append((fn, after, sem, 16))
        return (sem, 16 * count)

    def emit(self, eng):
        seen = {}

        def wait(after):
            for tok in after:
                while callable(tok):
                    tok = tok()
                if tok is None:
                    continue
                if isinstance(tok, list):
                    wait(tok)
                    continue
                s, v = tok
                if seen.get(id(s), 0) < v:
                    eng.wait_ge(s, v)
                    seen[id(s)] = v

        for fn, after, sem, by in self.items:
            wait(after)
            ins = fn(eng)
            if sem is not None:
                ins.then_inc(sem, by)


def program(nc, A, out):
    ctx = ExitStack()
    with ctx:
        build(nc, A, out, ctx)


def build(nc, A, out, ctx):
    def sb(name, shape, dt=F32):
        return ctx.enter_context(nc.sbuf_tensor(name, shape, dt))

    def sem(name):
        return ctx.enter_context(nc.semaphore(name))

    def pooled(fn, after=()):
        return pool.add(fn, list(after) + [(pool.sem, pool.n)])

    pe, act, dve, pool, sp = (Queue(n, sem("q_" + n)) for n in ("pe", "act", "dve", "pool", "sp"))
    dma_sems = [0]

    def load(q, dst, src, after=(), **kw):
        dma_sems[0] += 1
        s = sem(f"d{dma_sems[0]}")
        return q.dma(lambda e: e.dma_start(dst, src, **kw), s, 1, after)

    base0 = (nc.sbuf_base + 31) // 32 * 32
    NAR = 50400
    slab = ctx.enter_context(nc.sbuf_tensor("slab", [P, NAR], F32))
    made = [0]

    def at(off, shape, dt=F32):
        made[0] += 1
        t = nc.alloc_sbuf_tensor_at(f"t{made[0]}", [P] + list(shape), dt, offset=base0 + 4 * off, align_bytes=4)
        return t[tuple(slice(None) for _ in range(len(shape) + 1))]

    O_HH, O_CST, O_SCR, O_RST, O_RAW, O_HL, PH = 4096, 12288, 13632, 14656, 15168, 21312, 33600

    class Unit:
        pass

    class Place:

        def __init__(self, off, hl, free=None):
            self.free = free
            if hl:
                self.hi, self.lo = at(off, [2048], FR), at(off + 2048, [2048], FR)
            else:
                made[0] += 1
                self.raw, self.sem, self.count = at(off, [2048]), sem(f"rs{made[0]}"), 0

    raws = [Place(O_RAW + 2048 * i, False) for i in range(3)]
    hls = [Place(O_HL + 4096 * i, True) for i in range(3)]
    units = []
    state = {"queued": 0, "used": 0}

    def stream(view, split=True, guard=None):
        u = Unit()
        u.rp = raws.pop(0)
        raws.append(u.rp)
        u.k = view.shape[1]
        u.w = u.k * view.shape[2]
        u.raw = u.rp.raw[:, 0:u.w].rearrange("p (k n) -> p k n", k=u.k)
        u.rp.count += 1
        u.split, u.guard, u.read = split, guard, None
        before = u.rp.free
        u.rp.free = lambda: u.read
        u.tok = sp.dma(lambda e: e.dma_start(u.raw, view), u.rp.sem, u.rp.count, [before])
        units.append(u)

    def convert(u):
        if not u.split:
            return
        h = hls.pop(0)
        hls.append(h)
        u.hi = h.hi[:, 0:u.w].rearrange("p (k n) -> p k n", k=u.k)
        u.lo = h.lo[:, 0:u.w].rearrange("p (k n) -> p k n", k=u.k)
        before = h.free
        h.free = lambda: u.done_with
        t = act.add(lambda e: e.activation(u.hi, u.raw, ACT.Copy), [u.tok, before] + (u.guard() if u.guard else []))
        u.done = dve.add(lambda e: e.tensor_tensor(u.lo, u.raw, u.hi.bitcast(F32), ALU.subtract), [t])
        u.read = u.done

    AHEAD = [2]

    def ahead(n):
        n = state["used"] + n
        while state["queued"] < min(n, len(units)):
            convert(units[state["queued"]])
            state["queued"] += 1

    def use():
        n = state["used"]
        state["used"] += 1
        while state["queued"] < min(n + 1 + AHEAD[0], len(units)):
            if units[state["queued"]].guard is HOLD and state["queued"] > n:
                break
            convert(units[state["queued"]])
            state["queued"] += 1
        return units[n]

    def HOLD():
        return [(pe.sem, pe.n), (act.sem, act.n), (dve.sem, dve.n)]

    def give(u, tok):
        if u.split:
            u.done_with = tok
        else:
            u.read = tok

    def tri(w, x):
        return [(w[0], x[0]), (w[0], x[1]), (w[1], x[0])]

    banks = [ctx.enter_context(nc.psum_tensor(f"ps{i}", [P, 512], F32)) for i in range(8)]
    bank_free = [None] * 8
    bank_idle = list(range(8))

    class Bank:

        def __init__(self):
            self.i = bank_idle.pop(0)
            self.t = banks[self.i]
            self.wait = bank_free[self.i]

        def free(self, tok):
            assert self.i not in bank_idle
            bank_free[self.i] = tok
            bank_idle.append(self.i)

    def bank():
        return Bank()

    def mm(out_ap, pairs, after=()):
        n = len(pairs)
        for i, (l, r) in enumerate(pairs):
            tok = pe.add(lambda e, l=l, r=r, i=i: e.matmul(out_ap, l, r, start=(i == 0), stop=(i == n - 1)),
                         after if i == 0 else (), inc=(i == n - 1))
        return tok

    xT = at(0, [DK, T])
    hH = at(O_HH, [DK, T], FR)
    hL = at(O_HH + 4096, [DK, T], FR)

    ccols, cw = layout_constants()
    cst = at(O_CST, [cw])

    def C(name):
        o, w = ccols[name]
        return cst[:, o:o + w]

    ident = C("ident")
    ones = {}
    vA = sb("vA", [P, 128])
    vB = sb("vB", [P, 128])
    vC = sb("vC", [P, 128])
    gains = sb("gains", [P, 8])
    modc = sb("modc", [P, 48, 2])
    sil = sb("sil", [P, 16])
    A1 = sb("A1", [P, 8, 2])
    A2 = sb("A2", [P, 8])
    oneD = sb("oneD", [P, 4])
    oneQ = sb("oneQ", [P, 4])
    oneK = sb("oneK", [P, 128])
    one1 = sb("one1", [P, 128])
    one5 = sb("one5", [P, 128])
    eps = sb("eps", [P, 1])
    scr = at(O_SCR, [2, 512])
    rst = at(O_RST, [512])

    hd_ = nc.dram_tensor("h_scratch", [T, D], F32, kind="Internal").ap()
    yd = nc.dram_tensor("y_scratch", [2 * T, D], F32, kind="Internal").ap()
    tbl = nc.dram_tensor("slot_table", [NBLK * P, 1], F32, kind="Internal").ap()

    t_cst = load(act, cst, A["cst"])
    tm = None
    for t, v in ((oneD, 1.0 / 1024), (oneQ, 1.0 / 256), (oneK, 1.0 / 128), (one1, 1.0),
                 (one5, 1.0 / 512), (eps, EPS)):
        tm = pool.add(lambda e, t=t, v=v: e.memset(t[:, :], v))
    t_one = tm
    z32 = sb("z32", [P, 32])
    t_z32 = pool.add(lambda e: e.memset(z32[:, :], 0.0))
    none = at(PH + 16400, [P])[0:NBLK]
    t_none = pool.add(lambda e: e.memset(none, 4096.0))
    t_tbl = load(act, tbl.rearrange("(b p) a -> b (p a)", p=P), none, [t_none])

    vr = at(PH + 12288, [3, 128])
    va = {}
    rowsA = [("ada_b", 48), ("norm1_g", 8), ("norm2_g", 8), ("b_gate", 16), ("q_norm_g", 2), ("kv_norm_g", 1),
             ("c", 8), ("c_ctx", 8), ("norm_mix_g_2", 8), ("norm_ffn_g_2", 8), ("conv_b_2", 4),
             ("conv_ln_g_2", 4), ("conv_ln_b_2", 4)]
    rowsB = [("b_in_2", 24), ("qk_conv_b_2", 8), ("mlstm_norm_g_2", 4), ("qk_conv_w_2", 32)]
    rowsC = [("conv_w_2", 124)]
    s_v = sem("s_v")
    nv = 0
    t_v0 = pool.add(lambda e: e.memset(vr[:, :, :], 0.0))
    for j, rows in enumerate((rowsA, rowsB, rowsC)):
        o = 0
        for name, n in rows:
            va[name] = (j, o)
            a = A[name]
            if name == "b_in_2":
                a = a[:, 0:3072]
            shp = a.shape
            if len(shp) == 1:
                flat = a.rearrange("(r c) -> r c", c=128)
            elif len(shp) == 2:
                flat = a.rearrange("a (r c) -> (a r) c", c=128) if shp[0] == 1 else None
            else:
                flat = a.rearrange("a w (r c) -> (a w r) c", c=128)
            nv += 1
            act.dma(lambda e, j=j, o=o, n=n, f=flat: e.dma_start(vr[o:o + n, j, :], f[0:n, :]), s_v, nv, [t_v0])
            o += n
    t_vl = (s_v, 16 * nv)
    t_g = []
    for j, name in enumerate(("q_gain", "k_gain")):
        t_g.append(load(act, gains[0:96, j:j + 1], A[name].rearrange("a n -> n a")))
    t_g.append(load(act, gains[0:4, 2:3], A["b_in_2"][:, 3072:3076].rearrange("a n -> n a")))
    t_g.append(load(act, gains[0:4, 3:4], A["b_in_2"][:, 3076:3080].rearrange("a n -> n a")))
    def col(name, i=0):
        j, o = va[name]
        v = (vA, vB, vC)[j]
        return v[:, o + i:o + i + 1]

    def cols(name, n, step=1):
        j, o = va[name]
        return (vA, vB, vC)[j][:, o:o + n]

    scr_free = [None, None]
    rst_free = [None]

    rcol = sb("rcol", [P, 16])

    class Norm:

        def __init__(self, src, nd, n, one, place=0):
            self.res, self.col = None, rcol[:, 4 * place:4 * place + 4]
            self.src, self.nd, self.n, self.one = src, nd, n, one
            self.b = bank()
            self.sq = {}

        def square(self, d, after):
            self.sq[d] = act.add(lambda e: e.activation(scr[:, d % 2, 0:self.n], self.src(d), ACT.Square),
                                 list(after) + [scr_free[d % 2]])

        def sums(self, d):
            for i in range(self.n // 128):
                self.t = pe.add(lambda e, i=i: e.matmul(
                    self.b.t[:, i:i + 1], scr[:, d % 2, i * 128:(i + 1) * 128], self.one[:, 0:1],
                    start=(d == 0 and i == 0), stop=(d == self.nd - 1 and i == self.n // 128 - 1)),
                    [self.sq[d], t_one, self.b.wait])
            scr_free[d % 2] = self.t

        def finish(self):
            if self.res is None:
                nt = self.n // 128
                t = act.add(lambda e: e.activation(self.col[:, 0:nt], self.b.t[:, 0:nt], ACT.Sqrt, bias=eps[:, :]), [self.t])
                self.b.free(t)
                t = dve.add(lambda e: e.reciprocal(self.col[:, 0:nt], self.col[:, 0:nt]), [t])
                self.res = spread(self.col[:, 0:nt], nt, t)
            return self.res

        def all(self, after):
            for d in range(self.nd):
                self.square(d, after)
                self.sums(d)
            return self.finish()

    def spread(colv, nt, tok):
        t = dve.add(lambda e: e.tensor_tensor(
            rst[:, 0:nt * 128].rearrange("p (i c) -> p i c", i=nt), ident.unsqueeze(1).broadcast_to([P, nt, 128]),
            colv.unsqueeze(2).broadcast_to([P, nt, 128]), ALU.mult), [tok, rst_free[0], t_cst])
        b = bank()
        t = mm(b.t[:, 0:nt * 128], [(one1[:, :], rst[:, 0:nt * 128])], [t, b.wait])
        rst_free[0] = t
        return b, t

    def norm_split(src, nd, n, one, gain, shift, hi, lo, after, norm=None):
        b, t = norm.finish() if norm else Norm(src, nd, n, one).all(after)
        t3 = [None] * nd

        def tail(d):
            r = d % 2
            if shift is None:
                t4 = dve.add(lambda e: e.tensor_tensor(lo(d), scr[:, r, 0:n], hi(d).bitcast(F32), ALU.subtract), [t3[d]])
            else:
                t4 = dve.add(lambda e: e.scalar_tensor_tensor(
                    out=lo(d), in0=scr[:, r, 0:n], scalar=shift(d), in1=hi(d).bitcast(F32), op0=ALU.add,
                    op1=ALU.subtract), [t3[d]])
            scr_free[r] = t4
            return t4

        for d in range(nd):
            r = d % 2
            if d > 1:
                tail(d - 2)
            t2 = dve.add(lambda e, d=d, r=r: e.scalar_tensor_tensor(out=scr[:, r, 0:n], in0=src(d), scalar=gain(d),
                                                                  in1=b.t[:, 0:n], op0=ALU.mult, op1=ALU.mult),
                         [t, scr_free[r]] + after)
            if shift is None:
                t3[d] = act.add(lambda e, d=d, r=r: e.activation(hi(d), scr[:, r, 0:n], ACT.Copy), [t2])
            else:
                t3[d] = act.add(lambda e, d=d, r=r: e.activation(hi(d), scr[:, r, 0:n], ACT.Identity, bias=shift(d)), [t2])
        b.free(t2)
        tail(nd - 2)
        return tail(nd - 1)

    def norm_plain(src, dst, nd, n, one, gain, after, norm=None, each=None):
        b, t = norm.finish() if norm else Norm(src, nd, n, one).all(after)
        for d in range(nd):
            t2 = dve.add(lambda e, d=d: e.scalar_tensor_tensor(out=dst(d), in0=src(d), scalar=gain(d),
                                                               in1=b.t[:, 0:n], op0=ALU.mult, op1=ALU.mult),
                         [t] + after)
            if each:
                each(d, t2)
        b.free(t2)
        return t2

    xn = at(PH, [4, 1024])
    cn = at(PH + 4096, [2, 1024])
    ctxT = at(PH + 6144, [8, 256])
    ada = A["ada_w"][0].rearrange("(k p) n -> p k n", p=P)
    win = A["w_in"][0].rearrange("(k p) n -> p k n", p=P)
    win2 = A["w_in_2"][0].rearrange("(k p) n -> p k n", p=P)
    dft_d = A["dfts"].rearrange("(t p) n -> p t n", p=P)

    def cols256(v, c0, c1):
        for c in range(c0, c1, 256):
            stream(v[:, :, c:min(c + 256, c1)])

    def stream_mod(js, halves=(0, 1)):
        for j in js:
            for half in halves:
                stream(ada[:, 4 * half:4 * half + 4, j * 512:(j + 1) * 512])

    t_xl = load(sp, xn, A["x"][0].rearrange("(t p) d -> p t d", p=P))
    stream_mod([0])
    stream_mod([1], [0])
    t_cl = load(sp, cn, A["ctx"][0].rearrange("(t p) d -> p t d", p=P))
    stream_mod([1], [1])
    stream_mod([2, 3])
    cols256(win, 512, 768)
    stream(win[:, :, 768:928])
    cols256(win, 0, 512)
    for i in range(2):
        stream(dft_d[:, 2 * i:2 * i + 2, :], split=False)
    wf_d = A["w_fourier"][0].rearrange("(k p) n -> p k n", p=P)
    wo_d = A["w_mla_o"][0].rearrange("(k p) n -> p k n", p=P)
    for i in range(2):
        stream(wf_d[:, :, i * 512:(i + 1) * 512])
    for i in range(8):
        c0 = 928 + 256 * i
        stream(win[:, :, c0:c0 + 256])
        stream_mod([4 + i])
    stream(wo_d[:, :, 0:512], guard=HOLD)
    stream(wo_d[:, :, 512:1024])
    cols256(A["w_out"][0].rearrange("(k p) n -> p k n", p=P), 0, 1024)
    wup = A["w_up"][0].rearrange("(k p) n -> p k n", p=P)
    wdn = A["w_down"][0].rearrange("(k p) n -> p k n", p=P)
    for ch in range(4):
        cols256(wup, ch * 1024, ch * 1024 + 1024)
        cols256(wdn[:, ch * 8:(ch + 1) * 8, :], 0, 1024)
    for c0 in (1024, 1536, 512, 0, 2048, 2560):
        cols256(win2, c0, c0 + 512)
    wo2 = A["w_out_2"][0].rearrange("(k p) n -> p k n", p=P)
    stream(wo2[:, :, 0:256], guard=HOLD)
    cols256(wo2, 256, 1024)

    ahead(2)
    t_x = None
    for d in range(DK):
        b = bank()
        for i in range(4):
            t = pe.add(lambda e, d=d, i=i, b=b: e.transpose(b.t[:, i * 128:(i + 1) * 128],
                                                          xn[:, i, d * 128:(d + 1) * 128], ident),
                       [t_xl, t_cst, b.wait])
        t_x = dve.add(lambda e, d=d, b=b: e.tensor_copy(xT[:, d, :], b.t[:, :]), [t])
        b.free(t_x)
    for d in range(DK):
        b = bank()
        for i in range(2):
            t = pe.add(lambda e, d=d, i=i, b=b: e.transpose(b.t[:, i * 128:(i + 1) * 128],
                                                          cn[:, i, d * 128:(d + 1) * 128], ident),
                       [t_cl, b.wait])
        t_c = act.add(lambda e, d=d, b=b: e.activation(ctxT[:, d, :], b.t[:, 0:256], ACT.Copy), [t])
        b.free(t_c)

    b = bank()
    for j in range(3):
        t = pe.add(lambda e, j=j, b=b: e.transpose(b.t[:, j * 128:(j + 1) * 128], vr[:, j, :], ident),
                   [t_vl, t_cst, t_v0, b.wait])
    for j, v in enumerate((vA, vB, vC)):
        t_vc = dve.add(lambda e, j=j, v=v, b=b: e.tensor_copy(v[:, :], b.t[:, j * 128:(j + 1) * 128]), [t])
    b.free(t_vc)

    j, oc = va["c"]
    t_sg = act.add(lambda e: e.activation(sil[:, :], vA[:, oc:oc + 16], ACT.Sigmoid), [t_vc])
    t_sil = dve.add(lambda e: e.tensor_tensor(sil[:, :], sil[:, :], vA[:, oc:oc + 16], ALU.mult), [t_sg])
    silh = sb("silh", [P, 4, 8], FR)
    for q in range(2):
        t_sh = act.add(lambda e, q=q: e.activation(silh[:, 2 * q, :], sil[:, 8 * q:8 * q + 8], ACT.Copy), [t_sil])
        t_sl = dve.add(lambda e, q=q: e.tensor_tensor(silh[:, 2 * q + 1, :], sil[:, 8 * q:8 * q + 8],
                                                      silh[:, 2 * q, :].bitcast(F32), ALU.subtract), [t_sh])
    rowbuf = sb("rowbuf", [4, 512])
    row_free = [None]
    modtok = {}
    mc = sb("mc", [P, 4, 2])

    def mod_chunk(j):
        b = bank()
        for half in range(2):
            u = use()
            for k in range(4):
                for w in (u.hi, u.lo):
                    kk = 4 * half + k
                    first, fin = kk == 0 and w is u.hi, kk == 7 and w is u.lo
                    t = pe.add(lambda e, w=w, k=k, kk=kk, first=first, fin=fin: e.matmul(
                        b.t[0:4, :], silh[:, :, kk], w[:, k, :], start=first, stop=fin),
                        [u.done, t_sl, b.wait] if k == 0 else (), inc=(k == 3 and w is u.lo))
            give(u, t)
        t = act.add(lambda e: e.activation(rowbuf[:, :], b.t[0:4, :], ACT.Copy), [t, row_free[0]])
        b.free(t)
        b2 = bank()
        for i in range(4):
            t2 = pe.add(lambda e, i=i: e.transpose(b2.t[:, 4 * i:4 * i + 4], rowbuf[:, i * 128:(i + 1) * 128],
                                                   ident[0:4, 0:4]), [t, b2.wait])
        row_free[0] = t2
        _, ob = va["ada_b"]
        v = b2.t[:, 0:16].rearrange("p (i q c) -> p i q c", i=4, q=2)
        t3 = dve.add(lambda e: e.tensor_copy(mc[:, :, :], v[:, :, :, 1]), [t2, modtok.get(j - 1)])
        t3 = dve.add(lambda e: e.tensor_tensor(mc[:, :, :], v[:, :, :, 0], mc[:, :, :], ALU.add), [t3])
        for q in range(2):
            t3 = dve.add(lambda e, q=q: e.tensor_tensor(
                modc[:, 4 * j:4 * j + 4, q], mc[:, :, q], vA[:, ob + 4 * j:ob + 4 * j + 4], ALU.add), [t3, t_vc])
        b2.free(t3)
        modtok[j] = t3

    mod_chunk(0)
    n1x = Norm(lambda d: xT[:, d, :], 8, T, oneD)
    n1x.all([t_x])
    mod_chunk(1)
    n1c = Norm(lambda d: ctxT[:, d, :], 8, 256, oneD, 1)
    n1c.all([t_c])
    mod_chunk(2)
    mod_chunk(3)
    for q in range(2):
        t_a1 = dve.add(lambda e, q=q: e.scalar_tensor_tensor(
            out=A1[:, :, q], in0=modc[:, 8:16, q], scalar=1.0, in1=cols("norm1_g", 8), op0=ALU.add,
            op1=ALU.mult), [modtok[3]])

    def wx(u, m0, mw, hi, lo, n0=0, n1=T, nk=8, k0=0):
        out_ = []
        for k in range(nk):
            out_ += tri((u.hi[:, k, m0:m0 + mw], u.lo[:, k, m0:m0 + mw]),
                        (hi[:, k0 + k, n0:n1], lo[:, k0 + k, n0:n1]))
        return out_

    hcH = at(PH + 8192, [8, 256], FR)
    hcL = at(PH + 8192 + 2048, [8, 256], FR)
    t_hx = norm_split(lambda d: xT[:, d, :], 8, T, oneD, lambda d: A1[:, d, 0:1], lambda d: modc[:, d, 0:1],
                      lambda d: hH[:, d, :], lambda d: hL[:, d, :], [t_x, t_a1], n1x)
    t_hc = norm_split(lambda d: ctxT[:, d, :], 8, 256, oneD, lambda d: A1[:, d, 1:2], lambda d: modc[:, d, 1:2],
                      lambda d: hcH[:, d, :], lambda d: hcL[:, d, :], [t_c, t_a1], n1c)

    y = at(PH, [8, 512])
    qraw = at(PH, [2, 512])
    kvraw = at(PH + 1024, [768])
    qln = at(PH + 12672, [2, 512])
    kvn = at(PH + 13696, [768])
    kr = at(PH + 14464, [768])[0:32]
    u = use()
    for m in range(2):
        b = bank()
        t = mm(b.t[:, :], wx(u, m * 128, 128, hH, hL), [u.done, t_hx, b.wait])
        t_qr = act.add(lambda e, m=m, b=b: e.activation(qraw[:, m, :], b.t[:, :], ACT.Copy), [t])
        b.free(t_qr)
    give(u, t)
    u = use()
    for n0, n1, o, hi, lo in ((0, 512, 0, hH, hL), (0, 256, 512, hcH, hcL)):
        nn = n1 - n0
        b = bank()
        t = mm(b.t[:, 0:nn], wx(u, 0, 128, hi, lo, n0, n1), [u.done, t_hx if o == 0 else t_hc, b.wait])
        t_kvr = act.add(lambda e, b=b, nn=nn, o=o: e.activation(kvraw[:, o:o + nn], b.t[:, 0:nn], ACT.Copy), [t])
        b.free(t_kvr)
        b = bank()
        t = mm(b.t[0:32, 0:nn], wx(u, 128, 32, hi, lo, n0, n1), [b.wait])
        t_kr = act.add(lambda e, b=b, nn=nn, o=o: e.activation(kr[:, o:o + nn], b.t[0:32, 0:nn], ACT.Copy), [t, t_vc])
        b.free(t_kr)
    give(u, t)

    fT = at(PH + 2048, [4, 512])
    AB = at(PH + 4096, [4, 4, 256])
    fmH = at(PH + 8192, [4, 512], FR)
    fmL = at(PH + 8192 + 2048, [4, 512], FR)
    for m2 in range(2):
        u = use()
        for mi in range(2):
            m = 2 * m2 + mi
            b = bank()
            t = mm(b.t[:, :], wx(u, mi * 128, 128, hH, hL), [u.done, b.wait])
            t_f = act.add(lambda e, m=m, b=b: e.activation(fT[:, m, :], b.t[:, :], ACT.Copy), [t])
            b.free(t_f)
        give(u, t)
    t_qln = norm_plain(lambda d: qraw[:, d, :], lambda d: qln[:, d, :], 2, 512, oneQ, lambda d: col("q_norm_g", d),
                       [t_qr, t_vc])
    norm_plain(lambda d: kvraw[:, 0:512], lambda d: kvn[:, 0:512], 1, 512, oneK, lambda d: col("kv_norm_g"), [t_kvr])
    t_kvn = norm_plain(lambda d: kvraw[:, 512:768], lambda d: kvn[:, 512:768], 1, 256, oneK,
                       lambda d: col("kv_norm_g"), [t_kvr])
    for g in range(4):
        for t0 in range(0, 4, 2):
            b = bank()
            for i in range(2):
                t = mm(b.t[:, i * 256:(i + 1) * 256], [(fT[:, g, (t0 + i) * 128:(t0 + i + 1) * 128], C("dftc"))],
                       [t_f, b.wait])
            t_ab = dve.add(lambda e, b=b, g=g, t0=t0: e.tensor_copy(
                AB[:, t0:t0 + 2, g, :], b.t[:, :].rearrange("p (i c) -> p i c", i=2)), [t])
            b.free(t_ab)
    fb = [bank() for _ in range(4)]
    for half in range(2):
        u = use()
        for g in range(4):
            for i2 in range(2):
                i = 2 * half + i2
                for cs in range(2):
                    first, fin = i == 0 and cs == 0, i == 3 and cs == 1
                    t = pe.add(lambda e, g=g, i=i, i2=i2, cs=cs, u=u, first=first, fin=fin: e.matmul(
                        fb[g].t[:, :], AB[:, i, g, cs * 128:(cs + 1) * 128], u.raw[:, i2, cs * 512:(cs + 1) * 512],
                        start=first, stop=fin), [t_ab, u.tok, fb[g].wait], inc=(i2 == 1 and cs == 1))
            if half:
                t_f1 = act.add(lambda e, g=g: e.activation(fmH[:, g, :], fb[g].t[:, :], ACT.Copy), [t])
                t_fm = dve.add(lambda e, g=g: e.tensor_tensor(fmL[:, g, :], fb[g].t[:, :], fmH[:, g, :].bitcast(F32),
                                                              ALU.subtract), [t_f1])
                fb[g].free(t_fm)
        give(u, t)
    for half in range(2):
        u = use()
        for mi in range(4):
            m = 4 * half + mi
            b = bank()
            t = mm(b.t[:, :], wx(u, mi * 128, 128, fmH, fmL, nk=4), [u.done, t_fm, b.wait])
            t_y = act.add(lambda e, m=m, b=b: e.activation(y[:, m, :], b.t[:, :], ACT.Copy), [t, t_qln, t_kvn])
            b.free(t_y)
        give(u, t)
    ga = at(PH + 8192, [8, 512])
    for i in range(8):
        u = use()
        for mi in range(2):
            m = 2 * i + mi
            b = bank()
            t = mm(b.t[:, :], wx(u, mi * 128, 128, hH, hL), [u.done, b.wait])
            if m < 8:
                r = m % 2
                t = act.add(lambda e, b=b, m=m, r=r: e.activation(scr[:, r, :], b.t[:, :], ACT.Sigmoid,
                                                                bias=col("b_gate", m)), [t, scr_free[r]])
                b.free(t)
                t_y2 = dve.add(lambda e, m=m, r=r: e.tensor_tensor(y[:, m, :], y[:, m, :], scr[:, r, :], ALU.mult), [t, t_y])
                scr_free[r] = t_y2
            else:
                t_ga = act.add(lambda e, b=b, m=m: e.activation(ga[:, m - 8, :], b.t[:, :], ACT.Sigmoid,
                                                              bias=col("b_gate", m)), [t])
                b.free(t_ga)
        give(u, (pe.sem, pe.n))
        mod_chunk(4 + i)
    t_ge = (pe.sem, pe.n)
    t_a2 = dve.add(lambda e: e.scalar_tensor_tensor(out=A2[:, :], in0=modc[:, 32:40, 0], scalar=1.0,
                                                    in1=cols("norm2_g", 8), op0=ALU.add, op1=ALU.mult), [modtok[11]])

    attH = at(PH + 4096, [4, 512], FR)
    attL = at(PH + 4096 + 2048, [4, 512], FR)
    V = at(O_HH, [6, 512])
    PT = [at(O_HH + 3072, [6, 512]), at(PH + 12288, [6, 512])]
    wqb = at(O_HH + 3072, [2, 768])
    qgs = [at(O_HH + 4608 + 512 * i, [256]) for i in range(2)]
    qtm = [at(O_HH + 4864 + 512 * i, [256]) for i in range(2)]
    krg, ktm = at(O_HH + 5632, [6, 32]), at(O_HH + 5824, [4, 32])
    qhs = [at(O_HH + 6144, [512]), at(O_HH + 6656, [512])]
    ropet = at(O_HH + 7936, [4, 64])
    kt = at(O_HL, [6, 768])
    qt = at(O_HL + 4608, [4, 768])
    ph = [at(O_HL + 7680 + 768 * i, [768]) for i in range(4)]
    khead = [at(O_HH + 7168, [768]), at(O_HL + 10752, [768])]
    krr = at(O_HL + 11520, [6, 32])
    Gb = at(O_HL + 11712, [2, 32])
    ssk, ssq, krss = at(O_HL + 11776, [6, 8]), at(O_HL + 11824, [4, 8]), at(O_HL + 11856, [6])
    wkvb = at(PH + 15232, [1024])
    st = sb("st", [P, 4, 4])
    t_wk = load(act, wkvb, A["w_kvb"][0], [t_vc])
    t_wq = load(act, wqb, A["w_qb"][0].rearrange("(k p) n -> p k n", p=P), [t_ge])
    t_rp = load(act, ropet, A["rope"].rearrange("(t p) n -> p t n", p=P), [t_ge])
    t_gr = [load(act, rowbuf[0:1, 96 * j:96 * j + 96], A[name], [t_ge]) for j, name in enumerate(("q_gain", "k_gain"))]
    t_ge1 = dve.add(lambda e: e.tensor_copy(gains[0:96, 4:6], one1[0:96, 0:2]), [t_one] + t_g)
    t_ge1 = dve.add(lambda e: e.tensor_copy(gains[0:64, 4:6], gains[0:64, 0:2]), [t_ge1])
    b = bank()
    t = mm(b.t[:, 0:192], [(one1[0:1, :], rowbuf[0:1, 0:192])], t_gr + [t_one, b.wait])
    t_Gb = dve.add(lambda e, b=b: e.tensor_copy(Gb, b.t[:, 0:192].rearrange("p (j c) -> p j c", j=2)[:, :, 64:96]), [t, t_ge])
    b.free(t_Gb)

    def swapped(v, s_):
        return v.rearrange("p t (a s j) -> p t a s j", a=2, s=2)[:, :, :, s_, :]

    b = bank()
    for i in range(6):
        t = pe.add(lambda e, b=b, i=i: e.transpose(b.t[:, 32 * i:32 * i + 32], kr[:, i * 128:(i + 1) * 128],
                                                   ident[0:32, 0:32]), [t_kr, b.wait])
    krv = b.t[:, 0:192].rearrange("p (i c) -> p i c", i=6)
    t1 = act.add(lambda e, b=b: e.activation(scr[:, 0, 0:192], b.t[:, 0:192], ACT.Square), [t, scr_free[0]])
    t2 = dve.add(lambda e, krv=krv: e.tensor_tensor(krg, krv, Gb[:, 1:2, :].broadcast_to([P, 6, 32]), ALU.mult), [t1, t_Gb])
    t_ks = dve.add(lambda e: e.tensor_reduce(krss, scr[:, 0, 0:192].rearrange("p (i c) -> p i c", i=6), AX.X, ALU.add), [t1])
    b.free(t_ks)
    scr_free[0] = t_ks
    t3 = dve.add(lambda e: e.tensor_tensor(krr[:, 0:4, :], krg[:, 0:4, :], ropet[:, :, 0:32], ALU.mult), [t2, t_rp])
    for s_ in range(2):
        t4 = dve.add(lambda e, s_=s_: e.tensor_tensor(swapped(ktm, s_), swapped(krg[:, 0:4, :], 1 - s_),
                                                      swapped(ropet[:, :, 32:64], s_), ALU.mult), [t2])
    t3 = dve.add(lambda e: e.tensor_tensor(krr[:, 0:4, :], krr[:, 0:4, :], ktm, ALU.add), [t4])
    t_krr = dve.add(lambda e: e.tensor_copy(krr[:, 4:6, :], krg[:, 4:6, :]), [t3])

    kb = {}

    def k_project(i):
        bs = [bank(), bank()]
        for q, b in enumerate(bs):
            v = b.t[:, :].rearrange("p (h c) -> p h c", h=4)
            t = mm(b.t[:, :], [(kvn[:, i * 128:(i + 1) * 128], wkvb[:, q * 512:(q + 1) * 512])], [t_kvn, t_wk, b.wait])
            sv = scr[:, q, 0:256].rearrange("p (h c) -> p h c", h=4)
            t1 = act.add(lambda e, v=v, sv=sv: e.activation(sv, v[:, :, 0:64], ACT.Square), [t, scr_free[q]])
            tv = act.add(lambda e, v=v, q=q: e.activation(
                V[:, i, q * 256:(q + 1) * 256].rearrange("p (h c) -> p h c", h=4), v[:, :, 64:128], ACT.Copy), [t_ge])
            t2 = dve.add(lambda e, sv=sv, q=q: e.tensor_reduce(ssk[:, i, 4 * q:4 * q + 4], sv, AX.X, ALU.add), [t1])
            scr_free[q] = t2
        t3 = dve.add(lambda e: e.tensor_scalar(ssk[:, i, :], ssk[:, i, :], krss[:, i:i + 1], None, ALU.add), [t2, t_ks])
        t3 = act.add(lambda e: e.activation(ssk[:, i, :], ssk[:, i, :], ACT.Sqrt, bias=eps[:, :], scale=1.0 / 96), [t3])
        kb[i] = (bs, t3, tv)
        return tv

    def k_scale(i):
        bs, t, tv = kb[i]
        t = dve.add(lambda e: e.reciprocal(ssk[:, i, :], ssk[:, i, :]), [t])
        kv = kt[:, i, :].rearrange("p (h c) -> p h c", h=8)
        rk = ssk[:, i, :].unsqueeze(2)
        for q, b in enumerate(bs):
            v = b.t[:, :].rearrange("p (h c) -> p h c", h=4)
            t1 = dve.add(lambda e, v=v, q=q: e.tensor_tensor(kv[:, 4 * q:4 * q + 4, 0:64], v[:, :, 0:64],
                                                           rk[:, 4 * q:4 * q + 4, :].broadcast_to([P, 4, 64]), ALU.mult), [t])
            b.free([t1, tv])
        t2 = pooled(lambda e: e.tensor_tensor(kv[:, :, 64:96], krr[:, i:i + 1, :].broadcast_to([P, 8, 32]),
                                            rk.broadcast_to([P, 8, 32]), ALU.mult), [t, t_krr])
        return [t1, t2]

    def q_project(i):
        bs = [bank(), bank()]
        for q, (b, h0, nh) in enumerate(((bs[0], 0, 5), (bs[1], 5, 3))):
            w = nh * 96
            t = mm(b.t[:, 0:w], [(qln[:, k, i * 128:(i + 1) * 128], wqb[:, k, h0 * 96:h0 * 96 + w]) for k in range(2)],
                   [t_wq, t_qln, b.wait])
            t1 = act.add(lambda e, b=b, q=q, w=w: e.activation(scr[:, q, 0:w], b.t[:, 0:w], ACT.Square), [t, scr_free[q]])
            t2 = dve.add(lambda e, q=q, w=w, h0=h0, nh=nh: e.tensor_reduce(
                ssq[:, i, h0:h0 + nh], scr[:, q, 0:w].rearrange("p (h c) -> p h c", h=nh), AX.X, ALU.add), [t1])
            scr_free[q] = t2
        t3 = act.add(lambda e: e.activation(ssq[:, i, :], ssq[:, i, :], ACT.Sqrt, bias=eps[:, :], scale=1.0 / 96), [t2])
        kb["q", i] = (bs, t3)

    q_free = [None, None]

    def q_scale(i):
        bs, t = kb["q", i]
        r = i % 2
        t = dve.add(lambda e: e.reciprocal(ssq[:, i, :], ssq[:, i, :]), [t])
        qv = qt[:, i, :].rearrange("p (h c) -> p h c", h=8)
        rq = ssq[:, i, :].unsqueeze(2)
        for b, h0, nh in ((bs[0], 0, 5), (bs[1], 5, 3)):
            t1 = dve.add(lambda e, b=b, h0=h0, nh=nh: e.tensor_tensor(
                qv[:, h0:h0 + nh, :], b.t[:, 0:nh * 96].rearrange("p (h c) -> p h c", h=nh),
                rq[:, h0:h0 + nh, :].broadcast_to([P, nh, 96]), ALU.mult), [t])
            b.free(t1)
        g, m_ = qgs[r].rearrange("p (h c) -> p h c", h=8), qtm[r].rearrange("p (h c) -> p h c", h=8)
        t2 = pooled(lambda e: e.tensor_tensor(g, qv[:, :, 64:96], Gb[:, 0:1, :].broadcast_to([P, 8, 32]), ALU.mult),
                    [t1, t_Gb])
        t3 = pooled(lambda e: e.tensor_tensor(qv[:, :, 64:96], g, ropet[:, i:i + 1, 0:32].broadcast_to([P, 8, 32]), ALU.mult),
                    [t2, t_rp])
        sn = ropet[:, i:i + 1, 32:64].rearrange("p t (a s j) -> p t a s j", a=2, s=2)
        for s_ in range(2):
            t3 = pooled(lambda e, s_=s_: e.tensor_tensor(swapped(m_, s_), swapped(g, 1 - s_),
                                                       sn[:, :, :, s_, :].broadcast_to([P, 8, 2, 8]), ALU.mult), [t3])
        return pooled(lambda e: e.tensor_tensor(qv[:, :, 64:96], qv[:, :, 64:96], m_, ALU.add), [t3])

    t_kt, t_qt = [], []
    todo = [(q_project, q_scale, i, t_qt) for i in range(4)] + [(k_project, k_scale, i, t_kt) for i in range(6)]
    for n, (project_, scale_, i, ts_) in enumerate(todo):
        t = project_(i)
        if project_ is k_project:
            t_V = t
        if n:
            todo[n - 1][3].append(todo[n - 1][1](todo[n - 1][2]))
    t_kt.append(k_scale(5))
    SC = float(96) ** -0.5
    head = [dict() for _ in range(8)]
    fre = {"kh": [None, None], "qh": [None, None], "pt": [None, None], "ph": [None] * 4}

    def prep_k(h):
        H = head[h]
        kh = khead[h % 2]
        for b0, nb in ((0, 4), (4, 2)):
            b = bank()
            for j in range(nb):
                t = pe.add(lambda e, b=b, j=j, b0=b0: e.transpose(
                    b.t[0:96, j * 128:(j + 1) * 128], kt[:, b0 + j, h * 96:(h + 1) * 96], ident), [t_kt, b.wait])
            if b0 == 0:
                H["k1"] = act.add(lambda e, b=b: e.activation(kh[0:96, 0:512], b.t[0:96, :], ACT.Copy, scale=gains[0:96, 5:6]),
                                  [t, fre["kh"][h % 2], t_ge1])
                b.free(H["k1"])
            else:
                H["k2"] = dve.add(lambda e, b=b: e.tensor_scalar(kh[0:96, 512:768], b.t[0:96, 0:256], gains[0:96, 5:6], None,
                                                               ALU.mult), [t, fre["kh"][h % 2], t_ge1])
                b.free(H["k2"])

    def prep_q(h):
        qh = qhs[h % 2]
        b = bank()
        for j in range(4):
            t = pe.add(lambda e, b=b, j=j: e.transpose(
                b.t[0:96, j * 128:(j + 1) * 128], qt[:, j, h * 96:(h + 1) * 96], ident), [t_qt, b.wait])
        head[h]["q"] = dve.add(lambda e, b=b: e.tensor_scalar(qh[0:96, :], b.t[0:96, :], gains[0:96, 4:5], None, ALU.mult),
                               [t, fre["qh"][h % 2], t_ge1])
        b.free(head[h]["q"])

    S = {}

    def scores(n):
        h, i = divmod(n, 4)
        r = n % 4
        H = head[h]
        kh, qh = khead[h % 2], qhs[h % 2]
        sbk = [bank(), bank()]
        for b, n0, n1 in ((sbk[0], 0, 512), (sbk[1], 512, 768)):
            t = mm(b.t[:, 0:n1 - n0], [(qh[0:96, i * 128:(i + 1) * 128], kh[0:96, n0:n1])],
                   [H["q"], H["k1"], H["k2"], b.wait])
        if i == 3:
            fre["kh"][h % 2] = fre["qh"][h % 2] = t
        dve.add(lambda e, b=sbk[0]: e.tensor_reduce(st[:, r, 0:1], b.t[:, :], AX.X, ALU.max), [t, fre["ph"][r]])
        m2 = dve.add(lambda e, b=sbk[1]: e.tensor_reduce(st[:, r, 1:2], b.t[:, 0:256], AX.X, ALU.max), [])
        m3 = dve.add(lambda e: e.tensor_scalar(st[:, r, 2:3], st[:, r, 0:1], st[:, r, 1:2], -SC, ALU.max, ALU.mult), [m2])
        e1 = act.add(lambda e, b=sbk[0]: e.activation(ph[r][:, 0:512], b.t[:, :], ACT.Exp, bias=st[:, r, 2:3],
                                                    scale=SC, accum_out=st[:, r, 0:1]), [m3, fre["ph"][r]])
        e2 = act.add(lambda e, b=sbk[1]: e.activation(ph[r][:, 512:768], b.t[:, 0:256], ACT.Exp, bias=st[:, r, 2:3],
                                                    scale=SC, accum_out=st[:, r, 1:2]), [])
        sbk[0].free(e1)
        sbk[1].free(e2)
        d1 = dve.add(lambda e: e.tensor_tensor(st[:, r, 3:4], st[:, r, 0:1], st[:, r, 1:2], ALU.add), [e2])
        d2 = dve.add(lambda e: e.reciprocal(st[:, r, 3:4], st[:, r, 3:4]), [d1])
        S[n] = pooled(lambda e: e.tensor_scalar(ph[r], ph[r], st[:, r, 3:4], None, ALU.mult), [d2])

    def turn(n):
        h, i = divmod(n, 4)
        r = n % 4
        pt = PT[h % 2]
        for b0, nb in ((0, 4), (4, 2)):
            b = bank()
            for j in range(nb):
                t = pe.add(lambda e, b=b, j=j, b0=b0: e.transpose(
                    b.t[:, j * 128:(j + 1) * 128], ph[r][:, (b0 + j) * 128:(b0 + j + 1) * 128], ident), [S[n], b.wait])
            q, cp = (act, lambda e, o, a: e.activation(o, a, ACT.Copy)) if b0 == 0 else (dve, lambda e, o, a: e.tensor_copy(o, a))
            t_pt = q.add(lambda e, b=b, b0=b0, nb=nb, cp=cp: cp(
                e, pt[:, b0:b0 + nb, i * 128:(i + 1) * 128],
                b.t[:, 0:nb * 128].rearrange("p (j c) -> p j c", j=nb)), [t, fre["pt"][h % 2]])
            b.free(t_pt)
            head[h].setdefault("pt", []).append(t_pt)
        fre["ph"][r] = t

    def values(h):
        b = bank()
        pt = PT[h % 2]
        t = mm(b.t[0:64, :], [(V[:, j, h * 64:(h + 1) * 64], pt[:, j, :]) for j in range(6)], head[h]["pt"] + [t_V, b.wait])
        fre["pt"][h % 2] = t
        o = 64 * (h % 2)
        t1 = act.add(lambda e, b=b: e.activation(attH[o:o + 64, h // 2, :], b.t[0:64, :], ACT.Copy), [t])
        t2 = dve.add(lambda e, b=b: e.tensor_tensor(attL[o:o + 64, h // 2, :], b.t[0:64, :],
                                                    attH[o:o + 64, h // 2, :].bitcast(F32), ALU.subtract), [t1])
        b.free(t2)
        return t2

    prep_k(0)
    prep_q(0)
    scores(0)
    scores(1)
    for n in range(32):
        h, i = divmod(n, 4)
        if h < 7:
            if i == 0:
                prep_k(h + 1)
            if i == 1:
                prep_q(h + 1)
        if n + 2 < 32:
            scores(n + 2)
        turn(n)
        if i == 0 and h:
            t_att = values(h - 1)
    ahead(1)
    t_att = values(7)

    for half in range(2):
        u = use()
        for mi in range(4):
            m = half * 4 + mi
            b = bank()
            r = m % 2
            t = mm(b.t[:, :], wx(u, mi * 128, 128, attH, attL, nk=4), [u.done, t_att, b.wait])
            t3 = dve.add(lambda e, b=b, m=m, r=r: e.tensor_tensor(scr[:, r, :], b.t[:, :], ga[:, m, :], ALU.mult),
                         [t, t_ga, scr_free[r]])
            b.free(t3)
            t4 = dve.add(lambda e, m=m, r=r: e.tensor_tensor(scr[:, r, :], y[:, m, :], scr[:, r, :], ALU.add), [t3])
            t5 = act.add(lambda e, m=m, r=r: e.activation(hH[:, m, :], scr[:, r, :], ACT.Copy), [t4])
            t_y = dve.add(lambda e, m=m, r=r: e.tensor_tensor(hL[:, m, :], scr[:, r, :], hH[:, m, :].bitcast(F32),
                                                             ALU.subtract), [t5])
            scr_free[r] = t_y
        give(u, t)

    def project(t_src, scale, hi, lo, t_scale=None, norm=None):
        for c in range(4):
            u = use()
            for mi in range(2):
                m = 2 * c + mi
                b = bank()
                t = mm(b.t[:, :], wx(u, mi * 128, 128, hi, lo), [u.done, t_src, b.wait])
                if scale is None:
                    t2 = dve.add(lambda e, b=b, m=m: e.tensor_tensor(xT[:, m, :], xT[:, m, :], b.t[:, :], ALU.add), [t, xprev[m]])
                else:
                    t2 = dve.add(lambda e, b=b, m=m: e.scalar_tensor_tensor(
                        out=xT[:, m, :], in0=b.t[:, :], scalar=scale(m), in1=xT[:, m, :], op0=ALU.mult, op1=ALU.add),
                        [t, t_scale, xprev[m]])
                xprev[m] = t2
                b.free(t2)
                if norm:
                    norm.square(m, [t2])
                    if m:
                        norm.sums(m - 1)
            give(u, t)
        if norm:
            norm.sums(7)
        return t2

    def xnorm():
        return Norm(lambda d: xT[:, d, :], 8, T, oneD)

    xprev = [None] * 8
    nx = xnorm()
    t_x = project(t_y, lambda m: modc[:, 16 + m, 0:1], hH, hL, modtok[11], nx)

    t_h = norm_split(lambda d: xT[:, d, :], 8, T, oneD, lambda d: A2[:, d:d + 1], lambda d: modc[:, 24 + d, 0:1],
                     lambda d: hH[:, d, :], lambda d: hL[:, d, :], [t_x, t_a2], nx)
    UH = [at(PH + 8192 * i, [8, 512], FR) for i in range(2)]
    UL = [at(PH + 8192 * i + 4096, [8, 512], FR) for i in range(2)]
    u_free = [None, None]
    t_u = [None] * 4

    def mlp_up(ch):
        q = ch % 2
        for c in range(4):
            u = use()
            for mi in range(2):
                m = 2 * c + mi
                r = m % 2
                b = bank()
                t = mm(b.t[:, :], wx(u, mi * 128, 128, hH, hL), [u.done, t_h, b.wait])
                t1 = act.add(lambda e, b=b, r=r: e.activation(scr[:, r, :], b.t[:, :], ACT.Relu), [t, scr_free[r]])
                t2 = dve.add(lambda e, b=b, r=r: e.tensor_tensor(scr[:, r, :], b.t[:, :], scr[:, r, :], ALU.mult), [t1])
                b.free(t2)
                t3 = act.add(lambda e, m=m, r=r: e.activation(UH[q][:, m, :], scr[:, r, :], ACT.Copy), [t2, u_free[q]])
                t_u[ch] = dve.add(lambda e, m=m, r=r: e.tensor_tensor(
                    UL[q][:, m, :], scr[:, r, :], UH[q][:, m, :].bitcast(F32), ALU.subtract), [t3])
                scr_free[r] = t_u[ch]
            give(u, t)

    for ch in range(4):
        mlp_up(ch)
        nx = xnorm() if ch == 3 else None
        t_x = project(t_u[ch], lambda m: modc[:, 40 + m, 0:1], UH[ch % 2], UL[ch % 2], modtok[11], nx)
        u_free[ch % 2] = (pe.sem, pe.n)

    t_pe = (pe.sem, pe.n)
    t_h = norm_split(lambda d: xT[:, d, :], 8, T, oneD, lambda d: col("norm_mix_g_2", d), None,
                     lambda d: hH[:, d, :], lambda d: hL[:, d, :], [t_x], nx)
    up = at(PH, [4, 542])
    acc = at(PH + 2168, [4, 512])
    qkp = at(PH + 4216, [8, 515])
    qkc = at(PH + 8336, [8, 512])
    vN = at(PH + 12432, [4, 512])
    og = at(PH + 14480, [4, 512])
    wif = at(PH + 16528, [8, 8])
    wifs = sb("wifs", [P, 8, 40], FR)
    wifH, wifL = wifs[:, :, 0:36], wifs[:, :, 4:40]
    kw = at(PH, [4, 512])
    t_z1 = pool.add(lambda e: e.memset(up[:, :, 0:30], 0.0), [t_pe])
    t_z2 = pool.add(lambda e: e.memset(qkp[:, :, 0:3], 0.0), [t_pe])
    t_wif = load(act, wif, win2[:, :, 3072:3080], [t_pe])
    t_wz = act.add(lambda e: e.activation(wifs[:, :, :], z32[:, 0:8].unsqueeze(2).broadcast_to([P, 8, 40]), ACT.Copy), [t_z32])
    for q in range(2):
        t_wz = act.add(lambda e, q=q: e.activation(wifH[:, :, 32 * q:32 * q + 4], wif[:, :, 4 * q:4 * q + 4], ACT.Copy),
                       [t_wif, t_wz])
    for q in range(2):
        t_wif = dve.add(lambda e, q=q: e.tensor_tensor(wifL[:, :, 32 * q:32 * q + 4], wif[:, :, 4 * q:4 * q + 4],
                                                       wifH[:, :, 32 * q:32 * q + 4].bitcast(F32), ALU.subtract), [t_wz])

    def bcol(i):
        return col("b_in_2", i)

    t_cv = [None] * 8
    for c in range(4):
        u = use()
        for mi in range(2):
            m = 2 * c + mi
            b = bank()
            t = mm(b.t[:, :], wx(u, mi * 128, 128, hH, hL), [u.done, t_h, b.wait])
            t_qk = act.add(lambda e, b=b, m=m: e.activation(qkp[:, m, 3:515], b.t[:, :], ACT.Identity, bias=bcol(8 + m)),
                           [t, t_z2])
            b.free(t_qk)
            for j in range(4):
                wc = col("qk_conv_w_2", j * 8 + m)
                if j == 0:
                    t2 = dve.add(lambda e, m=m, wc=wc: e.tensor_scalar(qkc[:, m, :], qkp[:, m, 0:512], wc,
                                                                      col("qk_conv_b_2", m), ALU.mult, ALU.add), [t_qk])
                else:
                    t2 = dve.add(lambda e, m=m, wc=wc, j=j: e.scalar_tensor_tensor(
                        out=qkc[:, m, :], in0=qkp[:, m, j:j + 512], scalar=wc, in1=qkc[:, m, :], op0=ALU.mult,
                        op1=ALU.add), [t2])
            t_cv[m] = t2
        give(u, t)
    sg = acc
    for c in range(2):
        u = use()
        for mi in range(2):
            m = 2 * c + mi
            b = bank()
            t = mm(b.t[:, :], wx(u, mi * 128, 128, hH, hL), [u.done, b.wait])
            t_s = act.add(lambda e, b=b, m=m: e.activation(sg[:, m, :], b.t[:, :], ACT.Sigmoid, bias=bcol(4 + m)), [t, t_pe])
            b.free(t_s)
        give(u, t)
    t_cu = [None] * 4
    for c in range(2):
        u = use()
        for mi in range(2):
            m = 2 * c + mi
            b = bank()
            t = mm(b.t[:, :], wx(u, mi * 128, 128, hH, hL), [u.done, b.wait])
            t_cu[m] = dve.add(lambda e, b=b, m=m: e.scalar_tensor_tensor(
                out=up[:, m, 30:542], in0=b.t[:, :], scalar=bcol(m), in1=sg[:, m, :], op0=ALU.add, op1=ALU.mult),
                [t, t_s, t_z1])
            b.free(t_cu[m])
        give(u, t)

    for m in range(8):
        r = m % 2
        t2 = act.add(lambda e, m=m, r=r: e.activation(scr[:, r, :], qkc[:, m, :], ACT.Sigmoid), [t_cv[m], scr_free[r]])
        kscale = 1.0 if m < 4 else float(128) ** -0.5
        t_qkc = dve.add(lambda e, m=m, r=r, ks=kscale: e.scalar_tensor_tensor(
            out=qkc[:, m, :], in0=qkc[:, m, :], scalar=ks, in1=scr[:, r, :], op0=ALU.mult, op1=ALU.mult), [t2])
        scr_free[r] = t_qkc

    taps = [(m, j) for m in range(3) for j in range(31)]
    conv = {"t": None, "j": 0, "free": [t_pe, t_pe]}
    diag = [C("dftc")[:, 0:128], C("dftc")[:, 128:256]]

    def convolve_pe(n):
        if not conv["j"]:
            conv["bank"] = bank()
        for _ in range(n):
            j = conv["j"]
            if j == 31:
                return
            conv["j"] = j + 1
            d = diag[j % 2]
            t = pooled(lambda e, d=d, j=j: e.tensor_scalar(d, ident, col("conv_w_2", j * 4 + 3), None, ALU.mult),
                       [conv["free"][j % 2]])
            conv["free"][j % 2] = pe.add(lambda e, d=d, j=j, b=conv["bank"]: e.matmul(
                b.t[:, :], d, up[:, 3, j:j + 512], start=(j == 0), stop=(j == 30)), [t, conv["bank"].wait] + t_cu)
            if j == 30:
                conv["last"] = act.add(lambda e, b=conv["bank"]: e.activation(
                    acc[:, 3, :], b.t[:, :], ACT.Identity, bias=col("conv_b_2", 3)), [conv["free"][0]] + t_cu)
                conv["bank"].free(conv["last"])

    def convolve(n):
        for _ in range(n):
            if not taps:
                return
            m, j = taps.pop(0)
            wc = col("conv_w_2", j * 4 + m)
            if j == 0:
                conv["t"] = dve.add(lambda e, m=m, wc=wc: e.tensor_scalar(acc[:, m, :], up[:, m, 0:512], wc,
                                                             col("conv_b_2", m), ALU.mult, ALU.add), t_cu)
            else:
                conv["t"] = dve.add(lambda e, m=m, j=j, wc=wc: e.scalar_tensor_tensor(
                    out=acc[:, m, :], in0=up[:, m, j:j + 512], scalar=wc, in1=acc[:, m, :], op0=ALU.mult,
                    op1=ALU.add), [conv["t"]])

    brow = rowbuf[0:1, :]
    t_br = load(act, brow, A["b_in_2"][:, 2048:2560], [t_pe])
    for c in range(2):
        u = use()
        convolve(12)
        for i in range(4):
            vb = bank()
            prs = []
            for k in range(8):
                prs += tri((hH[:, k, i * 128:(i + 1) * 128], hL[:, k, i * 128:(i + 1) * 128]), (u.hi[:, k, :], u.lo[:, k, :]))
            t = mm(vb.t[:, 0:256], prs + [(one1[0:1, :], brow[0:1, c * 256:(c + 1) * 256])],
                   [u.done, t_br, vb.wait])
            t_vn = act.add(lambda e, i=i, c=c, vb=vb: e.activation(vN[:, i, c * 256:(c + 1) * 256],
                                                                 vb.t[:, 0:256], ACT.Copy), [t])
            vb.free(t_vn)
        give(u, t)
    for c in range(2):
        u = use()
        convolve(12)
        for mi in range(2):
            m = 2 * c + mi
            b = bank()
            t = mm(b.t[:, :], wx(u, mi * 128, 128, hH, hL), [u.done, b.wait])
            t_o = act.add(lambda e, b=b, m=m: e.activation(og[:, m, :], b.t[:, :], ACT.Sigmoid, bias=bcol(20 + m)), [t, t_tbl])
            b.free(t_o)
        give(u, t)
    g6 = at(PH + 4216, [6, 512])
    ga4 = [g6[0:4, i, :] for i in range(6)]
    aa, bc, Mm, negM, wi, ws = ga4
    ig, lf, em = aa, Mm, bc
    t0_ = rst[0:4, :]
    bi = bank()
    prs = []
    for k in range(8):
        prs += tri((wifH[:, k, :], wifL[:, k, :]), (hH[:, k, :], hL[:, k, :]))
    t_ig = mm(bi.t[0:36, :], prs, [t_wif, bi.wait])
    convolve_pe(12)
    t_i = act.add(lambda e: e.activation(ig, bi.t[0:4, :], ACT.Identity, bias=gains[0:4, 2:3]), [t_ig, t_cv[7]] + t_g)
    t1 = act.add(lambda e: e.activation(lf, bi.t[32:36, :], ACT.Identity, bias=gains[0:4, 3:4]), [])
    bi.free(t1)
    t2 = act.add(lambda e: e.activation(t0_, lf, ACT.Abs), [t1, rst_free[0]])
    t2 = act.add(lambda e: e.activation(t0_, t0_, ACT.Exp, scale=-1.0), [t2])
    t2 = act.add(lambda e: e.activation(t0_, t0_, ACT.Ln, bias=one1[0:4, 0:1]), [t2, t_one])
    t_lf = dve.add(lambda e: e.scalar_tensor_tensor(out=lf, in0=lf, scalar=0.0, in1=t0_, op0=ALU.min, op1=ALU.subtract), [t2])
    rst_free[0] = t_lf
    z4 = sb("z4", [4, 128])
    t_z4 = pool.add(lambda e: e.memset(z4[:, :], 0.0))
    for c in range(4):
        sl = slice(c * 128, (c + 1) * 128)
        t = dve.add(lambda e, sl=sl: e.tensor_tensor_scan(bc[:, sl], lf[:, sl], z4[:, :], 0.0, ALU.add, ALU.add), [t_lf, t_z4])
    t = dve.add(lambda e: e.tensor_tensor(aa, ig, bc, ALU.subtract), [t, t_i])
    mp = sb("mp", [4, 8])
    t_mp = pool.add(lambda e: e.memset(mp[:, :], 0.0))
    for c in range(4):
        sl = slice(c * 128, (c + 1) * 128)
        l = c * 128 + 127
        t = dve.add(lambda e, sl=sl, c=c: e.tensor_tensor_scan(Mm[:, sl], aa[:, sl], aa[:, sl], mp[:, c:c + 1], ALU.max, ALU.max), [t, t_mp])
        t = dve.add(lambda e, l=l, c=c: e.tensor_tensor(mp[:, c + 1:c + 2], bc[:, l:l + 1], Mm[:, l:l + 1], ALU.add), [t])
    t_M = t
    dec = sb("dec", [4, 4])
    nml = sb("nml", [4, 4])
    t_negM = dve.add(lambda e: e.tensor_scalar(negM, Mm, -1.0, None, ALU.mult), [t_M])
    t_nml = dve.add(lambda e: e.tensor_scalar(nml[:, :], Mm[:, 127::128], -1.0, None, ALU.mult), [t_M])
    t_em = dve.add(lambda e: e.tensor_tensor(em, bc, Mm, ALU.add), [t_M])
    for c in range(4):
        sl = slice(c * 128, (c + 1) * 128)
        t = act.add(lambda e, sl=sl, c=c: e.activation(wi[:, sl], negM[:, sl], ACT.Exp, bias=mp[:, c:c + 1]), [t_negM])
        t = act.add(lambda e, sl=sl, c=c: e.activation(ws[:, sl], aa[:, sl], ACT.Exp, bias=nml[:, c:c + 1]), [t_nml])
        t = act.add(lambda e, c=c: e.activation(dec[:, c:c + 1], mp[:, c:c + 1], ACT.Exp, bias=nml[:, c:c + 1]), [])
    t_rows = act.add(lambda e: e.activation(em, em, ACT.Exp, scale=-1.0), [t_em])
    convolve(12)
    acol = sb("acol", [P, 4, 4])
    wcol = sb("wcol", [P, 4, 4])
    dbc = sb("dbc", [P, 4, 4])
    ecol = sb("ecol", [P, 4, 4])
    b = bank()
    for c in range(4):
        sl = slice(c * 128, (c + 1) * 128)
        pe.add(lambda e, sl=sl, c=c, b=b: e.transpose(b.t[:, 4 * c:4 * c + 4], aa[:, sl], ident[0:4, 0:4]), [t_M, b.wait])
        pe.add(lambda e, sl=sl, c=c, b=b: e.transpose(b.t[:, 16 + 4 * c:20 + 4 * c], ws[:, sl], ident[0:4, 0:4]), [t_rows])
        pe.add(lambda e, sl=sl, c=c, b=b: e.transpose(b.t[:, 48 + 4 * c:52 + 4 * c], em[:, sl], ident[0:4, 0:4]), [t_rows])
    for h in range(4):
        t = mm(b.t[:, 32 + 4 * h:36 + 4 * h], [(C("sel")[0:4, h * 128:(h + 1) * 128], dec[:, :])], [])
    dve.add(lambda e, b=b: e.tensor_copy(acol[:, :, :], b.t[:, 0:16].rearrange("p (c h) -> p c h", c=4)), [t])
    dve.add(lambda e, b=b: e.tensor_copy(wcol[:, :, :], b.t[:, 16:32].rearrange("p (c h) -> p c h", c=4)), [])
    dve.add(lambda e, b=b: e.tensor_copy(ecol[:, :, :].rearrange("p h c -> p c h"), b.t[:, 48:64].rearrange("p (c h) -> p c h", c=4)), [])
    t_cols = dve.add(lambda e, b=b: e.tensor_copy(dbc[:, :, :], b.t[:, 32:48].rearrange("p (h c) -> p h c", h=4)), [])
    b.free(t_cols)
    t_zend = (pe.sem, pe.n)

    def bcast(row, h, after):
        b = bank()
        t = mm(b.t[:, :], [(C("sel")[0:4, h * 128:(h + 1) * 128], row)], after + [b.wait])
        return b, t

    Wm = [at(O_HL + 512 * h, [512]) for h in range(4)]
    qi = [at(O_HL + 2048 + 512 * h, [512]) for h in range(4)]
    den = [at(O_HL + 4096 + 512 * h, [512]) for h in range(4)]
    St = [at(O_HL + 6144 + 1024 * h, [4, 256]) for h in range(4)]
    kw = at(O_HL + 10240, [4, 512])
    t_S, t_qi, t_kw = [None] * 4, [None] * 4, [None] * 4
    for h in range(4):
        b, t = bcast(negM, h, [t_negM])
        for c in range(4):
            sl = slice(c * 128, (c + 1) * 128)
            t2 = dve.add(lambda e, b=b, sl=sl, c=c, h=h: e.scalar_tensor_tensor(
                out=Wm[h][:, sl], in0=b.t[:, sl], scalar=acol[:, c, h:h + 1], in1=C("mask"), op0=ALU.add, op1=ALU.add),
                [t, t_cols, t_zend])
        b.free(t2)
        t_W = act.add(lambda e, h=h: e.activation(Wm[h], Wm[h], ACT.Exp), [t2])
        b = bank()
        for c in range(4):
            t = pe.add(lambda e, b=b, c=c, h=h: e.transpose(b.t[:, c * 128:(c + 1) * 128],
                                                            qkc[:, 4 + h, c * 128:(c + 1) * 128], ident), [t_qkc, b.wait])
        for c in range(4):
            t_kw[h] = act.add(lambda e, b=b, c=c, h=h: e.activation(kw[:, c, h * 128:(h + 1) * 128],
                                                                  b.t[:, c * 128:(c + 1) * 128], ACT.Copy,
                                                                  scale=wcol[:, c, h:h + 1]), [t, t_cols, t_zend])
        b.free(t_kw[h])
        b, t = bcast(wi, h, [t_rows])
        t_qi[h] = dve.add(lambda e, b=b, h=h: e.tensor_tensor(qi[h], qkc[:, h, :], b.t[:, :], ALU.mult), [t, t_qkc])
        b.free(t_qi[h])
        b = bank()
        for c in range(4):
            sl = slice(c * 128, (c + 1) * 128)
            t = mm(b.t[:, sl], [(qkc[:, 4 + h, sl], qkc[:, h, sl])], [t_qkc, b.wait])
        t_S[h] = dve.add(lambda e, b=b, h=h: e.tensor_tensor(Wm[h], b.t[:, :], Wm[h], ALU.mult), [t, t_W])
        b.free(t_S[h])
        convolve(6)
        convolve_pe(2)
    hd = [dict() for _ in range(4)]
    for h in range(4):
        t_St = [None] * 4
        for c in range(3):
            b = bank()
            mm(b.t[:, 0:128], [(kw[:, c, h * 128:(h + 1) * 128], vN[:, c, h * 128:(h + 1) * 128])], [t_kw[h], t_vn, b.wait])
            t = mm(b.t[:, 128:256], [(kw[:, c, h * 128:(h + 1) * 128], one1[:, :])], [t_one])
            if c == 0:
                t_St[1] = dve.add(lambda e, b=b, h=h: e.tensor_copy(St[h][:, 1, :], b.t[:, 0:256]), [t])
            else:
                t_St[c + 1] = dve.add(lambda e, b=b, c=c, h=h: e.scalar_tensor_tensor(
                    out=St[h][:, c + 1, :], in0=St[h][:, c, :], scalar=dbc[:, h, c:c + 1], in1=b.t[:, 0:256], op0=ALU.mult,
                    op1=ALU.add), [t, t_St[c]])
            b.free(t_St[c + 1])
        hd[h]["St"] = t_St
        convolve_pe(2)
    yH, yL = hH, hL
    bd = bank()
    for h in range(4):
        t_St = hd[h]["St"]
        hd[h]["bn"] = bn = bank()
        for c in range(4):
            sl = slice(c * 128, (c + 1) * 128)
            n_ = [(vN[:, c, h * 128:(h + 1) * 128], Wm[h][:, sl])]
            if c:
                n_.append((St[h][:, c, 0:128], qi[h][:, sl]))
            hd[h]["n"] = mm(bn.t[:, sl], n_, [t_S[h], t_qi[h], t_St[c], bn.wait])
        for c in range(4):
            sl = slice(c * 128, (c + 1) * 128)
            d_ = [(Wm[h][:, sl], one1[:, 0:1])] + ([(qi[h][:, sl], St[h][:, c, 128:129])] if c else [])
            for j, (l, r) in enumerate(d_):
                td = pe.add(lambda e, l=l, r=r, h=h, c=c, j=j: e.matmul(
                    bd.t[:, 4 * h + c:4 * h + c + 1], l, r, start=(h == 0 and c == 0), stop=(h == 3 and c == 3 and j == 1)),
                    [bd.wait])
        t1 = dve.add(lambda e, bn=bn, h=h: e.tensor_tensor(den[h], bn.t[:, :], og[:, h, :], ALU.mult), [hd[h]["n"], t_o])
        bn.free(t1)
        convolve(2)
        convolve_pe(1)
    convolve_pe(4)
    t1 = act.add(lambda e: e.activation(rcol[:, :], bd.t[:, 0:16], ACT.Abs), [td])
    bd.free(t1)
    t2 = dve.add(lambda e: e.tensor_tensor(rcol[:, :], rcol[:, :], ecol[:, :, :].rearrange("p h c -> p (h c)"), ALU.max), [t1])
    t_rd = dve.add(lambda e: e.reciprocal(rcol[:, :], rcol[:, :]), [t2])
    for h in range(4):
        b, t = spread(rcol[:, 4 * h:4 * h + 4], 4, t_rd)
        hd[h]["h"] = dve.add(lambda e, b=b, h=h: e.tensor_tensor(Wm[h], den[h], b.t[:, :], ALU.mult), [t, td])
        b.free(hd[h]["h"])
        convolve(3)

    def split_y(m, src, after):
        t1 = act.add(lambda e: e.activation(yH[:, m, :], src, ACT.Copy), after)
        return dve.add(lambda e: e.tensor_tensor(yL[:, m, :], src, yH[:, m, :].bitcast(F32), ALU.subtract), [t1])

    for h in range(4):
        b = bank()
        t = mm(b.t[:, :], [(oneK[:, :], Wm[h])], [hd[h]["h"], b.wait])
        t6 = dve.add(lambda e, b=b, h=h: e.tensor_tensor(Wm[h], Wm[h], b.t[:, :], ALU.subtract), [t])
        b.free(t6)
        hd[h]["c"] = t6
        convolve(3)
    hn = [Norm(lambda d, h=h: Wm[h], 1, 512, oneK, h) for h in range(4)]
    for h in range(4):
        hn[h].square(0, [hd[h]["c"]])
        hn[h].sums(0)
    convolve(6)
    convolve_pe(31)
    for h in range(4):
        hn[h].finish()
    for h in range(4):
        t9 = norm_plain(lambda d, h=h: Wm[h], lambda d, h=h: Wm[h], 1, 512, oneK, lambda d, h=h: col("mlstm_norm_g_2", h),
                        [hd[h]["c"]], hn[h])
        t_yh = split_y(4 + h, Wm[h], [t9, t_zend])
    ahead(2)
    fgr = at(PH + 4216, [1024])
    t_fgr = load(act, fgr[0:1, :], A["final_norm_g_2"].rearrange("(a n) -> a n", a=1),
                 [(pe.sem, pe.n), (act.sem, act.n), (dve.sem, dve.n)])
    convolve(200)
    b = bank()
    t = mm(b.t[:, :], [(one5[:, :], acc[:, m, :]) for m in range(4)],
           [conv["t"], conv["last"], b.wait])
    for m in range(4):
        t2 = dve.add(lambda e, b=b, m=m: e.tensor_tensor(acc[:, m, :], acc[:, m, :], b.t[:, :], ALU.subtract), [t])
    b.free(t2)
    b, t = Norm(lambda d: acc[:, d, :], 4, 512, one5).all([t2])
    for m in range(4):
        r = m % 2
        t2 = dve.add(lambda e, m=m: e.scalar_tensor_tensor(out=acc[:, m, :], in0=acc[:, m, :], scalar=col("conv_ln_g_2", m),
                                                          in1=b.t[:, :], op0=ALU.mult, op1=ALU.mult), [t])
        if m == 3:
            b.free(t2)
        t3 = act.add(lambda e, m=m: e.activation(acc[:, m, :], acc[:, m, :], ACT.Identity, bias=col("conv_ln_b_2", m)), [t2])
        t3 = act.add(lambda e, m=m, r=r: e.activation(scr[:, r, :], acc[:, m, :], ACT.Sigmoid), [t3, scr_free[r]])
        t4 = dve.add(lambda e, m=m, r=r: e.tensor_tensor(acc[:, m, :], acc[:, m, :], scr[:, r, :], ALU.mult), [t3])
        scr_free[r] = t4
        t_yu = split_y(m, acc[:, m, :], [t4, t_zend])
    wr = at(PH + 8192, [8, 36])
    rb = sb("rb", [1, 36])
    t_pre = [(pe.sem, pe.n), (act.sem, act.n), (dve.sem, dve.n)]
    t_wr = [load(act, wr[:, :, 0:4], A["router_group_w_2"][0].rearrange("(k p) n -> p k n", p=P), t_pre),
            load(act, wr[:, :, 4:36], A["router_expert_w_2"][0].rearrange("(k p) n -> p k n", p=P), t_pre),
            load(act, rb[:, 0:4], A["router_group_b_2"]),
            load(act, rb[:, 4:36], A["router_expert_b_2"])]
    fgb = at(PH + 8192 + 3072, [1024])
    for q in range(2):
        b = bank()
        t = mm(b.t[:, :], [(one1[0:1, :], fgr[0:1, q * 512:(q + 1) * 512])], [t_fgr, b.wait])
        t_fgb = act.add(lambda e, b=b, q=q: e.activation(fgb[:, q * 512:(q + 1) * 512], b.t[:, :], ACT.Copy), [t])
        b.free(t_fgb)
    nx = xnorm()
    t_x = project(t_yu, None, yH, yL, None, nx)

    hF = at(O_HH, [8, 512])
    t_h = norm_plain(lambda d: xT[:, d, :], lambda d: hF[:, d, :], 8, T, oneD, lambda d: col("norm_ffn_g_2", d), [t_x], nx)
    xN = at(PH, [4, 1024])
    hN = at(PH + 4096, [4, 1024])
    RT = PH + 8192
    RT += 288
    t_mid = [(pe.sem, pe.n), (act.sem, act.n), (dve.sem, dve.n)]
    s_hd = sem("s_hd")

    def token_major(dst, src, tk, store):
        for i in range(4):
            for q in range(2):
                b = bank()
                for d in range(4):
                    t = pe.add(lambda e, b=b, d=d, q=q, i=i, src=src: e.transpose(
                        b.t[:, d * 128:(d + 1) * 128], src[:, 4 * q + d, i * 128:(i + 1) * 128], ident), [tk, b.wait])
                t_n = act.add(lambda e, b=b, q=q, i=i, dst=dst: e.activation(dst[:, i, q * 512:(q + 1) * 512], b.t[:, :],
                                                                           ACT.Copy), [t] + t_mid)
                b.free(t_n)
            if store:
                act.dma(lambda e, i=i: e.dma_start(hd_[i * 128:(i + 1) * 128, :], hN[:, i, :]), s_hd, i + 1, [t_n])
        return t_n

    wg_d, wu_d, wd_d = A["expert_w_gate_2"][0], A["expert_w_up_2"][0], A["expert_w_down_2"][0]

    def estream(what, e):
        if what == "d":
            v = wd_d[e].rearrange("(k p) n -> p k n", p=P)
            for h in range(2):
                stream(v[:, 2 * h:2 * h + 2, :])
        else:
            v = (wg_d if what == "g" else wu_d)[e].rearrange("(k p) n -> p k n", p=P)
            for h in range(2):
                stream(v[:, 4 * h:4 * h + 4, :])

    estream("g", 0)
    raws.append(Place(PH + 6144, False, (s_hd, 64)))
    hls.append(Place(PH + 12288, True, t_mid))
    estream("u", 0)
    for e in range(1, NEXP):
        estream("g", e)
        estream("d", e - 1)
        estream("u", e)
    estream("d", NEXP - 1)

    L = at(RT, [4, 36])
    RT += 144
    b = bank()
    for i in range(4):
        t2 = mm(b.t[:, i * 36:(i + 1) * 36], [(hF[:, k, i * 128:(i + 1) * 128], wr[:, k, :]) for k in range(8)]
                + [(one1[0:1, :], rb[0:1, :])], [t_h, t_wr, b.wait])
    t = dve.add(lambda e, b=b: e.tensor_copy(L, b.t[:, 0:144].rearrange("p (i c) -> p i c", i=4)), [t2] + t_mid)
    b.free(t)

    def tmp(*shape):
        nonlocal RT
        n = 1
        for s_ in shape:
            n *= s_
        v = at(RT, list(shape))
        RT += n
        return v

    last = [t]

    def dv(fn, *more):
        last[0] = dve.add(fn, [last[0], *more])
        return last[0]

    def TT(o, a, c, op):
        return dv(lambda e: e.tensor_tensor(o, a, c, op))

    def TS(o, a, s1, s2, o1, o2=None):
        if o2 is None:
            return dv(lambda e: e.tensor_scalar(o, a, s1, None, o1))
        return dv(lambda e: e.tensor_scalar(o, a, s1, s2, o1, o2))

    def bc3(ap, n):
        return ap.unsqueeze(2).broadcast_to([P, 4, n])

    def rowb(ap, n):
        return ap.unsqueeze(1).broadcast_to([P, 4, n])

    iota = C("iota")
    gl = L[:, :, 0:4]
    el = L[:, :, 4:36]
    gm, gi, ee, pg = tmp(4), tmp(4), tmp(4, 4), tmp(4)
    oh4, q4 = tmp(4, 4), tmp(4, 4)

    def onehot(vals, mx, idx, oh, n):
        TT(oh, vals, bc3(mx, n), ALU.is_equal)
        TS(oh, oh, -64.0, 64.0, ALU.mult, ALU.add)
        TT(oh, oh, rowb(iota[:, 0:n], n), ALU.add)
        dv(lambda e: e.tensor_reduce(idx, oh, AX.X, ALU.min))
        TT(oh, rowb(iota[:, 0:n], n), bc3(idx, n), ALU.is_equal)

    dv(lambda e: e.tensor_reduce(gm, gl, AX.X, ALU.max), t_cst)
    onehot(gl, gm, gi, oh4, 4)
    TT(ee, gl, bc3(gm, 4), ALU.subtract)
    t = act.add(lambda e: e.activation(ee, ee, ACT.Exp), [last[0]])
    token_major(hN, hF, t_h, True)
    dv(lambda e: e.tensor_reduce(pg, ee, AX.X, ALU.add), t)
    dv(lambda e: e.reciprocal(pg, pg))
    eg = tmp(4, 32)
    pen4 = tmp(4, 4)
    TS(pen4, oh4, BIG, -BIG, ALU.mult, ALU.add)
    for i in range(4):
        eo_ = eg[:, i, :].rearrange("p (g c) -> p g c", g=4)
        ei_ = el[:, i, :].rearrange("p (g c) -> p g c", g=4)
        pb_ = pen4[:, i, :].unsqueeze(2).broadcast_to([P, 4, 8])
        TT(eo_, ei_, pb_, ALU.add)
    v1, v2, i1, i2 = tmp(4), tmp(4), tmp(4), tmp(4)
    O1, O2_, e2_ = tmp(4, 32), tmp(4, 32), tmp(4, 32)
    dv(lambda e: e.tensor_reduce(v1, eg, AX.X, ALU.max))
    onehot(eg, v1, i1, O1, 32)
    dv(lambda e: e.scalar_tensor_tensor(out=e2_, in0=O1, scalar=-2.0 * BIG, in1=eg, op0=ALU.mult, op1=ALU.add))
    dv(lambda e: e.tensor_reduce(v2, e2_, AX.X, ALU.max))
    onehot(e2_, v2, i2, O2_, 32)
    gk = tmp(2, 4)
    dd = tmp(4)
    TT(dd, v2, v1, ALU.subtract)
    t = act.add(lambda e: e.activation(dd, dd, ACT.Exp), [last[0]])
    TSt = dv(lambda e: e.tensor_scalar(gk[:, 0, :], dd, 1.0, None, ALU.add), t)
    dv(lambda e: e.reciprocal(gk[:, 0, :], gk[:, 0, :]))
    TT(gk[:, 0, :], gk[:, 0, :], pg, ALU.mult)
    TT(gk[:, 1, :], gk[:, 0, :], dd, ALU.mult)
    AS, triB, oneB = at(RT, [4, 32], BF), at(RT + 64, [128], BF), at(RT + 128, [128], BF)
    RT += 192
    TT(AS, O1, O2_, ALU.add)
    t_tb = [pool.add(lambda e: e.tensor_copy(triB, C("tri")), t_mid), pool.add(lambda e: e.tensor_copy(oneB, one1[:, :]), t_mid)]
    b = bank()
    for i in range(4):
        prs = [(triB, AS[:, i, :])] + [(oneB, AS[:, j, :]) for j in range(i)]
        mm(b.t[:, i * 32:(i + 1) * 32], prs, [last[0], b.wait, t_tb])
    t = mm(b.t[:, 128:160], [(oneB, AS[:, j, :]) for j in range(4)], [])
    pos, cnt, nov, ob, oi = tmp(4, 32), tmp(32), tmp(32), tmp(32), tmp(32)
    dv(lambda e, b=b: e.tensor_copy(pos, b.t[:, 0:128].rearrange("p (i c) -> p i c", i=4)), t)
    dv(lambda e, b=b: e.tensor_copy(cnt, b.t[:, 128:160]))
    b.free(last[0])
    TS(nov, cnt, 128.5, None, ALU.is_gt)
    for lim in (256.5, 384.5):
        TS(oi, cnt, lim, None, ALU.is_gt)
        TT(nov, nov, oi, ALU.add)
    dv(lambda e: e.tensor_tensor_scan(oi, nov, z32[:, :], 0.0, ALU.add, ALU.add), t_z32)
    TT(ob, oi, nov, ALU.subtract)
    jump = tmp(32)
    TS(jump, ob, 128.0, 31.0 * 128.0, ALU.mult, ALU.add)
    TT(jump, jump, C("e128"), ALU.subtract)
    sl_ = tmp(4, 32)
    TS(sl_, pos, 127.5, None, ALU.is_gt)
    TT(sl_, sl_, rowb(jump, 32), ALU.mult)
    TT(sl_, sl_, pos, ALU.add)
    TT(sl_, sl_, rowb(C("e128"), 32), ALU.add)
    sidf = tmp(2, 4)
    for k, O_ in ((0, O1), (1, O2_)):
        TT(e2_, sl_, O_, ALU.mult)
        dv(lambda e, k=k: e.tensor_reduce(sidf[:, k, :], e2_, AX.X, ALU.add))
    sid = sb("sid", [P, 8], U32)
    t_sid = dv(lambda e: e.tensor_copy(sid[:, :].rearrange("p (k i) -> p k i", k=2), sidf))
    ovt, ovm, ovf = tmp(8, 32), tmp(8, 32), tmp(16)
    ovi = sb("ovi", [1, 16], I32)

    def b8(ap):
        return ap.unsqueeze(1).broadcast_to([P, 8, 32])

    j8 = C("j7").unsqueeze(2).broadcast_to([P, 8, 32])
    TT(ovt, b8(ob), j8, ALU.is_le)
    TT(ovm, b8(oi), j8, ALU.is_gt)
    TT(ovt, ovt, ovm, ALU.mult)
    TT(ovt, ovt, b8(iota), ALU.mult)
    dv(lambda e: e.tensor_reduce(ovf[:, 0:8], ovt, AX.X, ALU.add))
    dv(lambda e: e.tensor_copy(ovf[:, 8:16], oi[:, 31:32].broadcast_to([P, 8])))
    t_ovi = dv(lambda e: e.tensor_copy(ovi[:, :], ovf[0:1, :]))

    ahead(3)
    t_xN = token_major(xN, xT, t_x, False)

    s_sc = sem("s_sc")
    for c in range(8):
        pool.dma(lambda e, c=c: e.indirect_dma_start(
            out=tbl[:, :], out_offset=bass.IndirectOffsetOnAxis(ap=sid[:, c:c + 1], axis=0),
            in_=C("vals")[:, c:c + 1], in_offset=None), s_sc, c + 1, [t_sid, t_tbl, t_cst])
    trow = at(RT, [128])[0:NBLK]
    tvf = at(RT + 128, [2, NBLK])
    RT += 128 + 2 * NBLK
    t = load(act, trow, tbl.rearrange("(b p) a -> b (p a)", p=P), [(s_sc, 16 * 8)] + t_mid)
    b = bank()
    t = pe.add(lambda e, b=b: e.transpose(b.t[:, 0:NBLK], trow, ident[0:NBLK, 0:NBLK]), [t, b.wait])
    idy = sb("idy", [P, NBLK], U32)
    idt = sb("idt", [P, NBLK], U32)
    t_iy = dve.add(lambda e, b=b: e.tensor_copy(idy[:, :], b.t[:, 0:NBLK]), [t])
    t2 = dve.add(lambda e, b=b: e.tensor_scalar(tvf[:, 0, :], b.t[:, 0:NBLK], 511.5, -512.0, ALU.is_gt, ALU.mult), [t])
    t3 = dve.add(lambda e, b=b: e.tensor_tensor(tvf[:, 1, :], b.t[:, 0:NBLK], tvf[:, 0, :], ALU.add), [t2])
    b.free(t3)
    t_id = dve.add(lambda e: e.tensor_copy(idt[:, :], tvf[:, 1, :]), [t3])

    assert RT <= PH + 8192 + 3072
    NXG = 4
    xg = [at(1024 * i, [1024]) for i in range(NXG)]
    xH = [at(O_HH + 1024 * i, [8, 128], FR) for i in range(2)]
    xL = [at(O_HH + 2048 + 1024 * i, [8, 128], FR) for i in range(2)]
    aH = [at(O_HH + 4096 + 512 * i, [4, 128], FR) for i in range(2)]
    aL = [at(O_HH + 5120 + 512 * i, [4, 128], FR) for i in range(2)]
    ac = [at(O_HH + 6144 + 512 * i, [512]) for i in range(2)]
    yb = [at(o, [1024]) for o in (O_HH + 7168, PH + 4096, PH + 5120)]
    s_xg = [sem(f"s_xg{i}") for i in range(NXG)]
    s_yb = [sem(f"s_yb{i}") for i in range(3)]
    t_mid2 = [(pe.sem, pe.n), (act.sem, act.n), (dve.sem, dve.n), (s_hd, 64)]

    X = [dict() for _ in range(NEXP)]
    fx = {"xg": [None] * NXG, "x": [None, None], "ac": [None, None], "a": [None, None], "yb": [None] * 3}

    def gather(e):
        r = e % NXG
        X[e]["xg"] = pool.dma(lambda en: en.indirect_dma_start(
            out=xg[r], out_offset=None, in_=hd_[:, :],
            in_offset=bass.IndirectOffsetOnAxis(ap=idt[:, e:e + 1], axis=0), bounds_check=T - 1, oob_is_err=False),
            s_xg[r], e // NXG + 1, [t_id, t_mid2, fx["xg"][r]])

    def turn_x(e):
        r = e % 2
        for q in range(2):
            b = bank()
            for d in range(4):
                t = pe.add(lambda en, b=b, d=d, q=q: en.transpose(
                    b.t[:, d * 128:(d + 1) * 128], xg[e % NXG][:, (4 * q + d) * 128:(4 * q + d + 1) * 128], ident),
                    [X[e]["xg"], b.wait])
            v = b.t[:, :].rearrange("p (d c) -> p d c", d=4)
            t1 = act.add(lambda en, v=v, q=q: en.activation(xH[r][:, 4 * q:4 * q + 4, :], v, ACT.Copy),
                         [t, fx["x"][r]] + t_mid2)
            X[e]["x"] = dve.add(lambda en, v=v, q=q: en.tensor_tensor(
                xL[r][:, 4 * q:4 * q + 4, :], v, xH[r][:, 4 * q:4 * q + 4, :].bitcast(F32), ALU.subtract), [t1])
            b.free(X[e]["x"])
        fx["xg"][e % NXG] = t

    def half_mm(e, key, h):
        r = e % 2
        u = use()
        if h == 0:
            X[e][key] = bank()
        b = X[e][key]
        prs = []
        for k in range(4):
            kk = 4 * h + k
            prs += tri((xH[r][:, kk, :], xL[r][:, kk, :]), (u.hi[:, k, :], u.lo[:, k, :]))
        for i, (l, w) in enumerate(prs):
            t = pe.add(lambda en, l=l, w=w, i=i: en.matmul(b.t[:, :], l, w, start=(h == 0 and i == 0), stop=(h == 1 and i == 11)),
                       [X[e]["x"], u.done, b.wait] if i == 0 else (), inc=(i == 11))
        give(u, t)
        X[e]["t" + key] = t

    def silu(e):
        r = e % 2
        bg, bu = X[e]["g"], X[e]["u"]
        t2 = dve.add(lambda en: en.tensor_tensor(ac[r], ac[r], bg.t[:, :], ALU.mult), [X[e]["sig"]])
        bg.free(t2)
        t3 = dve.add(lambda en: en.tensor_tensor(ac[r], ac[r], bu.t[:, :], ALU.mult), [t2, X[e]["tu"]])
        bu.free(t3)
        X[e]["ac"] = t3

    def turn_a(e):
        r = e % 2
        b = bank()
        for d in range(4):
            t = pe.add(lambda en, d=d: en.transpose(b.t[:, d * 128:(d + 1) * 128], ac[r][:, d * 128:(d + 1) * 128], ident),
                       [X[e]["ac"], b.wait])
        fx["ac"][r] = t
        v = b.t[:, :].rearrange("p (d c) -> p d c", d=4)
        t1 = act.add(lambda en: en.activation(aH[r], v, ACT.Copy), [t, fx["a"][r]])
        X[e]["a"] = dve.add(lambda en: en.tensor_tensor(aL[r], v, aH[r].bitcast(F32), ALU.subtract), [t1])
        b.free(X[e]["a"])

    def down(e):
        r = e % 2
        ry = e % 3
        bs = [bank(), bank()]
        for h in range(2):
            u = use()
            for q in range(2):
                for k in range(2):
                    kk = 2 * h + k
                    prs = tri((aH[r][:, kk, :], aL[r][:, kk, :]),
                              (u.hi[:, k, q * 512:(q + 1) * 512], u.lo[:, k, q * 512:(q + 1) * 512]))
                    for i, (l, w) in enumerate(prs):
                        t = pe.add(lambda en, l=l, w=w, i=i, kk=kk, b=bs[q]: en.matmul(
                            b.t[:, :], l, w, start=(kk == 0 and i == 0), stop=(kk == 3 and i == 2)),
                            [X[e]["a"], u.done, bs[q].wait] if i == 0 else (), inc=(k == 1 and i == 2))
            give(u, t)
            if h == 0 and e + 2 < NEXP:
                turn_x(e + 2)
        fx["a"][r] = t
        t1 = act.add(lambda en: en.activation(yb[ry][:, 0:512], bs[0].t[:, :], ACT.Copy), [t, fx["yb"][ry]])
        bs[0].free(t1)
        t2 = act.add(lambda en: en.activation(yb[ry][:, 512:1024], bs[1].t[:, :], ACT.Copy), [t])
        bs[1].free(t2)
        fx["yb"][ry] = pool.dma(lambda en: en.indirect_dma_start(
            out=yd[:, :], out_offset=bass.IndirectOffsetOnAxis(ap=idy[:, e:e + 1], axis=0), in_=yb[ry],
            in_offset=None, bounds_check=2 * T - 1, oob_is_err=False), s_yb[ry], e // 3 + 1, [t2, t_iy])

    AHEAD[0] = 3
    for e in range(4):
        gather(e)
    turn_x(0)
    turn_x(1)
    half_mm(0, "g", 0)
    half_mm(0, "g", 1)
    for e in range(NEXP):
        if e + 4 < NEXP:
            gather(e + 4)
        r = e % 2
        X[e]["sig"] = act.add(lambda en, e=e, r=r: en.activation(ac[r], X[e]["g"].t[:, :], ACT.Sigmoid),
                              [X[e]["tg"], fx["ac"][r]])
        half_mm(e, "u", 0)
        half_mm(e, "u", 1)
        fx["x"][r] = (pe.sem, pe.n)
        silu(e)
        if e + 1 < NEXP:
            half_mm(e + 1, "g", 0)
            turn_a(e)
            half_mm(e + 1, "g", 1)
        else:
            turn_a(e)
        down(e)

    so_ = {n: sem("o_" + n) for n in ("ld", "xg", "pe", "act", "dve", "st")}
    yend = list(fx["yb"])
    OW = at(O_RAW, [3, 4096])
    OXG, OXT, OAC, OAT, OYB = xg[0], at(O_HH, [8, 128]), ac[0], at(O_HH + 4096, [4, 128]), yb[0]
    NPE, NACT, NDVE = 5, 4, 4

    def overflow(eng, body):
        n = eng.value_load(ovi[0:1, 8:9], min_val=0, max_val=NOV)
        for j in range(NOV):
            with eng.If(n > j):
                body(eng, j)
        return eng.nop()

    def o_sp(e, j):
        if j:
            e.wait_ge(so_["pe"], NPE * j)
        v = e.value_load(ovi[0:1, j:j + 1], min_val=0, max_val=NEXP - 1)
        for k, wv in enumerate((wg_d, wu_d, wd_d)):
            dst = OW[:, k, :].rearrange("p (k n) -> p k n", k=8 if k < 2 else 4)
            e.dma_start(dst, wv[bass.ds(v, 1)].rearrange("a (k p) n -> p (a k) n", p=P)).then_inc(so_["ld"], 16)

    def o_pool(e, j):
        if j:
            e.wait_ge(so_["pe"], NPE * (j - 1) + 1)
        c = NEXP + j
        e.indirect_dma_start(out=OXG, out_offset=None, in_=hd_[:, :],
                             in_offset=bass.IndirectOffsetOnAxis(ap=idt[:, c:c + 1], axis=0), bounds_check=T - 1,
                             oob_is_err=False).then_inc(so_["xg"], 16)
        e.wait_ge(so_["act"], NACT * (j + 1))
        e.indirect_dma_start(out=yd[:, :], out_offset=bass.IndirectOffsetOnAxis(ap=idy[:, c:c + 1], axis=0), in_=OYB,
                             in_offset=None, bounds_check=2 * T - 1, oob_is_err=False).then_inc(so_["st"], 16)
        e.wait_ge(so_["st"], 16 * (j + 1))

    def o_pe(e, j):
        o = so_["pe"]
        e.wait_ge(so_["xg"], 16 * (j + 1))
        wv = [OW[:, k, :].rearrange("p (k n) -> p k n", k=8 if k < 2 else 4) for k in range(3)]
        for d in range(8):
            l = e.transpose(banks[d // 4][:, (d % 4) * 128:(d % 4 + 1) * 128], OXG[:, d * 128:(d + 1) * 128], ident)
        l.then_inc(o, 1)
        e.wait_ge(so_["dve"], NDVE * j + 2)
        e.wait_ge(so_["ld"], 48 * (j + 1))
        for k in range(8):
            l = e.matmul(banks[2][:, :], OXT[:, k, :], wv[0][:, k, :], start=(k == 0), stop=(k == 7))
        l.then_inc(o, 1)
        for k in range(8):
            l = e.matmul(banks[3][:, :], OXT[:, k, :], wv[1][:, k, :], start=(k == 0), stop=(k == 7))
        l.then_inc(o, 1)
        e.wait_ge(so_["dve"], NDVE * j + 4)
        for d in range(4):
            l = e.transpose(banks[4][:, d * 128:(d + 1) * 128], OAC[:, d * 128:(d + 1) * 128], ident)
        l.then_inc(o, 1)
        e.wait_ge(so_["act"], NACT * j + 2)
        for q in range(2):
            for k in range(4):
                l = e.matmul(banks[5 + q][:, :], OAT[:, k, :], wv[2][:, k, q * 512:(q + 1) * 512],
                             start=(k == 0), stop=(k == 3))
        l.then_inc(o, 1)
        e.wait_ge(so_["act"], NACT * (j + 1))

    def o_act(e, j):
        o = so_["act"]
        e.wait_ge(so_["pe"], NPE * j + 2)
        e.activation(OAC, banks[2][:, :], ACT.Sigmoid).then_inc(o, 1)
        e.wait_ge(so_["pe"], NPE * j + 4)
        e.activation(OAT, banks[4][:, :].rearrange("p (d c) -> p d c", d=4), ACT.Copy).then_inc(o, 1)
        e.wait_ge(so_["pe"], NPE * j + 5)
        if j:
            e.wait_ge(so_["st"], 16 * j)
        for q in range(2):
            e.activation(OYB[:, q * 512:(q + 1) * 512], banks[5 + q][:, :], ACT.Copy).then_inc(o, 1)

    def o_dve(e, j):
        o = so_["dve"]
        e.wait_ge(so_["pe"], NPE * j + 1)
        for q in range(2):
            e.tensor_copy(OXT[:, 4 * q:4 * q + 4, :], banks[q][:, :].rearrange("p (d c) -> p d c", d=4)).then_inc(o, 1)
        e.wait_ge(so_["act"], NACT * j + 1)
        e.wait_ge(so_["pe"], NPE * j + 3)
        e.tensor_tensor(OAC, OAC, banks[2][:, :], ALU.mult).then_inc(o, 1)
        e.wait_ge(o, NDVE * j + 3)
        e.tensor_tensor(OAC, OAC, banks[3][:, :], ALU.mult).then_inc(o, 1)

    enter = [(pe.sem, pe.n), (act.sem, act.n), (dve.sem, dve.n), t_ovi] + yend
    for q, body in ((sp, o_sp), (pe, o_pe), (act, o_act), (dve, o_dve), (pool, o_pool)):
        q.add(lambda e, body=body: overflow(e, body), enter)
    t_past = [(q.sem, q.n) for q in (sp, pe, act, dve, pool)]

    Y = [at(O_HL + 4096 * k, [4, 1024]) for k in range(2)]
    s_ga = sem("s_ga")
    for i in range(4):
        for k in range(2):
            sp.dma(lambda e, k=k, i=i: e.dma_start(Y[k][:, i, :], yd[k * T + i * 128:k * T + (i + 1) * 128, :]),
                   s_ga, 2 * i + k + 1, t_past + yend)
    t_ga = (s_ga, 16 * 8)
    fs = sb("fs", [P, 8])
    s_o = sem("s_o")
    for i in range(4):
        t = dve.add(lambda e, i=i: e.scalar_tensor_tensor(out=xN[:, i, :], in0=Y[0][:, i, :], scalar=gk[:, 0, i:i + 1],
                                                          in1=xN[:, i, :], op0=ALU.mult, op1=ALU.add), [t_ga])
        t = dve.add(lambda e, i=i: e.scalar_tensor_tensor(out=xN[:, i, :], in0=Y[1][:, i, :], scalar=gk[:, 1, i:i + 1],
                                                          in1=xN[:, i, :], op0=ALU.mult, op1=ALU.add), [t])
        t = act.add(lambda e, i=i: e.activation(Y[0][:, i, :], xN[:, i, :], ACT.Square, accum_out=fs[:, i:i + 1]), [t])
        t = act.add(lambda e, i=i: e.activation(fs[:, 4 + i:5 + i], fs[:, i:i + 1], ACT.Sqrt, bias=eps[:, :],
                                                scale=1.0 / 1024), [t])
        t = dve.add(lambda e, i=i: e.reciprocal(fs[:, 4 + i:5 + i], fs[:, 4 + i:5 + i]), [t])
        t = dve.add(lambda e, i=i: e.scalar_tensor_tensor(out=xN[:, i, :], in0=xN[:, i, :], scalar=fs[:, 4 + i:5 + i],
                                                          in1=fgb, op0=ALU.mult, op1=ALU.mult), [t, t_fgb])
        sp.dma(lambda e, i=i: e.dma_start(out[0, i * 128:(i + 1) * 128, :], xN[:, i, :]), s_o, i + 1, [t])
    sp.add(lambda e: e.nop(), [(s_o, 64)])

    block = ctx.enter_context(nc.Block())

    @block.sync
    def _(e):
        sp.emit(e)

    @block.tensor
    def _(e):
        pe.emit(e)

    @block.scalar
    def _(e):
        act.emit(e)

    @block.vector
    def _(e):
        dve.emit(e)

    @block.gpsimd
    def _(e):
        pool.emit(e)


_INS = ["x", "c", "ctx", "c_ctx", "ada_w", "ada_b", "norm1_g", "norm2_g", "w_in", "b_gate", "w_fourier", "q_norm_g",
        "w_qb", "kv_norm_g", "w_kvb", "q_gain", "k_gain", "w_mla_o", "w_out", "w_up", "w_down", "norm_mix_g_2",
        "w_in_2", "b_in_2", "conv_w_2", "conv_b_2", "conv_ln_g_2", "conv_ln_b_2", "qk_conv_w_2", "qk_conv_b_2",
        "mlstm_norm_g_2", "w_out_2", "norm_ffn_g_2", "router_group_w_2", "router_group_b_2", "router_expert_w_2",
        "router_expert_b_2", "expert_w_gate_2", "expert_w_up_2", "expert_w_down_2", "final_norm_g_2"]


def kernel(**inputs):
    import concourse.bacc as _bacc
    from concourse.bass_utils import run_bass_kernel_spmd as _run

    nc = _bacc.Bacc("TRN2", target_bir_lowering=False, num_devices=1)
    arrays, args = {}, {}

    def give(name, a):
        arrays[f"in_{name}"] = a
        args[name] = nc.dram_tensor(f"in_{name}", a.shape, mybir.dt.from_np(a.dtype), kind="ExternalInput").ap()

    for name in _INS:
        give(name, np.ascontiguousarray(inputs[name]))
    cst, dfts, rope = constants()
    give("cst", cst)
    give("dfts", dfts)
    give("rope", rope)
    out = nc.dram_tensor("out_0", (1, T, D), F32, kind="ExternalOutput").ap()
    program(nc, args, out)
    r = _run(nc, [arrays], core_ids=[0])
    return r.results[0]["out_0"]
```
